# Optimizing a Trainium2 kernel written in Bass

```python
import jax, jax.numpy as jnp
from jax import lax
import numpy as np

D_MODEL = 1024
BATCH = 1
SEQ = 512
DEPTH = 1

CHUNK = 64

MIX_WIDTH = D_MODEL
CONV_W = MIX_WIDTH // 2
LRU_W = MIX_WIDTH - CONV_W
N_CONV_HEADS = 8
N_LRU_HEADS = 8
CONV_HD = CONV_W // N_CONV_HEADS
LRU_HD = LRU_W // N_LRU_HEADS
SHORT_CONV_K = 3
LRU_CONV_K = 4
LRU_C = 8.0
N_IN = 3 * CONV_W + 2 * LRU_W

PEER_HEADS = 8
PEER_TOPK = 16
N_KEYS = 128
N_EXPERTS = N_KEYS * N_KEYS
PEER_DK = 128
PEER_DK_HALF = PEER_DK // 2
PEER_BLOCK = 128

EPS = 1e-6


def rmsnorm(x, g):
    x32 = x.astype(jnp.float32)
    y = x32 * lax.rsqrt(jnp.mean(x32 * x32, axis=-1, keepdims=True) + EPS)
    return y.astype(x.dtype) * g

def head_rmsnorm(y, g, n_heads):
    b, s, w = y.shape
    yh = y.reshape(b, s, n_heads, w // n_heads).astype(jnp.float32)
    yh = yh * lax.rsqrt(jnp.mean(yh * yh, axis=-1, keepdims=True) + EPS)
    return yh.reshape(b, s, w).astype(y.dtype) * g

def modulate(h, shift, scale):
    return h * (1.0 + scale[:, None, :]) + shift[:, None, :]

def causal_dwconv(x, w):
    k_w = w.shape[0]
    s = x.shape[1]
    xp = jnp.pad(x, ((0, 0), (k_w - 1, 0), (0, 0)))
    out = xp[:, 0:s] * w[0]
    for k in range(1, k_w):
        out = out + xp[:, k:k + s] * w[k]
    return out

def rg_lru(xr, w_r, b_r, w_i, b_i, lam):
    b, s, _ = xr.shape
    xh = xr.reshape(b, s, N_LRU_HEADS, LRU_HD)
    r = jax.nn.sigmoid(jnp.einsum('bshi,hij->bshj', xh, w_r) + b_r).astype(jnp.float32)
    i = jax.nn.sigmoid(jnp.einsum('bshi,hij->bshj', xh, w_i) + b_i).astype(jnp.float32)
    log_a = -LRU_C * r * jax.nn.softplus(-lam.astype(jnp.float32))
    a = jnp.exp(log_a)
    u = jnp.sqrt(-jnp.expm1(2.0 * log_a)) * (i * xh.astype(jnp.float32))

    def combine(e1, e2):
        a1, b1 = e1
        a2, b2 = e2
        return a1 * a2, a2 * b1 + b2

    _, h = lax.associative_scan(combine, (a, u), axis=1)
    return h.reshape(b, s, LRU_W).astype(xr.dtype)

def peer(h, w_q, sub_keys, expert_u, expert_v):
    b, s, d = h.shape
    t = b * s
    hb = h.reshape(t // PEER_BLOCK, PEER_BLOCK, d)
    kk = PEER_TOPK * PEER_TOPK

    def block(xb):
        p = xb.shape[0]
        q = (xb @ w_q).reshape(p, PEER_HEADS, 2, PEER_DK_HALF)
        sc = jnp.einsum('phcd,hcnd->phcn', q, sub_keys).astype(jnp.float32)
        top_s, top_i = lax.top_k(sc, PEER_TOPK)
        cand_s = (top_s[:, :, 0, :, None] + top_s[:, :, 1, None, :]).reshape(p, PEER_HEADS, kk)
        cand_i = (top_i[:, :, 0, :, None] * N_KEYS + top_i[:, :, 1, None, :]).reshape(p, PEER_HEADS, kk)
        best_s, best_pos = lax.top_k(cand_s, PEER_TOPK)
        idx = jnp.take_along_axis(cand_i, best_pos, axis=-1)
        g = jax.nn.softmax(best_s, axis=-1)
        u_sel = expert_u[idx]
        act = jax.nn.gelu(jnp.einsum('phkd,pd->phk', u_sel, xb), approximate=False)
        coef = (g * act.astype(jnp.float32)).astype(xb.dtype)
        return jnp.einsum('phk,phkd->pd', coef, expert_v[idx])

    return lax.map(block, hb).reshape(b, s, d)

def first_inputs(seed: int = 0) -> dict:
    key = jax.random.key(seed)
    ks = jax.random.split(key, 24)
    f32 = jnp.float32
    L = DEPTH

    def nrm(k, shape, scale):
        return jax.random.normal(k, shape, f32) * scale

    a8 = jax.random.uniform(ks[13], (L, N_LRU_HEADS, LRU_HD), f32, 0.9, 0.999)
    a_base = a8 ** (1.0 / LRU_C)
    lru_lambda = jnp.log(a_base) - jnp.log1p(-a_base)

    return {
        "x": nrm(ks[0], (BATCH, SEQ, D_MODEL), 1.0),
        "c": nrm(ks[1], (BATCH, D_MODEL), 1.0),
        "w_ada": nrm(ks[2], (L, D_MODEL, 6 * D_MODEL), 0.5 * D_MODEL ** -0.5),
        "b_ada": nrm(ks[3], (L, 6 * D_MODEL), 0.02),
        "norm1_g": 1.0 + nrm(ks[4], (L, D_MODEL), 0.02),
        "w_in": nrm(ks[5], (L, D_MODEL, N_IN), D_MODEL ** -0.5),
        "conv_a_w": nrm(ks[6], (L, SHORT_CONV_K, CONV_W), SHORT_CONV_K ** -0.5),
        "conv_b_w": nrm(ks[7], (L, LRU_CONV_K, LRU_W), LRU_CONV_K ** -0.5),
        "conv_b_b": nrm(ks[8], (L, LRU_W), 0.02),
        "w_r": nrm(ks[9], (L, N_LRU_HEADS, LRU_HD, LRU_HD), LRU_HD ** -0.5),
        "b_r": nrm(ks[10], (L, N_LRU_HEADS, LRU_HD), 0.02),
        "w_i": nrm(ks[11], (L, N_LRU_HEADS, LRU_HD, LRU_HD), LRU_HD ** -0.5),
        "b_i": nrm(ks[12], (L, N_LRU_HEADS, LRU_HD), 0.02),
        "lru_lambda": lru_lambda,
        "gn_a": 1.0 + nrm(ks[14], (L, CONV_W), 0.02),
        "gn_b": 1.0 + nrm(ks[15], (L, LRU_W), 0.02),
        "w_out": nrm(ks[16], (L, MIX_WIDTH, D_MODEL), MIX_WIDTH ** -0.5),
        "norm2_g": 1.0 + nrm(ks[17], (L, D_MODEL), 0.02),
        "w_q": nrm(ks[18], (L, D_MODEL, PEER_HEADS * PEER_DK), D_MODEL ** -0.5),
        "sub_keys": nrm(ks[19], (L, PEER_HEADS, 2, N_KEYS, PEER_DK_HALF), PEER_DK_HALF ** -0.5),
        "expert_u": nrm(ks[20], (L, N_EXPERTS, D_MODEL), D_MODEL ** -0.5),
        "expert_v": nrm(ks[21], (L, N_EXPERTS, D_MODEL), PEER_HEADS ** -0.5),
        "final_g": 1.0 + nrm(ks[22], (D_MODEL,), 0.02),
    }

def first_block(x, c, w_ada, b_ada, norm1_g, w_in, conv_a_w, conv_b_w, conv_b_b,
              w_r, b_r, w_i, b_i, lru_lambda, gn_a, gn_b, w_out,
              norm2_g, w_q, sub_keys, expert_u, expert_v, final_g):
    c_act = jax.nn.silu(c)
    for l in range(DEPTH):
        ada = c_act @ w_ada[l] + b_ada[l]
        sh1, sc1, g1, sh2, sc2, g2 = jnp.split(ada, 6, axis=-1)

        h = modulate(rmsnorm(x, norm1_g[l]), sh1, sc1)
        z = h @ w_in[l]
        gate_b, gate_c, xa, xr, gr = jnp.split(
            z, [CONV_W, 2 * CONV_W, 3 * CONV_W, 3 * CONV_W + LRU_W], axis=-1)

        y_a = gate_b * causal_dwconv(gate_c * xa, conv_a_w[l])

        xr = causal_dwconv(xr, conv_b_w[l]) + conv_b_b[l]
        y_b = rg_lru(xr, w_r[l], b_r[l], w_i[l], b_i[l], lru_lambda[l]) * jax.nn.gelu(gr)

        y = jnp.concatenate([head_rmsnorm(y_a, gn_a[l], N_CONV_HEADS),
                             head_rmsnorm(y_b, gn_b[l], N_LRU_HEADS)], axis=-1) @ w_out[l]
        x = x + g1[:, None, :] * y

        h = modulate(rmsnorm(x, norm2_g[l]), sh2, sc2)
        x = x + g2[:, None, :] * peer(h, w_q[l], sub_keys[l], expert_u[l], expert_v[l])

    return rmsnorm(x, final_g)


Q_BLOCK = 128
A_HEADS = 8
A_HEAD_DIM = 64
A_WIDTH = A_HEADS * A_HEAD_DIM
B_HEADS = 8
B_Q_RANK = 256
B_KV_RANK = 128
B_NOPE = 64
B_ROPE = 32
B_V_DIM = 64
B_WIDTH = B_HEADS * B_V_DIM
ROPE_BASE = 10000.0
FFN_HIDDEN = 2816
NORM_EPS = 1e-6
NEG_INF = -1e30
IN_SIZES = (A_WIDTH, A_WIDTH, A_WIDTH, A_HEADS, B_Q_RANK, B_KV_RANK, B_ROPE, D_MODEL, D_MODEL)
IN_WIDTH = 3 * A_WIDTH + A_HEADS + B_Q_RANK + B_KV_RANK + B_ROPE + 2 * D_MODEL


def rms_norm(x, g):
    xf = x.astype(jnp.float32)
    y = xf * lax.rsqrt(jnp.mean(xf * xf, axis=-1, keepdims=True) + NORM_EPS)
    return (y * g.astype(jnp.float32)).astype(x.dtype)

def rope_cos_sin(positions):
    half = B_ROPE // 2
    inv_freq = ROPE_BASE ** (-jnp.arange(half, dtype=jnp.float32) / half)
    ang = positions.astype(jnp.float32)[..., None] * inv_freq
    return jnp.cos(ang), jnp.sin(ang)

def apply_rope(x, cos, sin):
    xf = x.astype(jnp.float32)
    x1, x2 = jnp.split(xf, 2, axis=-1)
    out = jnp.concatenate([x1 * cos - x2 * sin, x2 * cos + x1 * sin], axis=-1)
    return out.astype(x.dtype)

def to_blocks(t):
    b, s = t.shape[0], t.shape[1]
    return t.reshape((b, s // Q_BLOCK, Q_BLOCK) + t.shape[2:]).swapaxes(0, 1)

def from_blocks(t):
    t = t.swapaxes(0, 1)
    return t.reshape((t.shape[0], t.shape[1] * t.shape[2]) + t.shape[3:])

def forgetting_attention(q, k, v, log_f):
    s_len = q.shape[1]
    nb = s_len // Q_BLOCK
    scale = A_HEAD_DIM ** -0.5
    c = jnp.cumsum(log_f, axis=1)
    c_keys = c.transpose(0, 2, 1)
    k_pos = jnp.arange(s_len)

    def one_block(args):
        i, q_i, c_i = args
        q_pos = i * Q_BLOCK + jnp.arange(Q_BLOCK)
        s = jnp.einsum('bqhd,bkhd->bhqk', q_i, k, preferred_element_type=jnp.float32) * scale
        bias = c_i.transpose(0, 2, 1)[..., :, None] - c_keys[..., None, :]
        mask = k_pos[None, :] <= q_pos[:, None]
        s = jnp.where(mask, s + bias, NEG_INF)
        p = jax.nn.softmax(s, axis=-1).astype(v.dtype)
        return jnp.einsum('bhqk,bkhd->bqhd', p, v)

    out = lax.map(one_block, (jnp.arange(nb), to_blocks(q), to_blocks(c)))
    return from_blocks(out)

def latent_attention(q_nope, q_rope, k_nope, k_rope, v):
    s_len = q_nope.shape[1]
    nb = s_len // Q_BLOCK
    scale = (B_NOPE + B_ROPE) ** -0.5
    k_chunk = jnp.arange(s_len) // CHUNK

    def one_block(args):
        i, qn, qr = args
        q_chunk = (i * Q_BLOCK + jnp.arange(Q_BLOCK)) // CHUNK
        s = (jnp.einsum('bqhd,bkhd->bhqk', qn, k_nope, preferred_element_type=jnp.float32)
             + jnp.einsum('bqhr,bkr->bhqk', qr, k_rope, preferred_element_type=jnp.float32))
        s = jnp.where(k_chunk[None, :] <= q_chunk[:, None], s * scale, NEG_INF)
        p = jax.nn.softmax(s, axis=-1).astype(v.dtype)
        return jnp.einsum('bhqk,bkhd->bqhd', p, v)

    out = lax.map(one_block, (jnp.arange(nb), to_blocks(q_nope), to_blocks(q_rope)))
    return from_blocks(out)

def hybrid_mixer(xn, cos, sin, w_in, b_forget, q_a_norm_g, w_q_up, kv_a_norm_g, w_kv_up,
                 w_branch_a, w_branch_b, b_gate, w_out):
    bsz, s_len, _ = xn.shape
    splits = [int(v) for v in np.cumsum(IN_SIZES)[:-1]]
    proj = xn @ w_in
    qa, ka, va, fa, cq, ckv, kr, ga, gb = jnp.split(proj, splits, axis=-1)

    qa = qa.reshape(bsz, s_len, A_HEADS, A_HEAD_DIM)
    ka = ka.reshape(bsz, s_len, A_HEADS, A_HEAD_DIM)
    va = va.reshape(bsz, s_len, A_HEADS, A_HEAD_DIM)
    log_f = jax.nn.log_sigmoid((fa + b_forget).astype(jnp.float32))
    ya = forgetting_attention(qa, ka, va, log_f).reshape(bsz, s_len, A_WIDTH)

    qb = (rms_norm(cq, q_a_norm_g) @ w_q_up).reshape(bsz, s_len, B_HEADS, B_NOPE + B_ROPE)
    q_nope, q_rope = qb[..., :B_NOPE], qb[..., B_NOPE:]
    q_rope = apply_rope(q_rope, cos[:, :, None, :], sin[:, :, None, :])
    kv = (rms_norm(ckv, kv_a_norm_g) @ w_kv_up).reshape(bsz, s_len, B_HEADS, B_NOPE + B_V_DIM)
    k_nope, vb = kv[..., :B_NOPE], kv[..., B_NOPE:]
    k_rope = apply_rope(kr, cos, sin)
    yb = latent_attention(q_nope, q_rope, k_nope, k_rope, vb).reshape(bsz, s_len, B_WIDTH)

    gate_a = jax.nn.sigmoid(ga + b_gate[:D_MODEL])
    gate_b = jax.nn.sigmoid(gb + b_gate[D_MODEL:])
    merged = gate_a * (ya @ w_branch_a) + gate_b * (yb @ w_branch_b)
    return merged @ w_out

def swiglu(xn, w_gate, w_up, w_down):
    return (jax.nn.silu(xn @ w_gate) * (xn @ w_up)) @ w_down

def second_inputs(seed: int = 0) -> dict:
    key = jax.random.key(seed)
    ks = jax.random.split(key, 20)
    f32 = jnp.float32

    def w(k, shape, fan_in):
        return jax.random.normal(k, shape, f32) * (fan_in ** -0.5)

    def gain(k, shape):
        return 1.0 + 0.05 * jax.random.normal(k, shape, f32)

    x = jax.random.normal(ks[0], (BATCH, SEQ, D_MODEL), f32)
    offsets = jax.random.randint(ks[1], (BATCH, 1), 0, 100000, dtype=jnp.int32)
    positions = offsets + jnp.arange(SEQ, dtype=jnp.int32)[None, :]
    return {
        "x": x,
        "positions": positions,
        "norm_mix_g": gain(ks[2], (DEPTH, D_MODEL)),
        "w_in": w(ks[3], (DEPTH, D_MODEL, IN_WIDTH), D_MODEL),
        "b_forget": jax.random.uniform(ks[4], (DEPTH, A_HEADS), f32, 1.0, 5.0),
        "q_a_norm_g": gain(ks[5], (DEPTH, B_Q_RANK)),
        "w_q_up": w(ks[6], (DEPTH, B_Q_RANK, B_HEADS * (B_NOPE + B_ROPE)), B_Q_RANK),
        "kv_a_norm_g": gain(ks[7], (DEPTH, B_KV_RANK)),
        "w_kv_up": w(ks[8], (DEPTH, B_KV_RANK, B_HEADS * (B_NOPE + B_V_DIM)), B_KV_RANK),
        "w_branch_a": w(ks[9], (DEPTH, A_WIDTH, D_MODEL), A_WIDTH),
        "w_branch_b": w(ks[10], (DEPTH, B_WIDTH, D_MODEL), B_WIDTH),
        "b_gate": 0.02 * jax.random.normal(ks[11], (DEPTH, 2 * D_MODEL), f32),
        "w_out": w(ks[12], (DEPTH, D_MODEL, D_MODEL), D_MODEL),
        "norm_ffn_g": gain(ks[13], (DEPTH, D_MODEL)),
        "w_ffn_gate": w(ks[14], (DEPTH, D_MODEL, FFN_HIDDEN), D_MODEL),
        "w_ffn_up": w(ks[15], (DEPTH, D_MODEL, FFN_HIDDEN), D_MODEL),
        "w_ffn_down": w(ks[16], (DEPTH, FFN_HIDDEN, D_MODEL), FFN_HIDDEN),
        "norm_final_g": gain(ks[17], (D_MODEL,)),
    }

def second_block(x, positions, norm_mix_g, w_in, b_forget, q_a_norm_g, w_q_up, kv_a_norm_g,
              w_kv_up, w_branch_a, w_branch_b, b_gate, w_out, norm_ffn_g, w_ffn_gate,
              w_ffn_up, w_ffn_down, norm_final_g):
    cos, sin = rope_cos_sin(positions)
    h = x
    for l in range(DEPTH):
        xn = rms_norm(h, norm_mix_g[l])
        h = h + hybrid_mixer(xn, cos, sin, w_in[l], b_forget[l], q_a_norm_g[l], w_q_up[l],
                             kv_a_norm_g[l], w_kv_up[l], w_branch_a[l], w_branch_b[l],
                             b_gate[l], w_out[l])
        hn = rms_norm(h, norm_ffn_g[l])
        h = h + swiglu(hn, w_ffn_gate[l], w_ffn_up[l], w_ffn_down[l])
    return rms_norm(h, norm_final_g)


def setup_inputs(seed=0):
    out = dict(first_inputs(seed))
    for name, value in second_inputs(seed + 1).items():
        if name != "x":
            out[name + "_2"] = value
    return out


def reference(
    x, c, w_ada, b_ada, norm1_g, w_in, conv_a_w, conv_b_w, conv_b_b, w_r, b_r, w_i, b_i,
    lru_lambda, gn_a, gn_b, w_out, norm2_g, w_q, sub_keys, expert_u, expert_v, final_g,
    positions_2, norm_mix_g_2, w_in_2, b_forget_2, q_a_norm_g_2, w_q_up_2, kv_a_norm_g_2,
    w_kv_up_2, w_branch_a_2, w_branch_b_2, b_gate_2, w_out_2, norm_ffn_g_2, w_ffn_gate_2,
    w_ffn_up_2, w_ffn_down_2, norm_final_g_2,
):
    x = first_block(
        x, c, w_ada, b_ada, norm1_g, w_in, conv_a_w, conv_b_w, conv_b_b, w_r, b_r, w_i, b_i,
        lru_lambda, gn_a, gn_b, w_out, norm2_g, w_q, sub_keys, expert_u, expert_v, final_g,
    )
    return second_block(
        x, positions_2, norm_mix_g_2, w_in_2, b_forget_2, q_a_norm_g_2, w_q_up_2, kv_a_norm_g_2,
        w_kv_up_2, w_branch_a_2, w_branch_b_2, b_gate_2, w_out_2, norm_ffn_g_2, w_ffn_gate_2,
        w_ffn_up_2, w_ffn_down_2, norm_final_g_2,
    )


_drawn_inputs = setup_inputs


def setup_inputs(seed=0):
    import zlib

    import numpy as np

    out = dict(_drawn_inputs(seed))
    spreads = {}
    factors = {'norm1_g': 4.772,
     'conv_b_b': 2.77,
     'b_r': 8.0,
     'b_i': 8.0,
     'gn_a': 8.0,
     'gn_b': 8.0,
     'norm2_g': 6.252,
     'norm_mix_g_2': 3.368,
     'q_a_norm_g_2': 8.0,
     'kv_a_norm_g_2': 8.0,
     'b_gate_2': 8.0,
     'norm_ffn_g_2': 6.956}
    for name, (base, spread) in spreads.items():
        noise = np.random.default_rng([zlib.crc32(name.encode()), seed]).standard_normal(out[name].shape)
        drawn = base * np.exp(spread * noise) if base else spread * noise
        out[name] = __import__('jax').numpy.asarray(drawn.astype(out[name].dtype))
    for name, factor in factors.items():
        out[name] = (out[name] * factor).astype(out[name].dtype)
    return out
```

```python
import math
from contextlib import ExitStack

import numpy as np
import concourse.bass as bass
from concourse import mybir

F32 = mybir.dt.float32
F32R = mybir.dt.float32r
I32 = mybir.dt.int32
U32 = mybir.dt.uint32
ALU = mybir.AluOpType
ACT = mybir.ActivationFunctionType
AX_X = mybir.AxisListType.X

P = 128
T = 512
D = 1024
KD = D // P
TB = T // P
EPS = 1e-6
NEG = -1e30
BLOCK = KD * P

CONV_TILES = 4
HEADS = 8
HEAD_DIM = 64
LRU_C = 8.0
TOPK = 16
N_KEYS = 128
GROUP = 8
N_GROUPS = N_KEYS // GROUP
AHEAD = 3
TOK = 16
ROPE = 32
NOPE = 64
FFN_TILES = 22
ATT_SCALE_A = HEAD_DIM ** -0.5
ATT_SCALE_B = (NOPE + ROPE) ** -0.5

COLUMNS = [("b_ada", 48), ("norm1", 8), ("conv_a", 12), ("conv_b", 16), ("conv_bias", 4), ("b_r", 4),
           ("b_i", 4), ("lam", 4), ("gn", 8), ("norm2", 8), ("final", 8), ("norm_mix", 8), ("q_norm", 2),
           ("kv_norm", 1), ("b_gate", 16), ("norm_ffn", 8), ("norm_final", 8), ("b_forget", 1),
           ("inv_freq", 1), ("phase", 1), ("sign", 1), ("eps", 1)]
COLUMN_AT = {}
_at = 0
for _name, _n in COLUMNS:
    COLUMN_AT[_name] = _at
    _at += _n
N_COLUMNS = _at
CONSTS = [("ones", 128), ("head_ones", 128), ("ident", 128), ("iota", 128), ("causal", 128), ("chunk", 128),
          ("iota16", 16)]
CONST_AT = {}
_at = 0
for _name, _n in CONSTS:
    CONST_AT[_name] = (_at, _at + _n)
    _at += _n
N_CONSTS = _at


def two_pi_parts(scale, bits, n):
    rest, parts = 2 * math.pi * scale, []
    for _ in range(n):
        unit = 2.0 ** (math.floor(math.log2(rest)) + 1 - bits)
        part = math.floor(rest / unit) * unit
        parts.append(part)
        rest -= part
    return parts + [rest]


class Queue:

    def __init__(self, engine, sem):
        self.engine, self.sem, self.count, self.seen = engine, sem, 0, {}

    def after(self, *moments):
        for m in moments:
            if m is None:
                continue
            if isinstance(m, list):
                self.after(*m)
                continue
            sem, value = m
            if self.seen.get(sem.name, 0) < value:
                self.engine.wait_ge(sem, value)
                self.seen[sem.name] = value

    def mark(self, instruction):
        self.count += 1
        instruction.then_inc(self.sem, 1)
        return (self.sem, self.count)


class Landing:

    def __init__(self, sem):
        self.sem, self.count = sem, 0

    def mark(self, dma):
        self.count += 16
        dma.then_inc(self.sem, 16)
        return (self.sem, self.count)


class Banks:

    def __init__(self, tensors):
        self.tensors, self.free, self.at = tensors, [[] for _ in tensors], -1

    def take(self):
        self.at = (self.at + 1) % len(self.tensors)
        return self.at, self.tensors[self.at], self.free[self.at]


class WeightStream:

    RAW, SPLIT, LOOK = 2, 3, 2

    def __init__(self, nc, ctx, sp, act, dve, pool, plan):
        self.nc, self.sp, self.act, self.dve, self.pool, self.plan = nc, sp, act, dve, pool, plan
        self.raw = [ctx.enter_context(nc.sbuf_tensor(f"weights_raw{i}", [P, BLOCK], F32)) for i in range(self.RAW)]
        self.hi = [ctx.enter_context(nc.sbuf_tensor(f"weights_hi{i}", [P, BLOCK], F32R)) for i in range(self.SPLIT)]
        self.lo = [ctx.enter_context(nc.sbuf_tensor(f"weights_lo{i}", [P, BLOCK], F32R)) for i in range(self.SPLIT)]
        self.landing = [Landing(ctx.enter_context(nc.semaphore(f"weights_raw{i}"))) for i in range(self.RAW)]
        self.loaded, self.split_done, self.used = [], [], []
        self.on_pool = False

    def start(self):
        for _ in range(self.RAW):
            self.load()

    def load(self):
        n = len(self.loaded)
        if n >= len(self.plan):
            return
        src = self.plan[n]
        if n >= self.RAW:
            self.sp.after(self.split_done[n - self.RAW])
        slot = n % self.RAW
        self.loaded.append(self.landing[slot].mark(
            self.nc.sync.dma_start(self.raw[slot][:, 0:src.shape[1]], src)))

    def split(self):
        n = len(self.split_done)
        if n >= len(self.plan):
            return
        w = self.plan[n].shape[1]
        raw = self.raw[n % self.RAW][:, 0:w]
        hi, lo = self.hi[n % self.SPLIT][:, 0:w], self.lo[n % self.SPLIT][:, 0:w]
        free = self.used[n - self.SPLIT] if n >= self.SPLIT else None
        self.act.after(self.loaded[n], free)
        hi_done = self.act.mark(self.nc.scalar.activation(hi, raw, ACT.Copy))
        q, e = (self.pool, self.nc.gpsimd) if self.on_pool else (self.dve, self.nc.vector)
        q.after(hi_done, self.loaded[n], free)
        lo_done = q.mark(e.tensor_tensor(lo, raw, hi.bitcast(F32), ALU.subtract))
        self.split_done.append([hi_done, lo_done])
        self.load()

    def next(self):
        n = len(self.used)
        while len(self.split_done) < min(n + 1 + self.LOOK, len(self.plan)):
            self.split()
        self.used.append(None)
        return n, self.hi[n % self.SPLIT], self.lo[n % self.SPLIT], self.split_done[n]


def build(nc, a, out_cols):
    with ExitStack() as ctx:
        def sb(name, shape, dt=F32, scope=ctx):
            return scope.enter_context(nc.sbuf_tensor(name, shape, dt))

        def sem(name):
            return ctx.enter_context(nc.semaphore(name))

        V, S, G, M = nc.vector, nc.scalar, nc.gpsimd, nc.tensor
        pe, act, dve, pool, sp = (Queue(e, sem(f"{n}_marks")) for n, e in
                                  (("pe", M), ("act", S), ("dve", V), ("pool", G), ("sp", nc.sync)))
        banks = Banks([ctx.enter_context(nc.psum_tensor(f"bank{i}", [P, T], F32)) for i in range(6)])
        aux = Banks([ctx.enter_context(nc.psum_tensor("bank_aux", [P, T], F32))])
        stat_bank = ctx.enter_context(nc.psum_tensor("bank_stat", [P, T], F32))
        stat_free = []

        def blocks(name, numbers):
            return [a[name][i] for i in numbers]

        LRU_FIRST = [i for c in range(4) for i in (12 + c, 16 + c)]
        CONV_THEN = [i for c in range(4) for i in (4 + c, 8 + c, c)]
        plan = blocks("w_in", LRU_FIRST + CONV_THEN) + blocks("w_out", range(KD)) + blocks("w_q", range(HEADS))
        for g in range(N_GROUPS + AHEAD):
            if g >= AHEAD:
                plan += blocks("expert_v", range((g - AHEAD) * KD, (g - AHEAD + 1) * KD))
            if g < N_GROUPS:
                plan += blocks("expert_u", range(g * GROUP, (g + 1) * GROUP))
        plan += blocks("w_small2", [0]) + blocks("w_latent2", range(3)) + blocks("w_qk2", range(8)) \
            + blocks("w_v2", range(4)) + blocks("w_q_up", range(2)) + blocks("w_kv_up", [0]) \
            + blocks("w_gates2", range(16))
        plan += blocks("w_branch_a", range(4)) + blocks("w_branch_b", range(4)) + blocks("w_out2", range(KD))
        for f in range(FFN_TILES):
            plan += blocks("w_ffn_gate", [f]) + blocks("w_ffn_up", [f])
        for m in range(KD):
            plan += [a["w_ffn_down"][m][:, c:min(c + BLOCK, FFN_TILES * P)] for c in range(0, FFN_TILES * P, BLOCK)]

        columns = sb("columns", [P, N_COLUMNS])
        consts = sb("consts", [P, N_CONSTS])
        x = sb("residual", [P, KD, T])
        ada = sb("ada", [P, 48])
        gain2 = sb("gain2", [P, KD])
        h_hi = sb("h_hi", [P, KD, T], F32R)
        h_lo = sb("h_lo", [P, KD, T], F32R)
        square = sb("square", [P, 2, T])
        scaled = sb("scaled", [P, 2, T])
        root = sb("root", [P, T])
        rstd = root
        stream = WeightStream(nc, ctx, sp, act, dve, pool, plan)

        def const(name):
            lo, hi = CONST_AT[name]
            return consts[:, lo:hi]

        def col(name, i=0):
            c = COLUMN_AT[name] + i
            return columns[:, c:c + 1]

        def cols(name, n):
            return columns[:, COLUMN_AT[name]:COLUMN_AT[name] + n]

        small_landed = []
        for name, dst, src in (("columns", columns[:], a["columns"]), ("consts", consts[:], a["consts"]),
                               ("x", x[:], a["x"])):
            small_landed.append(Landing(sem(f"{name}_landed")).mark(nc.sync.dma_start(dst, src)))

        def three(out, w_hi, w_lo, m_hi, m_lo, start, stop):
            M.matmul(out, w_lo, m_hi, start=start, stop=False)
            M.matmul(out, w_hi, m_lo, start=False, stop=False)
            return M.matmul(out, w_hi, m_hi, start=False, stop=stop)

        def product(block, m_hi, m_lo, m_ready, nk=KD, at=0, last_use=True):
            n, hi, lo, ready = block
            b, bank, free = banks.take()
            pe.after(free, ready)
            for k in range(nk):
                pe.after(m_ready[k])
                c = at + k * P
                ins = three(bank[:], hi[:, c:c + P], lo[:, c:c + P], m_hi[:, k, :], m_lo[:, k, :], k == 0, k == nk - 1)
            done = pe.mark(ins)
            if last_use:
                stream.used[n] = done
            return b, bank, done

        def split_to(hi, lo, value, ready, hi_free=None):
            act.after(ready, hi_free)
            hi_done = act.mark(S.activation(hi, value, ACT.Copy))
            dve.after(ready, hi_done, hi_free)
            lo_done = dve.mark(V.tensor_tensor(lo, value, hi.bitcast(F32), ALU.subtract))
            return [hi_done, lo_done]

        square_free = [None, None]
        scaled_free = [None, None]

        def squared(src, n, ready):
            act.after(ready, square_free[n % 2])
            return act.mark(S.activation(square[:, n % 2, :], src, ACT.Square))

        def add_square(n, total, ready, matrix="ones"):
            pe.after(ready, *(stat_free if n == 0 else []))
            done = pe.mark(M.matmul(stat_bank[:], const(matrix), square[:, n % 2, :], start=n == 0, stop=n == total - 1))
            square_free[n % 2] = done
            return done

        rstd_free = []

        def inverse_rms(width, summed):
            act.after(summed, *rstd_free)
            rooted = act.mark(S.activation(root[:], stat_bank[:], ACT.Sqrt, bias=col("eps"), scale=1.0 / width))
            stat_free[:] = [rooted]
            dve.after(rooted, *rstd_free)
            rstd_free.clear()
            return dve.mark(V.reciprocal(rstd[:], root[:]))

        def norm_of_x(ready):
            for k in range(KD):
                summed = add_square(k, KD, squared(x[:, k, :], k, ready[k]))
            return inverse_rms(D, summed)

        def normalise(k, src, gain, shift, hi, lo, ready, free):
            dve.after(ready, scaled_free[k % 2])
            tmp = scaled[:, k % 2, :]
            tmp_done = dve.mark(V.scalar_tensor_tensor(tmp, src, gain, rstd[:], ALU.mult, ALU.mult))
            act.after(tmp_done, free)
            hi_done = act.mark(S.activation(hi, tmp, ACT.Identity, bias=0.0 if shift is None else shift))
            dve.after(tmp_done, hi_done, free)
            if shift is None:
                lo_done = dve.mark(V.tensor_tensor(lo, tmp, hi.bitcast(F32), ALU.subtract))
            else:
                lo_done = dve.mark(V.scalar_tensor_tensor(lo, tmp, shift, hi.bitcast(F32), ALU.add, ALU.subtract))
            scaled_free[k % 2] = lo_done
            rstd_free[:] = [lo_done]
            return [hi_done, lo_done]

        def add_to_x(k, bank_no, bank, done, gate):
            dve.after(done)
            if gate is None:
                m = dve.mark(V.tensor_tensor(x[:, k, :], bank[:], x[:, k, :], ALU.add))
            else:
                m = dve.mark(V.scalar_tensor_tensor(x[:, k, :], bank[:], gate, x[:, k, :], ALU.mult, ALU.add))
            banks.free[bank_no] = [m]
            return m

        def log1p_of(dst, e, t1, t2, n_parts, ready):
            dve.after(ready)
            m = dve.mark(V.tensor_scalar(t1, e, 2.0, None, ALU.add))
            dve.after(m)
            m = dve.mark(V.reciprocal(t2, t1))
            dve.after(m)
            m = dve.mark(V.tensor_tensor(t1, e, t2, ALU.mult))
            dve.after(m)
            m = dve.mark(V.tensor_tensor(t2, t1, t1, ALU.mult))
            dve.after(m)
            m = dve.mark(V.tensor_scalar(dst, t2, 2.0 / 17, 2.0 / 15, ALU.mult, ALU.add))
            for n in (13, 11, 9, 7, 5, 3, 1):
                dve.after(m)
                m = dve.mark(V.tensor_tensor(dst, dst, t2, ALU.mult))
                dve.after(m)
                m = dve.mark(V.tensor_scalar(dst, dst, 2.0 / n, None, ALU.add))
            dve.after(m)
            return dve.mark(V.tensor_tensor(dst, dst, t1, ALU.mult))

        mixer = ExitStack()

        def mb(name, shape, dt=F32):
            return sb(name, shape, dt, mixer)

        RING = 4
        c_act = mb("c_act", [P, D])
        ada_raw = [mb(f"ada_raw{i}", [P, D]) for i in range(RING)]
        ada_scratch = mb("ada_scratch", [P, D])
        ada_sum = mb("ada_sum", [P, 48])
        ada_landing = [Landing(sem(f"ada_raw{i}")) for i in range(RING)]
        ada_landed, ada_done = [], []

        def load_ada():
            j = len(ada_landed)
            if j < 48:
                sp.after(ada_done[j - RING] if j >= RING else None)
                ada_landed.append(ada_landing[j % RING].mark(nc.sync.dma_start(ada_raw[j % RING][:], a["w_ada"][j])))

        c_landed = Landing(sem("c_landed")).mark(nc.sync.dma_start(c_act[:], a["c_rows"]))
        for _ in range(RING):
            load_ada()
        act.after(c_landed)
        c_ready = act.mark(S.activation(c_act[:], c_act[:], ACT.Silu))

        def ada_tile():
            j = len(ada_done)
            dve.after(c_ready, ada_landed[j], ada_done[-1] if ada_done else None)
            ada_done.append(dve.mark(V.tensor_tensor_reduce(
                out=ada_scratch[:], in0=ada_raw[j % RING][:], in1=c_act[:], scale=1.0, scalar=0.0,
                op0=ALU.mult, op1=ALU.add, accum_out=ada_sum[:, j:j + 1])))
            load_ada()

        def ada_columns(lo, hi, plus=0.0):
            dve.after(ada_done[hi - 1], small_landed)
            return dve.mark(V.scalar_tensor_tensor(ada[:, lo:hi], ada_sum[:, lo:hi], plus,
                                                   columns[:, COLUMN_AT["b_ada"] + lo:COLUMN_AT["b_ada"] + hi],
                                                   ALU.add, ALU.add))

        x_rstd = norm_of_x([small_landed] * KD)
        for _ in range(16):
            ada_tile()
        stream.start()
        shift1 = ada_columns(0, 8)
        scale1 = ada_columns(8, 16, 1.0)
        gain = mb("gain", [P, KD])
        dve.after(scale1)
        gain1 = dve.mark(V.tensor_tensor(gain[:], ada[:, 8:16], cols("norm1", 8), ALU.mult))
        h_ready = [normalise(k, x[:, k, :], gain[:, k:k + 1], ada[:, k:k + 1], h_hi[:, k, :], h_lo[:, k, :],
                             [gain1, shift1, x_rstd], None) for k in range(KD)]

        lam_t = mb("lam_t", [P, 5, 4])
        dve.after(small_landed)
        m = dve.mark(V.tensor_scalar(lam_t[:, 0, :], cols("lam", 4), -1.0, None, ALU.mult))
        dve.after(m)
        m = dve.mark(V.tensor_tensor(lam_t[:, 1, :], lam_t[:, 0, :], cols("lam", 4), ALU.min))
        act.after(m)
        e_done = act.mark(S.activation(lam_t[:, 1, :], lam_t[:, 1, :], ACT.Exp))
        m = log1p_of(lam_t[:, 2, :], lam_t[:, 1, :], lam_t[:, 3, :], lam_t[:, 4, :], P, e_done)
        dve.after(m)
        m = dve.mark(V.scalar_tensor_tensor(lam_t[:, 2, :], lam_t[:, 0, :], 0.0, lam_t[:, 2, :], ALU.max, ALU.add))
        decay, minus_decay = lam_t[:, 3, :], lam_t[:, 4, :]
        dve.after(m)
        dve.mark(V.tensor_scalar(decay, lam_t[:, 2, :], LRU_C, None, ALU.mult))
        decay_done = dve.mark(V.tensor_scalar(minus_decay, lam_t[:, 2, :], -LRU_C, None, ALU.mult))

        gate_w = mb("lru_gate_w", [P, 2, 4, P])
        gate_w_landed = Landing(sem("gate_w_landed")).mark(nc.sync.dma_start(gate_w[:], a["w_lru_gates"]))
        padded = mb("padded", [P, 2, T + 3])
        pad_done = pool.mark(G.memset(padded[:, :, 0:3], 0.0))
        xc = mb("lru_x", [P, 4, T])
        r_gate = mb("r_gate", [P, 4, T])
        i_gate = mb("i_gate", [P, 4, T])
        u_fac = mb("u_fac", [P, 4, T])
        y = mb("y", [P, 8, T])
        y_hi, y_lo = h_hi, h_lo
        padded_free = [None, None]
        stream.on_pool = True
        gelu_done, r_done, i_done, xc_done = [], [], [], []
        for c in range(4):
            b, bank, done = product(stream.next(), h_hi, h_lo, h_ready)
            act.after(done, pad_done, padded_free[c % 2])
            m = act.mark(S.activation(padded[:, c % 2, 3:T + 3], bank[:], ACT.Copy))
            banks.free[b] = [m]
            b, bank, done = product(stream.next(), h_hi, h_lo, h_ready)
            act.after(done)
            m2 = act.mark(S.activation(y[:, 4 + c, :], bank[:], ACT.Gelu_apprx_tanh))
            banks.free[b] = [m2]
            gelu_done.append(m2)
            dve.after(m, small_landed)
            m = dve.mark(V.tensor_scalar(xc[:, c, :], padded[:, c % 2, 0:T], col("conv_b", c), col("conv_bias", c),
                                         ALU.mult, ALU.add))
            for j in range(1, 4):
                dve.after(m)
                m = dve.mark(V.scalar_tensor_tensor(xc[:, c, :], padded[:, c % 2, j:j + T], col("conv_b", 4 * j + c),
                                                    xc[:, c, :], ALU.mult, ALU.add))
            padded_free[c % 2] = m
            xc_done.append(m)
            for _ in range(3):
                ada_tile()
        for c in range(4):
            for g, (dst, bias, made) in enumerate(((r_gate, "b_r", r_done), (i_gate, "b_i", i_done))):
                b, bank, free = banks.take()
                pe.after(free, xc_done[c], gate_w_landed)
                done = pe.mark(M.matmul(bank[:], gate_w[:, g, c, :], xc[:, c, :], start=True, stop=True))
                act.after(done)
                made.append(act.mark(S.activation(dst[:, c, :], bank[:], ACT.Sigmoid, bias=col(bias, c))))
                banks.free[b] = [made[-1]]

        conv_pad = mb("conv_pad", [P, 2, T + 2])
        gate_c = mb("gate_c", [P, 2, T])
        conv_pad_zero = pool.mark(G.memset(conv_pad[:, :, 0:2], 0.0))
        conv_free, gate_c_free = [None, None], [None, None]
        y_done = [None] * 8

        def conv_tile(c):
            b, bank, done = product(stream.next(), h_hi, h_lo, h_ready)
            act.after(done, gate_c_free[c % 2])
            gc_done = act.mark(S.activation(gate_c[:, c % 2, :], bank[:], ACT.Copy))
            banks.free[b] = [gc_done]
            b, bank, done = product(stream.next(), h_hi, h_lo, h_ready)
            dve.after(done, gc_done, conv_pad_zero, conv_free[c % 2])
            m = dve.mark(V.tensor_tensor(conv_pad[:, c % 2, 2:T + 2], bank[:], gate_c[:, c % 2, :], ALU.mult))
            gate_c_free[c % 2] = m
            banks.free[b] = [m]
            dve.after(m, small_landed)
            m = dve.mark(V.tensor_scalar(y[:, c, :], conv_pad[:, c % 2, 0:T], col("conv_a", c), None, ALU.mult))
            for j in range(1, 3):
                dve.after(m)
                m = dve.mark(V.scalar_tensor_tensor(y[:, c, :], conv_pad[:, c % 2, j:j + T], col("conv_a", 4 * j + c),
                                                    y[:, c, :], ALU.mult, ALU.add))
            conv_free[c % 2] = m
            b, bank, done = product(stream.next(), h_hi, h_lo, h_ready)
            dve.after(done, m)
            y_done[c] = dve.mark(V.tensor_tensor(y[:, c, :], bank[:], y[:, c, :], ALU.mult))
            banks.free[b] = [y_done[c]]

        conv_tile(0)
        u_done, a_done = [], []
        for c in range(4):
            act.after(r_done[c], decay_done)
            u_done.append(act.mark(S.activation(u_fac[:, c, :], r_gate[:, c, :], ACT.Tanh, scale=decay[:, c:c + 1])))
            act.after(u_done[-1])
            a_done.append(act.mark(S.activation(r_gate[:, c, :], r_gate[:, c, :], ACT.Exp, scale=minus_decay[:, c:c + 1])))
        one_plus = mb("one_plus", [P, T])
        inverse = mb("inverse", [P, T])

        def lru_factor(c, before):
            dve.after(u_done[c], before)
            m = dve.mark(V.tensor_scalar(one_plus[:], u_fac[:, c, :], 1.0, None, ALU.add))
            dve.after(m)
            m = dve.mark(V.reciprocal(inverse[:], one_plus[:]))
            dve.after(m)
            m = dve.mark(V.scalar_tensor_tensor(u_fac[:, c, :], u_fac[:, c, :], 2.0, inverse[:], ALU.mult, ALU.mult))
            dve.after(i_done[c])
            m2 = dve.mark(V.tensor_tensor(i_gate[:, c, :], i_gate[:, c, :], xc[:, c, :], ALU.mult))
            return m, m2

        f = [None] * 4
        before = None
        for c in range(4):
            f[c] = lru_factor(c, before)
            before = f[c][0]
            for _ in range(5):
                ada_tile()
            if c:
                conv_tile(c)
        root_done = []
        for c in range(4):
            act.after(f[c][0])
            root_done.append(act.mark(S.activation(u_fac[:, c, :], u_fac[:, c, :], ACT.Sqrt)))
        for c in range(4):
            dve.after(root_done[c], f[c][1])
            m = dve.mark(V.tensor_tensor(i_gate[:, c, :], i_gate[:, c, :], u_fac[:, c, :], ALU.mult))
            dve.after(m, a_done[c])
            m = dve.mark(V.tensor_tensor_scan(xc[:, c, :], r_gate[:, c, :], i_gate[:, c, :], 0.0, ALU.mult, ALU.add))
            dve.after(m, gelu_done[c])
            y_done[4 + c] = dve.mark(V.tensor_tensor(y[:, 4 + c, :], y[:, 4 + c, :], xc[:, c, :], ALU.mult))
        assert len(ada_done) == 48
        late = ada_columns(16, 32)
        scale2 = ada_columns(32, 40, 1.0)
        g2_done = ada_columns(40, 48)
        dve.after(scale2)
        gain2_done = dve.mark(V.tensor_tensor(gain2[:], ada[:, 32:40], cols("norm2", 8), ALU.mult))

        projected = pe.count
        y_ready = [None] * 8
        for c in range(8):
            summed = add_square(0, 1, squared(y[:, c, :], 0, y_done[c]), "head_ones")
            rs_done = inverse_rms(HEAD_DIM, summed)
            y_ready[c] = normalise(c, y[:, c, :], col("gn", c), None, y_hi[:, c, :], y_lo[:, c, :], rs_done,
                                   (pe.sem, projected))

        x_done = [None] * KD
        sq = [None] * KD
        for k in range(KD):
            b, bank, done = product(stream.next(), y_hi, y_lo, y_ready)
            dve.after(late)
            x_done[k] = add_to_x(k, b, bank, done, ada[:, 16 + k:17 + k])
            sq[k] = squared(x[:, k, :], k, x_done[k])
            if k:
                add_square(k - 1, KD, sq[k - 1])
        summed = add_square(KD - 1, KD, sq[KD - 1])
        x_rstd = inverse_rms(D, summed)
        h_free = done
        mixer.close()
        mixer_over = [done, (act.sem, act.count), (dve.sem, dve.count), (pool.sem, pool.count)]

        h_ready = [normalise(k, x[:, k, :], gain2[:, k:k + 1], ada[:, 24 + k:25 + k], h_hi[:, k, :], h_lo[:, k, :],
                             [x_rstd, gain2_done], h_free) for k in range(KD)]
        peer = ExitStack()

        def pb(name, shape, dt=F32, scope=peer):
            return sb(name, shape, dt, scope)

        hidden = [pb(f"hidden{i}", [P, GROUP, T]) for i in range(AHEAD - 1)]
        route = ExitStack()

        def rb(name, shape, dt=F32):
            return sb(name, shape, dt, route)

        scores = rb("scores", [P, TB, HEADS, 2, N_KEYS])
        q_tile = scaled
        key_scope = ExitStack()
        keys = sb("keys", [P, HEADS, N_KEYS], F32, key_scope)
        sp.after(mixer_over)
        keys_landed = Landing(sem("keys_landed")).mark(nc.sync.dma_start(keys[:], a["keys"]))
        act.after(mixer_over)
        dve.after(mixer_over)
        pool.after(mixer_over)

        q_free = list(scaled_free)
        score_done = []
        for h in range(HEADS):
            b, bank, done = product(stream.next(), h_hi, h_lo, h_ready)
            act.after(done, q_free[h % 2])
            q_done = act.mark(S.activation(q_tile[:, h % 2, :], bank[:], ACT.Copy))
            banks.free[b] = [q_done]
            for c in range(2):
                b, bank, free = banks.take()
                pe.after(free, q_done, keys_landed)
                for tb in range(TB):
                    ins = M.matmul(bank[:, tb * N_KEYS:(tb + 1) * N_KEYS],
                                   q_tile[64 * c:64 * c + 64, h % 2, tb * P:(tb + 1) * P],
                                   keys[64 * c:64 * c + 64, h, :], start=True, stop=True)
                done = pe.mark(ins)
                act.after(done)
                m = act.mark(S.activation(scores[:, :, h, c, :], bank[:].rearrange("p (t n) -> p t n", t=TB), ACT.Copy))
                banks.free[b] = [m]
                score_done.append(m)
            q_free[h % 2] = done
            scaled_free[h % 2] = done
        key_scope.close()
        keys_over = done

        top_s = rb("top_s", [P, HEADS, 2, TOPK])
        top_i = rb("top_i", [P, HEADS, 2, TOPK], U32)
        top_f = rb("top_f", [P, HEADS, 2, TOPK])
        sums = rb("sums", [P, 4, TOPK, TOPK])
        best = rb("best", [P, HEADS, TOPK])
        best_at = rb("best_at", [P, HEADS, TOPK], U32)
        half_at = rb("half_at", [P, 2, HEADS, TOPK], U32)
        half_f = rb("half_f", [P, 2, HEADS, TOPK])
        chosen = rb("chosen", [P, 3, HEADS * TOPK])
        total = rb("total", [P, 2, HEADS])
        equal = sums
        chosen_t = rb("chosen_t", [P, 3, P])
        one_hot = [rb(f"one_hot{i}", [P, 2, 4, P]) for i in range(2)]
        stage = [rb(f"stage{i}", [P, N_GROUPS, GROUP, TOK]) for i in range(2)]
        stage_sem = [Landing(sem(f"stage{i}_stored")) for i in range(2)]
        coefs = nc.dram_tensor("expert_coefs", [N_GROUPS, P, T // TOK, GROUP, TOK], F32, kind="Internal")

        def chain(ins):
            m = dve.mark(ins)
            dve.after(m)
            return m

        chosen_free, chosen_t_free = None, None
        act.after(keys_over)
        dve.after(keys_over)

        def route_tokens(tb):
            dve.after(score_done[-1], score_done[-2])
            for h in range(HEADS):
                for c in range(2):
                    s, v, i = scores[:, tb, h, c, :], top_s[:, h, c, :], top_i[:, h, c, :]
                    chain(V.max(v[:, 0:8], s))
                    chain(V.max_index(i[:, 0:8], v[:, 0:8], s))
                    chain(V.match_replace(s, v[:, 0:8], s, NEG))
                    chain(V.max(v[:, 8:16], s))
                    chain(V.max_index(i[:, 8:16], v[:, 8:16], s))
            chain(V.tensor_copy(top_f[:], top_i[:]))
            for q in range(2):
                hs = slice(4 * q, 4 * q + 4)
                for n in range(4):
                    h = 4 * q + n
                    s = sums[:, n, :, :]
                    chain(V.tensor_tensor(s, top_s[:, h, 0, :].unsqueeze(2).broadcast_to([P, TOPK, TOPK]),
                                          top_s[:, h, 1, :].unsqueeze(1).broadcast_to([P, TOPK, TOPK]), ALU.add))
                    s = s.rearrange("p a b -> p (a b)")
                    chain(V.max(best[:, h, 0:8], s))
                    chain(V.max_index(best_at[:, h, 0:8], best[:, h, 0:8], s))
                    chain(V.match_replace(s, best[:, h, 0:8], s, 2 * NEG))
                    chain(V.max(best[:, h, 8:16], s))
                    chain(V.max_index(best_at[:, h, 8:16], best[:, h, 8:16], s))
            chain(V.tensor_scalar(half_at[:, 0], best_at[:], 4, None, ALU.logical_shift_right))
            chain(V.tensor_scalar(half_at[:, 1], best_at[:], TOPK - 1, None, ALU.bitwise_and))
            chain(V.tensor_copy(half_f[:], half_at[:]))
            dve.after(chosen_free)
            for c in range(2):
                for q in range(2):
                    hs = slice(4 * q, 4 * q + 4)
                    for n in range(4):
                        h = 4 * q + n
                        chain(V.tensor_tensor(equal[:, n], half_f[:, c, h, :].unsqueeze(2).broadcast_to([P, TOPK, TOPK]),
                                              const("iota16").unsqueeze(1).broadcast_to([P, TOPK, TOPK]), ALU.is_equal))
                        chain(V.tensor_tensor(equal[:, n], equal[:, n],
                                              top_f[:, h, c, :].unsqueeze(1).broadcast_to([P, TOPK, TOPK]), ALU.mult))
                    chain(V.tensor_reduce(chosen[:, c, 64 * q:64 * q + 64],
                                          equal[:].rearrange("p h a b -> p (h a) b"), AX_X, ALU.add))
            w = chosen[:, 2, :].rearrange("p (h s) -> p h s", h=HEADS)
            m = chain(V.tensor_tensor(w, best[:], best[:, :, 0:1].broadcast_to([P, HEADS, TOPK]), ALU.subtract))
            act.after(m)
            m = act.mark(S.activation(w, w, ACT.Exp))
            dve.after(m)
            chain(V.tensor_reduce(total[:, 0, :], w, AX_X, ALU.add))
            chain(V.reciprocal(total[:, 1, :], total[:, 0, :]))
            return chain(V.tensor_tensor(w, w, total[:, 1, :].unsqueeze(2).broadcast_to([P, HEADS, TOPK]), ALU.mult))

        stored = []
        stage_free = [None, None]
        hot_free = [None, None]

        def place_tokens(tb, routed):
            nonlocal chosen_free, chosen_t_free
            b, bank, free = banks.take()
            pe.after(free, routed)
            for n in range(3):
                ins = M.transpose(bank[:, n * P:(n + 1) * P], chosen[:, n, :], const("ident"))
            done = pe.mark(ins)
            chosen_free = done
            act.after(done, chosen_t_free)
            turned = act.mark(S.activation(chosen_t[:].rearrange("p n t -> p (n t)"), bank[:, 0:3 * P], ACT.Copy))
            banks.free[b] = [turned]
            for quad in range(P // 4):
                hot, k = one_hot[quad % 2], quad % 2
                t0 = 4 * quad
                iota = const("iota").unsqueeze(1).broadcast_to([P, 4, P])
                dve.after(turned, hot_free[k])
                dve.mark(V.tensor_tensor(hot[:, 0], chosen_t[:, 0, t0:t0 + 4].unsqueeze(2).broadcast_to([P, 4, P]),
                                         iota, ALU.is_equal))
                for t in range(4):
                    m = dve.mark(V.tensor_scalar(hot[:, 1, t, :], const("iota"), chosen_t[:, 1, t0 + t:t0 + t + 1],
                                                 chosen_t[:, 2, t0 + t:t0 + t + 1], ALU.is_equal, ALU.mult))
                b, bank, free = banks.take()
                pe.after(free, m)
                for t in range(4):
                    ins = M.matmul(bank[:, t * P:(t + 1) * P], hot[:, 0, t, :], hot[:, 1, t, :], start=True, stop=True)
                done = pe.mark(ins)
                hot_free[k] = done
                at = (t0 % TOK)
                s = ((tb * P + t0) // TOK)
                st = stage[s % 2]
                act.after(done, stage_free[s % 2] if at == 0 else None)
                e_done = act.mark(S.activation(st[:, :, :, at:at + 4].rearrange("p g j t -> p (g j) t"),
                                               bank[:].rearrange("p (t n) -> p n t", t=4), ACT.Copy))
                banks.free[b] = [e_done]
                if at == TOK - 4:
                    sp.after(e_done)
                    stage_free[s % 2] = stage_sem[s % 2].mark(nc.sync.dma_start(
                        coefs[:, :, s, :, :].rearrange("g p j t -> p g (j t)"),
                        st[:].rearrange("p g j t -> p g (j t)")))
            chosen_t_free = m

        hidden_done = {}
        hidden_free = [None] * AHEAD

        def hidden_block(j):
            g, n = divmod(j, GROUP)
            b, bank, done = product(stream.next(), h_hi, h_lo, h_ready)
            act.after(done, hidden_free[g % AHEAD])
            m = act.mark(S.activation(hidden[g % AHEAD][:, n, :], bank[:], ACT.Gelu))
            banks.free[b] = [m]
            hidden_done[j] = m

        routed = route_tokens(0)
        step = (AHEAD - 1) * GROUP // TB
        for tb in range(TB):
            for j in range(step * tb, step * tb + step):
                hidden_block(j)
            place_tokens(tb, routed)
            if tb + 1 < TB:
                routed = route_tokens(tb + 1)
        route_over = [(act.sem, act.count), (dve.sem, dve.count), (pool.sem, pool.count), (pe.sem, pe.count)] + stage_free
        route.close()
        stream.on_pool = False

        act.after(route_over)
        dve.after(route_over)
        hidden.append(pb("hidden_last", [P, GROUP, T]))
        for n in range(GROUP):
            hidden_block((AHEAD - 1) * GROUP + n)

        weight = [pb(f"weight{i}", [P, T // TOK, GROUP, TOK]) for i in range(2)]
        weight_landing = [Landing(sem(f"weight{i}_landed")) for i in range(2)]
        mixed_hi = pb("mixed_hi", [P, GROUP, T], F32R)
        mixed_lo = pb("mixed_lo", [P, GROUP, T], F32R)
        weight_landed, weight_used = {}, {}

        def load_weight(g):
            if g < N_GROUPS:
                sp.after(route_over, weight_used.get(g - 2))
                weight_landed[g] = weight_landing[g % 2].mark(nc.sync.dma_start(
                    weight[g % 2][:].rearrange("p s j t -> p (s j t)"), coefs[g].rearrange("p s j t -> p (s j t)")))

        load_weight(0)
        load_weight(1)
        mixed_free = None
        for g in range(N_GROUPS):
            mixed_ready = []
            for n in range(GROUP):
                v = hidden[g % AHEAD][:, n, :]
                dve.after(hidden_done[g * GROUP + n], weight_landed[g])
                m = dve.mark(V.tensor_tensor(v.rearrange("p (s t) -> p s t", t=TOK), v.rearrange("p (s t) -> p s t", t=TOK),
                                             weight[g % 2][:, :, n, :], ALU.mult))
                mixed_ready.append(split_to(mixed_hi[:, n, :], mixed_lo[:, n, :], v, m, mixed_free))
            weight_used[g] = m
            hidden_free[g % AHEAD] = mixed_ready[-1]
            load_weight(g + 2)
            for k in range(KD):
                b, bank, done = product(stream.next(), mixed_hi, mixed_lo, mixed_ready, nk=GROUP)
                dve.after(g2_done)
                x_done[k] = add_to_x(k, b, bank, done, ada[:, 40 + k:41 + k])
            mixed_free = done
            if g + AHEAD < N_GROUPS:
                for n in range(GROUP):
                    hidden_block((g + AHEAD) * GROUP + n)
        peer.close()
        peer_over = [(act.sem, act.count), (dve.sem, dve.count), (pe.sem, pe.count)]
        h_free = (pe.sem, pe.count)

        x_rstd = norm_of_x(x_done)
        for k in range(KD):
            dve.after(x_rstd)
            x_done[k] = dve.mark(V.scalar_tensor_tensor(x[:, k, :], x[:, k, :], col("final", k), rstd[:], ALU.mult, ALU.mult))
            rstd_free[:] = [x_done[k]]
        x_rstd = norm_of_x(x_done)
        h_ready = [normalise(k, x[:, k, :], col("norm_mix", k), None, h_hi[:, k, :], h_lo[:, k, :], x_rstd, h_free)
                   for k in range(KD)]
        att = ExitStack()

        def ab(name, shape, dt=F32):
            return sb(name, shape, dt, att)

        act.after(peer_over)
        dve.after(peer_over)
        pool.after(peer_over)
        sp.after(peer_over)
        q_a = ab("q_a", [P, 4, T])
        k_a = ab("k_a", [P, 4, T])
        v_a = ab("v_a", [P, TB, 512])
        v_b = ab("v_b", [P, TB, 512])
        q_b = ab("q_b", [P, 4, T])
        k_b = ab("k_b", [P, 4, T])
        q_rot = ab("q_rot", [P, 2, T])
        k_rot = ab("k_rot", [P, T])
        key_bias = ab("key_bias", [HEADS, T])
        gates = ab("gates", [P, 16, T])
        latent = gates[:, 13:16, :]
        forget = gates[0:HEADS, 8:13, :]
        turns = gates[:, 7, :]
        position = gates[:, 6, :].bitcast(I32)
        table = gates[:, 5, :]
        early = ExitStack()
        latent_hi = sb("latent_hi", [P, 3, T], F32R, early)
        latent_lo = sb("latent_lo", [P, 3, T], F32R, early)
        rotated = sb("rotated", [P, 2, T], F32, early)

        position_landed = Landing(sem("position_landed")).mark(nc.sync.dma_start(position, a["positions"]))
        dve.after(position_landed)
        chain(V.tensor_copy(table, position))
        chain(V.tensor_scalar(table[:], table[:], col("inv_freq"), None, ALU.mult))
        ROUND = 1.5 * 2.0 ** 23
        for scale, parts in ((256.0, two_pi_parts(256.0, 10, 5)), (1.0, two_pi_parts(1.0, 14, 2))):
            chain(V.tensor_scalar(turns, table, 1.0 / (2 * math.pi * scale), ROUND, ALU.mult, ALU.add))
            chain(V.tensor_scalar(turns, turns, -ROUND, None, ALU.add))
            for part in parts:
                chain(V.scalar_tensor_tensor(table, turns, -part, table, ALU.mult, ALU.add))
        chain(V.tensor_scalar(table, table, col("phase"), None, ALU.add))
        chain(V.tensor_scalar(turns, table, math.pi, -2 * math.pi, ALU.is_gt, ALU.mult))
        chain(V.tensor_tensor(table, table, turns, ALU.add))
        m = chain(V.tensor_scalar(table, table, 3.1415925, -3.1415925, ALU.min, ALU.max))
        act.after(m)
        m = act.mark(S.activation(table, table, ACT.Sin))
        dve.after(m)
        table_done = chain(V.tensor_scalar(table, table, col("sign"), None, ALU.mult))

        def rotate(dsts, bank, ready):
            dve.after(ready, table_done, (dve.sem, dve.count))
            m1 = dve.mark(V.tensor_tensor(rotated[64:96, 0, :], bank[64:96, :], table[64:96, :], ALU.mult))
            dve.after(m1)
            m = dve.mark(V.tensor_tensor(rotated[64:96, 1, :], bank[96:128, :], table[96:128, :], ALU.mult))
            dve.after(m)
            for dst in dsts:
                m2 = dve.mark(V.tensor_tensor(dst, rotated[64:96, 0, :], rotated[64:96, 1, :], ALU.add))
            return m, m2

        b, bank, done = product(stream.next(), h_hi, h_lo, h_ready)
        dve.after(done)
        m = chain(V.tensor_scalar(forget[:, 0, :], bank[0:8, :], columns[0:8, COLUMN_AT["b_forget"]:COLUMN_AT["b_forget"] + 1],
                                  None, ALU.add))
        m_rot, k_rot_done = rotate([k_rot[32 * n:32 * n + 32, :] for n in range(4)], bank, done)
        banks.free[b] = [m_rot, m]
        chain(V.tensor_scalar(forget[:, 1, :], forget[:, 0, :], -1.0, None, ALU.mult))
        m = chain(V.tensor_tensor(forget[:, 1, :], forget[:, 1, :], forget[:, 0, :], ALU.min))
        act.after(m)
        m = act.mark(S.activation(forget[:, 1, :], forget[:, 1, :], ACT.Exp))
        m = log1p_of(forget[:, 2, :], forget[:, 1, :], forget[:, 3, :], forget[:, 4, :], HEADS, m)
        dve.after(m)
        chain(V.scalar_tensor_tensor(forget[:, 1, :], forget[:, 0, :], 0.0, forget[:, 2, :], ALU.min, ALU.subtract))
        chain(V.memset(forget[:, 2, :], 1.0))
        chain(V.tensor_tensor_scan(forget[:, 3, :], forget[:, 2, :], forget[:, 1, :], 0.0, ALU.mult, ALU.add))
        bias_done = chain(V.tensor_scalar(key_bias[:], forget[:, 3, :], -1.0 / ATT_SCALE_A, None, ALU.mult))

        lat = []
        for n in range(3):
            b, bank, done = product(stream.next(), h_hi, h_lo, h_ready)
            act.after(done)
            lat.append(act.mark(S.activation(latent[:, n, :], bank[:], ACT.Copy)))
            banks.free[b] = [lat[-1]]
        add_square(0, 2, squared(latent[:, 0, :], 0, lat[0]))
        summed = add_square(1, 2, squared(latent[:, 1, :], 1, lat[1]))
        rs = inverse_rms(2 * P, summed)
        lat_ready = [normalise(n, latent[:, n, :], col("q_norm", n), None, latent_hi[:, n, :], latent_lo[:, n, :], rs, None)
                     for n in range(2)]
        summed = add_square(0, 1, squared(latent[:, 2, :], 0, lat[2]))
        rs = inverse_rms(P, summed)
        lat_ready.append(normalise(0, latent[:, 2, :], col("kv_norm"), None, latent_hi[:, 2, :], latent_lo[:, 2, :], rs, None))

        qk_done = []
        for n in range(8):
            b, bank, done = product(stream.next(), h_hi, h_lo, h_ready)
            act.after(done)
            qk_done.append(act.mark(S.activation((q_a if n < 4 else k_a)[:, n % 4, :], bank[:], ACT.Copy)))
            banks.free[b] = [qk_done[-1]]
        taken = [banks.take() for _ in range(TB)]
        for n in range(4):
            block = stream.next()
            pe.after(block[3])
            for kk in range(2):
                k = 2 * n + kk
                for tb, (b, bank, free) in enumerate(taken):
                    pe.after(free if k == 0 else None)
                    w = slice(kk * 512, kk * 512 + 512)
                    t = slice(tb * P, tb * P + P)
                    ins = three(bank[:], h_hi[:, k, t], h_lo[:, k, t], block[1][:, w], block[2][:, w], k == 0, k == KD - 1)
            stream.used[block[0]] = pe.mark(ins)
        va_done = []
        for tb, (b, bank, free) in enumerate(taken):
            act.after(stream.used[block[0]])
            va_done.append(act.mark(S.activation(v_a[:, tb, :], bank[:], ACT.Copy)))
            banks.free[b] = [va_done[-1]]
        qb_done = []
        for h in range(HEADS):
            if h % 4 == 0:
                n, hi, lo, ready = stream.next()
            b, bank, free = banks.take()
            pe.after(free, ready)
            for k in range(2):
                pe.after(lat_ready[k])
                c = k * 512 + (h % 4) * P
                ins = three(bank[:], hi[:, c:c + P], lo[:, c:c + P], latent_hi[:, k, :], latent_lo[:, k, :], k == 0, k == 1)
            done = pe.mark(ins)
            if h % 4 == 3:
                stream.used[n] = done
            m_rot, rot_done = rotate([q_rot[32 * (h % 4):32 * (h % 4) + 32, h // 4, :]], bank, done)
            act.after(done, m_rot)
            m = act.mark(S.activation(q_b[64 * (h % 2):64 * (h % 2) + 64, h // 2, :], bank[0:64, :], ACT.Copy))
            banks.free[b] = [m_rot, m]
            qb_done.append([m, rot_done])
        block = stream.next()
        kb_done = []
        for h in range(0, HEADS, 2):
            b, bank, free = banks.take()
            pe.after(free, block[3], lat_ready[2])
            c = h * 64
            done = pe.mark(three(bank[:], block[1][:, c:c + P], block[2][:, c:c + P], latent_hi[:, 2, :], latent_lo[:, 2, :],
                                 True, True))
            act.after(done)
            kb_done.append(act.mark(S.activation(k_b[:, h // 2, :], bank[:], ACT.Copy)))
            banks.free[b] = [kb_done[-1]]
        vb_done = []
        for tb in range(TB):
            b, bank, free = banks.take()
            pe.after(free)
            t = slice(tb * P, tb * P + P)
            done = pe.mark(three(bank[:], latent_hi[:, 2, t], latent_lo[:, 2, t], block[1][:, 512:], block[2][:, 512:], True, True))
            act.after(done)
            vb_done.append(act.mark(S.activation(v_b[:, tb, :], bank[:], ACT.Copy)))
            banks.free[b] = [vb_done[-1]]
        stream.used[block[0]] = done

        gate_done = []

        def gate_block():
            n = len(gate_done)
            b, bank, done = product(stream.next(), h_hi, h_lo, h_ready)
            act.after(done)
            gate_done.append(act.mark(S.activation(gates[:, n, :], bank[:], ACT.Sigmoid, bias=col("b_gate", n))))
            banks.free[b] = [gate_done[-1]]

        for _ in range(16):
            gate_block()
        early_over = [(pe.sem, pe.count), (dve.sem, dve.count), (act.sem, act.count)]
        early.close()
        act.after(early_over)
        dve.after(early_over)
        prob = [square[:, 0, :], square[:, 1, :], scaled[:, 0, :]]
        prob_t = [ab(f"prob_t{i}", [P, TB, T]) for i in range(2)]
        stats = ab("att_stats", [P, 64, 4])
        att_hi, att_lo = h_hi, h_lo
        units = [(kind, h, i) for kind in (0, 1) for h in range(HEADS) for i in range(TB)]
        state = {}
        prob_free, prob_t_free = [None] * 3, [None] * 2
        att_ready = [None] * 8

        def score(u):
            kind, h, i = units[u]
            n = (i + 1) * P
            b, bank, free = banks.take()
            pe.after(free)
            q = slice(i * P, i * P + P)
            if kind == 0:
                r = slice(64 * (h % 2), 64 * (h % 2) + 64)
                pe.after(qk_done[h // 2], qk_done[4 + h // 2], bias_done)
                M.matmul(bank[:, 0:n], q_a[r, h // 2, q], k_a[r, h // 2, 0:n], start=True, stop=False)
                pick_head = const("ident")[0:HEADS, h:h + 1].broadcast_to([HEADS, P])
                M.matmul(bank[:, 0:n], pick_head, key_bias[:, 0:n], start=False, stop=False)
            else:
                pe.after(qb_done[h], kb_done[h // 2], k_rot_done)
                r = slice(64 * (h % 2), 64 * (h % 2) + 64)
                M.matmul(bank[:, 0:n], q_b[r, h // 2, q], k_b[r, h // 2, 0:n], start=True, stop=False)
                r = slice(32 * (h % 4), 32 * (h % 4) + 32)
                M.matmul(bank[:, 0:n], q_rot[r, h // 4, q], k_rot[r, 0:n], start=False, stop=False)
            mask = const("causal" if kind == 0 else "chunk")
            state[u] = {"scored": pe.mark(M.matmul(bank[:, n - P:n], const("ident"), mask, start=False, stop=True)),
                        "bank": bank, "b": b, "n": n}

        def row_max(u):
            s = state[u]
            scale = ATT_SCALE_A if units[u][0] == 0 else ATT_SCALE_B
            dve.after(s["scored"])
            m = dve.mark(V.tensor_reduce(stats[:, u, 0:1], s["bank"][:, 0:s["n"]], AX_X, ALU.max))
            dve.after(m)
            s["max"] = dve.mark(V.tensor_scalar(stats[:, u, 1:2], stats[:, u, 0:1], -scale, None, ALU.mult))

        def exponent(u):
            s = state[u]
            scale = ATT_SCALE_A if units[u][0] == 0 else ATT_SCALE_B
            act.after(s["max"], prob_free[u % 3])
            s["exp"] = act.mark(S.activation(prob[u % 3][:, 0:s["n"]], s["bank"][:, 0:s["n"]], ACT.Exp,
                                             bias=stats[:, u, 1:2], scale=scale, accum_out=stats[:, u, 2:3]))
            banks.free[s["b"]] = [s["exp"]]

        def divide(u):
            s = state[u]
            dve.after(s["exp"])
            m = dve.mark(V.reciprocal(stats[:, u, 3:4], stats[:, u, 2:3]))
            dve.after(m)
            p = prob[u % 3][:, 0:s["n"]]
            s["prob"] = dve.mark(V.tensor_scalar(p, p, stats[:, u, 3:4], None, ALU.mult))

        def turn(u):
            kind, h, i = units[u]
            s = state[u]
            b, bank, free = banks.take()
            pe.after(free, s["prob"])
            for kb in range(i + 1):
                ins = M.transpose(bank[:, kb * P:(kb + 1) * P], prob[u % 3][:, kb * P:(kb + 1) * P], const("ident"))
            s["turned"] = pe.mark(ins)
            prob_free[u % 3] = s["turned"]
            head_no = u // TB
            q, e = (act, S) if u % 2 else (dve, V)
            q.after(s["turned"], prob_t_free[head_no % 2])
            dst = prob_t[head_no % 2][:, 0:i + 1, i * P:(i + 1) * P]
            src = bank[:, 0:(i + 1) * P].rearrange("p (k q) -> p k q", q=P)
            s["kept"] = q.mark(e.activation(dst, src, ACT.Copy) if u % 2 else e.tensor_copy(dst, src))
            banks.free[b] = [s["kept"]]

        def values(head_no):
            kind, h = divmod(head_no, HEADS)
            b, bank, free = banks.take()
            pe.after(free, *[state[head_no * TB + i]["kept"] for i in range(TB)])
            pe.after(va_done if kind == 0 else vb_done)
            v = v_a if kind == 0 else v_b
            pair = slice((h // 2) * P, (h // 2) * P + P)
            for kb in range(TB):
                ins = M.matmul(bank[:, kb * P:T], v[:, kb, pair], prob_t[head_no % 2][:, kb, kb * P:T],
                               start=kb == 0, stop=kb == TB - 1)
            done = pe.mark(ins)
            prob_t_free[head_no % 2] = done
            r = slice(64 * (h % 2), 64 * (h % 2) + 64)
            tile = 4 * kind + h // 2
            act.after(done)
            hi_done = act.mark(S.activation(att_hi[r, tile, :], bank[r, :], ACT.Copy))
            dve.after(hi_done)
            lo_done = dve.mark(V.tensor_tensor(att_lo[r, tile, :], bank[r, :], att_hi[r, tile, :].bitcast(F32), ALU.subtract))
            banks.free[b] = [lo_done]
            att_ready[tile] = (att_ready[tile] or []) + [hi_done, lo_done]

        n_units = len(units)
        for s in range(n_units + 5):
            if s < n_units:
                score(s)
                row_max(s)
                exponent(s)
            if 0 <= s - 1 < n_units:
                divide(s - 1)
            if 0 <= s - 2 < n_units:
                turn(s - 2)
            if s >= 4 and (s - 3) % TB == 0 and (s - 3) // TB <= 2 * HEADS:
                values((s - 3) // TB - 1)
            if s == n_units + 3:
                break

        merged = gates
        for m2 in range(4):
            block = stream.next()
            for n in range(2):
                k = 2 * m2 + n
                b, bank, done = product(block, att_hi[:, 0:4], att_lo[:, 0:4], att_ready[0:4], nk=4, at=n * 512, last_use=n == 1)
                dve.after(done, gate_done[k])
                x_m = dve.mark(V.tensor_tensor(merged[:, k, :], bank[:], gates[:, k, :], ALU.mult))
                banks.free[b] = [x_m]
        pending = []
        for m2 in range(4):
            block = stream.next()
            for n in range(2):
                k = 2 * m2 + n
                b, bank, done = product(block, att_hi[:, 4:8], att_lo[:, 4:8], att_ready[4:8], nk=4, at=n * 512, last_use=n == 1)
                dve.after(done, gate_done[8 + k])
                m = dve.mark(V.tensor_tensor(gates[:, 8 + k, :], bank[:], gates[:, 8 + k, :], ALU.mult))
                banks.free[b] = [m]
                dve.after(m, x_m)
                pending.append(dve.mark(V.tensor_tensor(merged[:, k, :], merged[:, k, :], gates[:, 8 + k, :], ALU.add)))
        h_free = done
        for k in range(KD):
            h_ready[k] = split_to(h_hi[:, k, :], h_lo[:, k, :], merged[:, k, :], pending[k], h_free)

        def residual(n_blocks, m_hi, m_lo, m_ready, gate=None):
            for k in range(KD):
                b, bank, free = banks.take()
                pe.after(free)
                kk = 0
                for n in range(n_blocks):
                    no, hi, lo, ready = stream.next()
                    pe.after(ready)
                    tiles = stream.plan[no].shape[1] // P
                    for c in range(0, tiles * P, P):
                        pe.after(m_ready[kk])
                        ins = three(bank[:], hi[:, c:c + P], lo[:, c:c + P], m_hi[:, kk, :], m_lo[:, kk, :], kk == 0,
                                    kk == len(m_ready) - 1)
                        kk += 1
                    done = pe.mark(ins)
                    stream.used[no] = done
                x_done[k] = add_to_x(k, b, bank, done, gate)
                sq[k] = squared(x[:, k, :], k, x_done[k])
                if k:
                    add_square(k - 1, KD, sq[k - 1])
            return inverse_rms(D, add_square(KD - 1, KD, sq[KD - 1])), done

        x_rstd, h_free = residual(1, h_hi, h_lo, h_ready)
        att.close()
        att_over = [(act.sem, act.count), (dve.sem, dve.count), (pe.sem, pe.count)]

        h_ready = [normalise(k, x[:, k, :], col("norm_ffn", k), None, h_hi[:, k, :], h_lo[:, k, :], x_rstd, h_free)
                   for k in range(KD)]
        ffn = ExitStack()
        f_hi = sb("ffn_hi", [P, FFN_TILES, T], F32R, ffn)
        f_lo = sb("ffn_lo", [P, FFN_TILES, T], F32R, ffn)
        silu = sb("silu", [P, 2, T], F32, ffn)
        act.after(att_over)
        dve.after(att_over)
        f_ready, silu_free = [], [None, None]
        for f in range(FFN_TILES):
            b, bank, done = product(stream.next(), h_hi, h_lo, h_ready)
            act.after(done, silu_free[f % 2])
            s_done = act.mark(S.activation(silu[:, f % 2, :], bank[:], ACT.Silu))
            banks.free[b] = [s_done]
            b, bank, done = product(stream.next(), h_hi, h_lo, h_ready)
            dve.after(done, s_done)
            m = dve.mark(V.tensor_tensor(silu[:, f % 2, :], bank[:], silu[:, f % 2, :], ALU.mult))
            banks.free[b] = [m]
            f_ready.append(split_to(f_hi[:, f, :], f_lo[:, f, :], silu[:, f % 2, :], m))
            silu_free[f % 2] = f_ready[-1]
        x_rstd, _ = residual(3, f_hi, f_lo, f_ready)
        ffn.close()

        stored = Landing(sem("out_stored"))
        for k in range(KD):
            dve.after(x_rstd)
            m = dve.mark(V.scalar_tensor_tensor(x[:, k, :], x[:, k, :], col("norm_final", k), rstd[:], ALU.mult, ALU.mult))
            sp.after(m)
            end = stored.mark(nc.sync.dma_start(out_cols[:, k, :], x[:, k, :]))
        sp.after(end)
        assert len(stream.used) == len(plan)


def in_tiles(w):
    k, n = w.shape
    return w.reshape(k // P, P, n // P, P).transpose(2, 1, 0, 3).reshape(n // P, P, k)


def per_column(v):
    return np.asarray(v).reshape(-1, P).T


def constant_matrices():
    r = np.arange(P)
    m = {
        "ones": np.ones((P, P)),
        "head_ones": (r[:, None] // HEAD_DIM == r[None, :] // HEAD_DIM),
        "ident": np.eye(P),
        "iota": np.broadcast_to(r[None, :], (P, P)),
        "causal": np.where(r[None, :] <= r[:, None], 0.0, NEG),
        "chunk": np.where(r[None, :] // 64 <= r[:, None] // 64, 0.0, NEG),
        "iota16": np.broadcast_to(np.arange(16)[None, :], (P, 16)),
    }
    return np.concatenate([m[n].astype(np.float32) for n, _ in CONSTS], axis=1)


def lay_out(i):
    f32 = np.float32
    half = ROPE // 2
    row = np.arange(P)
    inv = (10000.0 ** (-np.arange(half, dtype=np.float64) / half)).astype(f32)
    is_cos = (row >= 64) & (row < 96)
    first = (row % 32) < half
    forget_col = np.zeros((P, 1), f32)
    forget_col[0:HEADS, 0] = i["b_forget_2"][0]
    parts = {
        "b_ada": per_column(i["b_ada"][0]), "norm1": per_column(i["norm1_g"][0]),
        "conv_a": per_column(i["conv_a_w"][0]), "conv_b": per_column(i["conv_b_w"][0]),
        "conv_bias": per_column(i["conv_b_b"][0]), "b_r": per_column(i["b_r"][0]), "b_i": per_column(i["b_i"][0]),
        "lam": per_column(i["lru_lambda"][0]),
        "gn": np.concatenate([per_column(i["gn_a"][0]), per_column(i["gn_b"][0])], axis=1),
        "norm2": per_column(i["norm2_g"][0]), "final": per_column(i["final_g"]),
        "norm_mix": per_column(i["norm_mix_g_2"][0]), "q_norm": per_column(i["q_a_norm_g_2"][0]),
        "kv_norm": per_column(i["kv_a_norm_g_2"][0]), "b_gate": per_column(i["b_gate_2"][0]),
        "norm_ffn": per_column(i["norm_ffn_g_2"][0]), "norm_final": per_column(i["norm_final_g_2"]),
        "b_forget": forget_col, "inv_freq": inv[row % half][:, None],
        "phase": np.where(is_cos, math.pi / 2, 0.0).astype(f32)[:, None],
        "sign": np.where(~is_cos & first, -1.0, 1.0).astype(f32)[:, None],
        "eps": np.full((P, 1), EPS, f32),
    }
    out = {"columns": np.concatenate([parts[n] for n, _ in COLUMNS], axis=1), "consts": constant_matrices()}
    out["x"] = i["x"][0].T.reshape(KD, P, T).transpose(1, 0, 2)
    out["c_rows"] = np.broadcast_to(i["c"][0], (P, D))
    out["w_ada"] = i["w_ada"][0].T.reshape(48, P, D)
    out["w_in"] = in_tiles(i["w_in"][0])
    out["w_out"] = in_tiles(i["w_out"][0])
    out["w_q"] = in_tiles(i["w_q"][0])
    gates = np.zeros((P, 2, 4, P), f32)
    for g, name in enumerate(("w_r", "w_i")):
        for h in range(HEADS):
            r = slice(64 * (h % 2), 64 * (h % 2) + 64)
            gates[r, g, h // 2, r] = i[name][0, h]
    out["w_lru_gates"] = gates
    out["keys"] = i["sub_keys"][0].transpose(1, 3, 0, 2).reshape(P, HEADS, N_KEYS)
    out["expert_u"] = i["expert_u"][0].reshape(N_KEYS, N_KEYS, KD, P).transpose(1, 3, 2, 0).reshape(N_KEYS, P, BLOCK)
    out["expert_v"] = i["expert_v"][0].reshape(N_KEYS, N_GROUPS, GROUP, KD, P).transpose(1, 3, 0, 2, 4).reshape(
        N_GROUPS * KD, P, BLOCK)
    w = i["w_in_2"][0]
    qa, ka, va, fa, cq, ckv, kr, ga, gb = np.split(w, np.cumsum([512, 512, 512, 8, 256, 128, 32, 1024]), axis=1)
    small = np.concatenate([fa, np.zeros((D, 56), f32), kr, kr[:, half:], kr[:, :half]], axis=1)
    out["w_small2"] = in_tiles(small)
    out["w_latent2"] = in_tiles(np.concatenate([cq, ckv], axis=1))
    out["w_qk2"] = in_tiles(np.concatenate([qa, ka], axis=1))
    out["w_v2"] = va.reshape(4, 2, P, 512).transpose(0, 2, 1, 3).reshape(4, P, BLOCK)
    out["w_gates2"] = in_tiles(np.concatenate([ga, gb], axis=1))
    qu = i["w_q_up_2"][0].reshape(2 * P, HEADS, NOPE + ROPE)
    qu = np.concatenate([qu, qu[:, :, NOPE + half:], qu[:, :, NOPE:NOPE + half]], axis=2)
    out["w_q_up"] = qu.reshape(2, P, 2, 4, P).transpose(2, 1, 0, 3, 4).reshape(2, P, BLOCK)
    kv = i["w_kv_up_2"][0].reshape(P, HEADS, 2, 64).transpose(0, 2, 1, 3)
    out["w_kv_up"] = kv.reshape(1, P, BLOCK)
    for name, w in (("w_branch_a", i["w_branch_a_2"][0]), ("w_branch_b", i["w_branch_b_2"][0])):
        out[name] = w.reshape(4, P, 4, 2, P).transpose(2, 1, 3, 0, 4).reshape(4, P, BLOCK)
    out["w_out2"] = in_tiles(i["w_out_2"][0])
    out["w_ffn_gate"] = in_tiles(i["w_ffn_gate_2"][0])
    out["w_ffn_up"] = in_tiles(i["w_ffn_up_2"][0])
    out["w_ffn_down"] = in_tiles(i["w_ffn_down_2"][0])
    out["positions"] = np.broadcast_to(i["positions_2"][0], (P, T))
    return {k: np.ascontiguousarray(v) for k, v in out.items()}


def kernel(**inputs):
    import concourse.bacc as bacc
    from concourse.bass_utils import run_bass_kernel_spmd

    arrays = lay_out({k: np.asarray(v) for k, v in inputs.items()})
    nc = bacc.Bacc("TRN2", target_bir_lowering=False, num_devices=1)
    aps = {k: nc.dram_tensor(f"in_{k}", v.shape, mybir.dt.from_np(v.dtype), kind="ExternalInput").ap()
           for k, v in arrays.items()}
    out = nc.dram_tensor("out_cols", (P, KD, T), F32, kind="ExternalOutput").ap()
    build(nc, aps, out)
    r = run_bass_kernel_spmd(nc, [{f"in_{k}": v for k, v in arrays.items()}], core_ids=[0])
    got = np.asarray(r.results[0]["out_cols"])
    return np.ascontiguousarray(got.transpose(1, 0, 2).reshape(1, D, T).transpose(0, 2, 1))
```

```python
import math
from contextlib import ExitStack

import numpy as np
import concourse.bass as bass
from concourse import mybir

F32 = mybir.dt.float32
F32R = mybir.dt.float32r
I32 = mybir.dt.int32
U32 = mybir.dt.uint32
ALU = mybir.AluOpType
ACT = mybir.ActivationFunctionType
AX_X = mybir.AxisListType.X

P = 128
T = 512
D = 1024
KD = D // P
TB = T // P
EPS = 1e-6
NEG = -1e30
BLOCK = KD * P

CONV_TILES = 4
HEADS = 8
HEAD_DIM = 64
LRU_C = 8.0
TOPK = 16
N_KEYS = 128
GROUP = 8
N_GROUPS = N_KEYS // GROUP
AHEAD = 8
KEPT = AHEAD - 1
N_HOT = 4
FIRST_U = 14
ROUTE_PIECES = 17
TOK = 16
ROPE = 32
NOPE = 64
FFN_TILES = 22
ATT_SCALE_A = HEAD_DIM ** -0.5
ATT_SCALE_B = (NOPE + ROPE) ** -0.5

COLUMNS = [("b_ada", 48), ("norm1", 8), ("conv_a", 12), ("conv_b", 16), ("conv_bias", 4), ("b_r", 4),
           ("b_i", 4), ("lam", 4), ("gn", 8), ("norm2", 8), ("final", 8), ("norm_mix", 8), ("q_norm", 2),
           ("kv_norm", 1), ("b_gate", 16), ("norm_ffn", 8), ("norm_final", 8), ("b_forget", 1),
           ("inv_freq", 1), ("phase", 1), ("sign", 1), ("eps", 1)]
COLUMN_AT = {}
_at = 0
for _name, _n in COLUMNS:
    COLUMN_AT[_name] = _at
    _at += _n
N_COLUMNS = _at
CONSTS = [("ones", 128), ("head_ones", 128), ("ident", 128), ("iota", 128), ("causal", 128), ("chunk", 128),
          ("iota16", 16)]
CONST_AT = {}
_at = 0
for _name, _n in CONSTS:
    CONST_AT[_name] = (_at, _at + _n)
    _at += _n
N_CONSTS = _at


def two_pi_parts(scale, bits, n):
    rest, parts = 2 * math.pi * scale, []
    for _ in range(n):
        unit = 2.0 ** (math.floor(math.log2(rest)) + 1 - bits)
        part = math.floor(rest / unit) * unit
        parts.append(part)
        rest -= part
    return parts + [rest]


class Queue:

    def __init__(self, engine, sem):
        self.engine, self.sem, self.count, self.seen = engine, sem, 0, {}

    def after(self, *moments):
        for m in moments:
            if m is None:
                continue
            if isinstance(m, list):
                self.after(*m)
                continue
            sem, value = m
            if self.seen.get(sem.name, 0) < value:
                self.engine.wait_ge(sem, value)
                self.seen[sem.name] = value

    def mark(self, instruction):
        self.count += 1
        instruction.then_inc(self.sem, 1)
        return (self.sem, self.count)


class Landing:

    def __init__(self, sem):
        self.sem, self.count = sem, 0

    def mark(self, dma):
        self.count += 16
        dma.then_inc(self.sem, 16)
        return (self.sem, self.count)


class Banks:

    def __init__(self, tensors):
        self.tensors, self.free, self.at = tensors, [[] for _ in tensors], -1

    def take(self):
        self.at = (self.at + 1) % len(self.tensors)
        return self.at, self.tensors[self.at], self.free[self.at]


class WeightStream:

    RAW, SPLIT = 3, 3

    def __init__(self, nc, ctx, sp, act, dve, pool, plan):
        self.nc, self.sp, self.act, self.dve, self.pool, self.plan = nc, sp, act, dve, pool, plan
        self.raw = [ctx.enter_context(nc.sbuf_tensor(f"weights_raw{i}", [P, BLOCK], F32)) for i in range(self.RAW)]
        self.hi = [ctx.enter_context(nc.sbuf_tensor(f"weights_hi{i}", [P, BLOCK], F32R)) for i in range(self.SPLIT)]
        self.lo = [ctx.enter_context(nc.sbuf_tensor(f"weights_lo{i}", [P, BLOCK], F32R)) for i in range(self.SPLIT)]
        self.landing = [Landing(ctx.enter_context(nc.semaphore(f"weights_raw{i}"))) for i in range(self.RAW)]
        self.loaded, self.hi_done, self.lo_done, self.used = [], [], [], []
        self.on_pool = False

    def start(self):
        for _ in range(self.RAW):
            self.load()

    def load(self):
        n = len(self.loaded)
        if n < len(self.plan):
            if n >= self.RAW:
                self.sp.after(self.hi_done[n - self.RAW], self.lo_done[n - self.RAW])
            src, slot = self.plan[n], n % self.RAW
            self.loaded.append(self.landing[slot].mark(
                self.nc.sync.dma_start(self.raw[slot][:, 0:src.shape[1]], src)))

    def parts(self, n):
        w = self.plan[n].shape[1]
        free = self.used[n - self.SPLIT] if n >= self.SPLIT else None
        assert n < self.SPLIT or free
        return self.raw[n % self.RAW][:, 0:w], self.hi[n % self.SPLIT][:, 0:w], self.lo[n % self.SPLIT][:, 0:w], free

    def split_hi(self):
        n = len(self.hi_done)
        if n < len(self.plan):
            raw, hi, _, free = self.parts(n)
            self.act.after(self.loaded[n], free)
            self.hi_done.append(self.act.mark(self.nc.scalar.activation(hi, raw, ACT.Copy)))

    def split_lo(self):
        n = len(self.lo_done)
        if n < len(self.plan):
            raw, hi, lo, free = self.parts(n)
            q, e = (self.pool, self.nc.gpsimd) if self.on_pool else (self.dve, self.nc.vector)
            q.after(self.hi_done[n], self.loaded[n], free)
            self.lo_done.append(q.mark(e.tensor_tensor(lo, raw, hi.bitcast(F32), ALU.subtract)))
            self.load()

    def next(self):
        n = len(self.used)
        while len(self.hi_done) < min(n + 3, len(self.plan)):
            self.split_hi()
        while len(self.lo_done) < min(n + 2, len(self.plan)):
            self.split_lo()
        self.used.append(None)
        return n, self.hi[n % self.SPLIT], self.lo[n % self.SPLIT], self.hi_done[n], self.lo_done[n]


def build(nc, a, out_cols):
    with ExitStack() as ctx:
        def sb(name, shape, dt=F32, scope=ctx):
            return scope.enter_context(nc.sbuf_tensor(name, shape, dt))

        def sem(name):
            return ctx.enter_context(nc.semaphore(name))

        V, S, G, M = nc.vector, nc.scalar, nc.gpsimd, nc.tensor
        pe, act, dve, pool, sp = (Queue(e, sem(f"{n}_marks")) for n, e in
                                  (("pe", M), ("act", S), ("dve", V), ("pool", G), ("sp", nc.sync)))
        banks = Banks([ctx.enter_context(nc.psum_tensor(f"bank{i}", [P, T], F32)) for i in range(6)])
        aux = Banks([ctx.enter_context(nc.psum_tensor("bank_aux", [P, T], F32))])
        stat_bank = ctx.enter_context(nc.psum_tensor("bank_stat", [P, T], F32))
        stat_free = []

        def blocks(name, numbers):
            return [a[name][i] for i in numbers]

        LRU_FIRST = [i for c in range(4) for i in (12 + c, 16 + c)]
        CONV_THEN = [i for c in range(4) for i in (4 + c, 8 + c, c)]
        plan = blocks("w_in", LRU_FIRST + CONV_THEN) + blocks("w_out", range(KD)) + blocks("w_q", range(HEADS))
        plan += blocks("expert_u", range(AHEAD * GROUP))
        mix_order = list(range(KEPT, N_GROUPS)) + list(range(KEPT))
        for g in mix_order:
            if g >= KEPT and g + 1 < N_GROUPS:
                plan += blocks("expert_u", range((g + 1) * GROUP, (g + 2) * GROUP))
            plan += blocks("expert_v", range(g * KD, (g + 1) * KD))
        plan += blocks("w_small2", [0]) + blocks("w_latent2", range(3)) + blocks("w_qk2", range(8)) \
            + blocks("w_v2", range(4)) + blocks("w_q_up", range(2)) + blocks("w_kv_up", [0]) \
            + blocks("w_gates2", range(16))
        plan += blocks("w_branch_a", range(4)) + blocks("w_branch_b", range(4)) + blocks("w_out2", range(KD))
        for f in range(FFN_TILES):
            plan += blocks("w_ffn_gate", [f]) + blocks("w_ffn_up", [f])
        for m in range(KD):
            plan += [a["w_ffn_down"][m][:, c:min(c + BLOCK, FFN_TILES * P)] for c in range(0, FFN_TILES * P, BLOCK)]

        columns = sb("columns", [P, N_COLUMNS])
        consts = sb("consts", [P, N_CONSTS])
        x = sb("residual", [P, KD, T])
        ada = sb("ada", [P, 48])
        gain2 = sb("gain2", [P, KD])
        h_hi = sb("h_hi", [P, KD, T], F32R)
        h_lo = sb("h_lo", [P, KD, T], F32R)
        square = sb("square", [P, 2, T])
        scaled = sb("scaled", [P, 2, T])
        root = sb("root", [P, T])
        rstd = root
        stream = WeightStream(nc, ctx, sp, act, dve, pool, plan)

        def const(name):
            lo, hi = CONST_AT[name]
            return consts[:, lo:hi]

        def col(name, i=0):
            c = COLUMN_AT[name] + i
            return columns[:, c:c + 1]

        def cols(name, n):
            return columns[:, COLUMN_AT[name]:COLUMN_AT[name] + n]

        small_landed = []
        for name, dst, src in (("columns", columns[:], a["columns"]), ("consts", consts[:], a["consts"]),
                               ("x", x[:], a["x"])):
            small_landed.append(Landing(sem(f"{name}_landed")).mark(nc.sync.dma_start(dst, src)))

        def three(out, w_hi, w_lo, m_hi, m_lo, start, stop):
            M.matmul(out, w_hi, m_lo, start=start, stop=False)
            M.matmul(out, w_hi, m_hi, start=False, stop=False)
            return M.matmul(out, w_lo, m_hi, start=False, stop=stop)

        def block_product(bank, block, m_hi, m_lo, m_ready, tiles, start, stop):
            _, hi, lo, hi_ready, lo_ready = block
            pe.after(hi_ready)
            for n, (c, k) in enumerate(tiles):
                pe.after(m_ready[k])
                M.matmul(bank[:], hi[:, c:c + P], m_lo[:, k, :], start=start and n == 0, stop=False)
                M.matmul(bank[:], hi[:, c:c + P], m_hi[:, k, :], start=False, stop=False)
            pe.after(lo_ready)
            for n, (c, k) in enumerate(tiles):
                ins = M.matmul(bank[:], lo[:, c:c + P], m_hi[:, k, :], start=False, stop=stop and n == len(tiles) - 1)
            return pe.mark(ins)

        def product(block, m_hi, m_lo, m_ready, nk=KD, at=0, last_use=True):
            b, bank, free = banks.take()
            pe.after(free)
            done = block_product(bank, block, m_hi, m_lo, m_ready, [(at + k * P, k) for k in range(nk)], True, True)
            if last_use:
                stream.used[block[0]] = done
            return b, bank, done

        def split_to(hi, lo, value, ready, hi_free=None):
            act.after(ready, hi_free)
            hi_done = act.mark(S.activation(hi, value, ACT.Copy))
            dve.after(ready, hi_done, hi_free)
            lo_done = dve.mark(V.tensor_tensor(lo, value, hi.bitcast(F32), ALU.subtract))
            return [hi_done, lo_done]

        square_free = [None, None]
        scaled_free = [None, None]

        def squared(src, n, ready):
            act.after(ready, square_free[n % 2])
            return act.mark(S.activation(square[:, n % 2, :], src, ACT.Square))

        def add_square(n, total, ready, matrix="ones"):
            pe.after(ready, *(stat_free if n == 0 else []))
            done = pe.mark(M.matmul(stat_bank[:], const(matrix), square[:, n % 2, :], start=n == 0, stop=n == total - 1))
            square_free[n % 2] = done
            return done

        rstd_free = []

        def inverse_rms(width, summed):
            act.after(summed, *rstd_free)
            rooted = act.mark(S.activation(root[:], stat_bank[:], ACT.Sqrt, bias=col("eps"), scale=1.0 / width))
            stat_free[:] = [rooted]
            dve.after(rooted, *rstd_free)
            rstd_free.clear()
            return dve.mark(V.reciprocal(rstd[:], root[:]))

        def norm_of_x(ready):
            for k in range(KD):
                summed = add_square(k, KD, squared(x[:, k, :], k, ready[k]))
            return inverse_rms(D, summed)

        def normalise(k, src, gain, shift, hi, lo, ready, free):
            dve.after(ready, scaled_free[k % 2])
            tmp = scaled[:, k % 2, :]
            tmp_done = dve.mark(V.scalar_tensor_tensor(tmp, src, gain, rstd[:], ALU.mult, ALU.mult))
            act.after(tmp_done, free)
            hi_done = act.mark(S.activation(hi, tmp, ACT.Identity, bias=0.0 if shift is None else shift))
            dve.after(tmp_done, hi_done, free)
            if shift is None:
                lo_done = dve.mark(V.tensor_tensor(lo, tmp, hi.bitcast(F32), ALU.subtract))
            else:
                lo_done = dve.mark(V.scalar_tensor_tensor(lo, tmp, shift, hi.bitcast(F32), ALU.add, ALU.subtract))
            scaled_free[k % 2] = lo_done
            rstd_free[:] = [lo_done]
            return [hi_done, lo_done]

        def add_to_x(k, bank_no, bank, done, gate):
            dve.after(done)
            if gate is None:
                m = dve.mark(V.tensor_tensor(x[:, k, :], bank[:], x[:, k, :], ALU.add))
            else:
                m = dve.mark(V.scalar_tensor_tensor(x[:, k, :], bank[:], gate, x[:, k, :], ALU.mult, ALU.add))
            banks.free[bank_no] = [m]
            return m

        def log1p_of(dst, e, t1, t2, n_parts, ready):
            dve.after(ready)
            m = dve.mark(V.tensor_scalar(t1, e, 2.0, None, ALU.add))
            dve.after(m)
            m = dve.mark(V.reciprocal(t2, t1))
            dve.after(m)
            m = dve.mark(V.tensor_tensor(t1, e, t2, ALU.mult))
            dve.after(m)
            m = dve.mark(V.tensor_tensor(t2, t1, t1, ALU.mult))
            dve.after(m)
            m = dve.mark(V.tensor_scalar(dst, t2, 2.0 / 17, 2.0 / 15, ALU.mult, ALU.add))
            for n in (13, 11, 9, 7, 5, 3, 1):
                dve.after(m)
                m = dve.mark(V.tensor_tensor(dst, dst, t2, ALU.mult))
                dve.after(m)
                m = dve.mark(V.tensor_scalar(dst, dst, 2.0 / n, None, ALU.add))
            dve.after(m)
            return dve.mark(V.tensor_tensor(dst, dst, t1, ALU.mult))

        mixer = ExitStack()

        def mb(name, shape, dt=F32):
            return sb(name, shape, dt, mixer)

        RING = 4
        c_act = mb("c_act", [P, D])
        ada_raw = [mb(f"ada_raw{i}", [P, D]) for i in range(RING)]
        ada_scratch = mb("ada_scratch", [P, D])
        ada_sum = mb("ada_sum", [P, 48])
        ada_landing = [Landing(sem(f"ada_raw{i}")) for i in range(RING)]
        ada_landed, ada_done = [], []

        def load_ada():
            j = len(ada_landed)
            if j < 48:
                sp.after(ada_done[j - RING] if j >= RING else None)
                ada_landed.append(ada_landing[j % RING].mark(nc.sync.dma_start(ada_raw[j % RING][:], a["w_ada"][j])))

        c_landed = Landing(sem("c_landed")).mark(nc.sync.dma_start(c_act[:], a["c_rows"]))
        for _ in range(RING):
            load_ada()
        act.after(c_landed)
        c_ready = act.mark(S.activation(c_act[:], c_act[:], ACT.Silu))

        def ada_tile():
            j = len(ada_done)
            dve.after(c_ready, ada_landed[j], ada_done[-1] if ada_done else None)
            ada_done.append(dve.mark(V.tensor_tensor_reduce(
                out=ada_scratch[:], in0=ada_raw[j % RING][:], in1=c_act[:], scale=1.0, scalar=0.0,
                op0=ALU.mult, op1=ALU.add, accum_out=ada_sum[:, j:j + 1])))
            load_ada()

        def ada_columns(lo, hi, plus=0.0):
            dve.after(ada_done[hi - 1], small_landed)
            return dve.mark(V.scalar_tensor_tensor(ada[:, lo:hi], ada_sum[:, lo:hi], plus,
                                                   columns[:, COLUMN_AT["b_ada"] + lo:COLUMN_AT["b_ada"] + hi],
                                                   ALU.add, ALU.add))

        x_rstd = norm_of_x([small_landed] * KD)
        for _ in range(16):
            ada_tile()
        stream.start()
        shift1 = ada_columns(0, 8)
        scale1 = ada_columns(8, 16, 1.0)
        gain = mb("gain", [P, KD])
        dve.after(scale1)
        gain1 = dve.mark(V.tensor_tensor(gain[:], ada[:, 8:16], cols("norm1", 8), ALU.mult))
        h_ready = [normalise(k, x[:, k, :], gain[:, k:k + 1], ada[:, k:k + 1], h_hi[:, k, :], h_lo[:, k, :],
                             [gain1, shift1, x_rstd], None) for k in range(KD)]

        lam_t = mb("lam_t", [P, 5, 4])
        dve.after(small_landed)
        m = dve.mark(V.tensor_scalar(lam_t[:, 0, :], cols("lam", 4), -1.0, None, ALU.mult))
        dve.after(m)
        m = dve.mark(V.tensor_tensor(lam_t[:, 1, :], lam_t[:, 0, :], cols("lam", 4), ALU.min))
        act.after(m)
        e_done = act.mark(S.activation(lam_t[:, 1, :], lam_t[:, 1, :], ACT.Exp))
        m = log1p_of(lam_t[:, 2, :], lam_t[:, 1, :], lam_t[:, 3, :], lam_t[:, 4, :], P, e_done)
        dve.after(m)
        m = dve.mark(V.scalar_tensor_tensor(lam_t[:, 2, :], lam_t[:, 0, :], 0.0, lam_t[:, 2, :], ALU.max, ALU.add))
        decay, minus_decay = lam_t[:, 3, :], lam_t[:, 4, :]
        dve.after(m)
        dve.mark(V.tensor_scalar(decay, lam_t[:, 2, :], LRU_C, None, ALU.mult))
        decay_done = dve.mark(V.tensor_scalar(minus_decay, lam_t[:, 2, :], -LRU_C, None, ALU.mult))

        gate_w = mb("lru_gate_w", [P, 2, 4, P])
        gate_w_landed = Landing(sem("gate_w_landed")).mark(nc.sync.dma_start(gate_w[:], a["w_lru_gates"]))
        padded = mb("padded", [P, 2, T + 3])
        pad_done = pool.mark(G.memset(padded[:, :, 0:3], 0.0))
        xc = mb("lru_x", [P, 4, T])
        r_gate = mb("r_gate", [P, 4, T])
        i_gate = mb("i_gate", [P, 4, T])
        u_fac = mb("u_fac", [P, 4, T])
        y = mb("y", [P, 8, T])
        y_hi, y_lo = h_hi, h_lo
        padded_free = [None, None]
        stream.on_pool = True
        gelu_done, r_done, i_done, xc_done = [], [], [], []
        for c in range(4):
            b, bank, done = product(stream.next(), h_hi, h_lo, h_ready)
            act.after(done, pad_done, padded_free[c % 2])
            m = act.mark(S.activation(padded[:, c % 2, 3:T + 3], bank[:], ACT.Copy))
            banks.free[b] = [m]
            b, bank, done = product(stream.next(), h_hi, h_lo, h_ready)
            act.after(done)
            m2 = act.mark(S.activation(y[:, 4 + c, :], bank[:], ACT.Gelu_apprx_tanh))
            banks.free[b] = [m2]
            gelu_done.append(m2)
            dve.after(m, small_landed)
            m = dve.mark(V.tensor_scalar(xc[:, c, :], padded[:, c % 2, 0:T], col("conv_b", c), col("conv_bias", c),
                                         ALU.mult, ALU.add))
            for j in range(1, 4):
                dve.after(m)
                m = dve.mark(V.scalar_tensor_tensor(xc[:, c, :], padded[:, c % 2, j:j + T], col("conv_b", 4 * j + c),
                                                    xc[:, c, :], ALU.mult, ALU.add))
            padded_free[c % 2] = m
            xc_done.append(m)
            for _ in range(3):
                ada_tile()
        for c in range(4):
            for g, (dst, bias, made) in enumerate(((r_gate, "b_r", r_done), (i_gate, "b_i", i_done))):
                b, bank, free = banks.take()
                pe.after(free, xc_done[c], gate_w_landed)
                done = pe.mark(M.matmul(bank[:], gate_w[:, g, c, :], xc[:, c, :], start=True, stop=True))
                act.after(done)
                made.append(act.mark(S.activation(dst[:, c, :], bank[:], ACT.Sigmoid, bias=col(bias, c))))
                banks.free[b] = [made[-1]]

        conv_pad = mb("conv_pad", [P, 2, T + 2])
        gate_c = mb("gate_c", [P, 2, T])
        conv_pad_zero = pool.mark(G.memset(conv_pad[:, :, 0:2], 0.0))
        conv_free, gate_c_free = [None, None], [None, None]
        y_done = [None] * 8

        def conv_tile(c):
            b, bank, done = product(stream.next(), h_hi, h_lo, h_ready)
            act.after(done, gate_c_free[c % 2])
            gc_done = act.mark(S.activation(gate_c[:, c % 2, :], bank[:], ACT.Copy))
            banks.free[b] = [gc_done]
            b, bank, done = product(stream.next(), h_hi, h_lo, h_ready)
            dve.after(done, gc_done, conv_pad_zero, conv_free[c % 2])
            m = dve.mark(V.tensor_tensor(conv_pad[:, c % 2, 2:T + 2], bank[:], gate_c[:, c % 2, :], ALU.mult))
            gate_c_free[c % 2] = m
            banks.free[b] = [m]
            dve.after(m, small_landed)
            m = dve.mark(V.tensor_scalar(y[:, c, :], conv_pad[:, c % 2, 0:T], col("conv_a", c), None, ALU.mult))
            for j in range(1, 3):
                dve.after(m)
                m = dve.mark(V.scalar_tensor_tensor(y[:, c, :], conv_pad[:, c % 2, j:j + T], col("conv_a", 4 * j + c),
                                                    y[:, c, :], ALU.mult, ALU.add))
            conv_free[c % 2] = m
            b, bank, done = product(stream.next(), h_hi, h_lo, h_ready)
            dve.after(done, m)
            y_done[c] = dve.mark(V.tensor_tensor(y[:, c, :], bank[:], y[:, c, :], ALU.mult))
            banks.free[b] = [y_done[c]]

        conv_tile(0)
        u_done, a_done = [], []
        for c in range(4):
            act.after(r_done[c], decay_done)
            u_done.append(act.mark(S.activation(u_fac[:, c, :], r_gate[:, c, :], ACT.Tanh, scale=decay[:, c:c + 1])))
            act.after(u_done[-1])
            a_done.append(act.mark(S.activation(r_gate[:, c, :], r_gate[:, c, :], ACT.Exp, scale=minus_decay[:, c:c + 1])))
        one_plus = mb("one_plus", [P, T])
        inverse = mb("inverse", [P, T])

        def lru_factor(c, before):
            dve.after(u_done[c], before)
            m = dve.mark(V.tensor_scalar(one_plus[:], u_fac[:, c, :], 1.0, None, ALU.add))
            dve.after(m)
            m = dve.mark(V.reciprocal(inverse[:], one_plus[:]))
            dve.after(m)
            m = dve.mark(V.scalar_tensor_tensor(u_fac[:, c, :], u_fac[:, c, :], 2.0, inverse[:], ALU.mult, ALU.mult))
            dve.after(i_done[c])
            m2 = dve.mark(V.tensor_tensor(i_gate[:, c, :], i_gate[:, c, :], xc[:, c, :], ALU.mult))
            return m, m2

        f = [None] * 4
        before = None
        for c in range(4):
            f[c] = lru_factor(c, before)
            before = f[c][0]
            for _ in range(5):
                ada_tile()
            if c:
                conv_tile(c)
        root_done = []
        for c in range(4):
            act.after(f[c][0])
            root_done.append(act.mark(S.activation(u_fac[:, c, :], u_fac[:, c, :], ACT.Sqrt)))
        for c in range(4):
            dve.after(root_done[c], f[c][1])
            m = dve.mark(V.tensor_tensor(i_gate[:, c, :], i_gate[:, c, :], u_fac[:, c, :], ALU.mult))
            dve.after(m, a_done[c])
            m = dve.mark(V.tensor_tensor_scan(xc[:, c, :], r_gate[:, c, :], i_gate[:, c, :], 0.0, ALU.mult, ALU.add))
            dve.after(m, gelu_done[c])
            y_done[4 + c] = dve.mark(V.tensor_tensor(y[:, 4 + c, :], y[:, 4 + c, :], xc[:, c, :], ALU.mult))
        assert len(ada_done) == 48
        late = ada_columns(16, 32)
        scale2 = ada_columns(32, 40, 1.0)
        g2_done = ada_columns(40, 48)
        dve.after(scale2)
        gain2_done = dve.mark(V.tensor_tensor(gain2[:], ada[:, 32:40], cols("norm2", 8), ALU.mult))

        projected = pe.count
        y_ready = [None] * 8
        for c in range(8):
            summed = add_square(0, 1, squared(y[:, c, :], 0, y_done[c]), "head_ones")
            rs_done = inverse_rms(HEAD_DIM, summed)
            y_ready[c] = normalise(c, y[:, c, :], col("gn", c), None, y_hi[:, c, :], y_lo[:, c, :], rs_done,
                                   (pe.sem, projected))

        x_done = [None] * KD
        sq = [None] * KD
        for k in range(KD):
            b, bank, done = product(stream.next(), y_hi, y_lo, y_ready)
            dve.after(late)
            x_done[k] = add_to_x(k, b, bank, done, ada[:, 16 + k:17 + k])
            sq[k] = squared(x[:, k, :], k, x_done[k])
            if k:
                add_square(k - 1, KD, sq[k - 1])
        summed = add_square(KD - 1, KD, sq[KD - 1])
        x_rstd = inverse_rms(D, summed)
        h_free = done
        mixer.close()
        mixer_over = [done, (act.sem, act.count), (dve.sem, dve.count), (pool.sem, pool.count)]

        h_ready = [normalise(k, x[:, k, :], gain2[:, k:k + 1], ada[:, 24 + k:25 + k], h_hi[:, k, :], h_lo[:, k, :],
                             [x_rstd, gain2_done], h_free) for k in range(KD)]
        peer = ExitStack()

        def pb(name, shape, dt=F32, scope=peer):
            return sb(name, shape, dt, scope)

        hidden = [pb(f"hidden{i}", [P, GROUP, T]) for i in range(2)]
        route = ExitStack()

        def rb(name, shape, dt=F32):
            return sb(name, shape, dt, route)

        scores = rb("scores", [P, TB, HEADS, 2, N_KEYS])
        q_tile = scaled
        key_scope = ExitStack()
        keys = sb("keys", [P, HEADS, N_KEYS], F32, key_scope)
        sp.after(mixer_over)
        keys_landed = Landing(sem("keys_landed")).mark(nc.sync.dma_start(keys[:], a["keys"]))
        act.after(mixer_over)
        dve.after(mixer_over)
        pool.after(mixer_over)

        q_free = list(scaled_free)
        score_done = []
        for h in range(HEADS):
            b, bank, done = product(stream.next(), h_hi, h_lo, h_ready)
            act.after(done, q_free[h % 2])
            q_done = act.mark(S.activation(q_tile[:, h % 2, :], bank[:], ACT.Copy))
            banks.free[b] = [q_done]
            for c in range(2):
                b, bank, free = banks.take()
                pe.after(free, q_done, keys_landed)
                for tb in range(TB):
                    ins = M.matmul(bank[:, tb * N_KEYS:(tb + 1) * N_KEYS],
                                   q_tile[64 * c:64 * c + 64, h % 2, tb * P:(tb + 1) * P],
                                   keys[64 * c:64 * c + 64, h, :], start=True, stop=True)
                done = pe.mark(ins)
                act.after(done)
                m = act.mark(S.activation(scores[:, :, h, c, :], bank[:].rearrange("p (t n) -> p t n", t=TB), ACT.Copy))
                banks.free[b] = [m]
                score_done.append(m)
            q_free[h % 2] = done
            scaled_free[h % 2] = done
        key_scope.close()
        keys_over = done

        top_s = rb("top_s", [P, HEADS, 2, TOPK])
        top_i = rb("top_i", [P, HEADS, 2, TOPK], U32)
        top_f = rb("top_f", [P, HEADS, 2, TOPK])
        sums = rb("sums", [P, 4, TOPK, TOPK])
        best = rb("best", [P, HEADS, TOPK])
        best_at = rb("best_at", [P, HEADS, TOPK], U32)
        half_at = rb("half_at", [P, 2, HEADS, TOPK], U32)
        half_f = rb("half_f", [P, 2, HEADS, TOPK])
        chosen = rb("chosen", [P, 3, HEADS * TOPK])
        total = rb("total", [P, 2, HEADS])
        equal = sums
        chosen_t = rb("chosen_t", [P, 3, P])
        one_hot = [rb(f"one_hot{i}", [P, 2, 4, P]) for i in range(N_HOT)]
        stage = [rb(f"stage{i}", [P, N_GROUPS, GROUP, TOK]) for i in range(2)]
        stage_sem = [Landing(sem(f"stage{i}_stored")) for i in range(2)]
        hidden_store = nc.dram_tensor("hidden_store", [KEPT, P, GROUP, T], F32, kind="Internal")
        coefs = nc.dram_tensor("expert_coefs", [N_GROUPS, P, T // TOK, GROUP, TOK], F32, kind="Internal")

        def chain(ins):
            m = dve.mark(ins)
            dve.after(m)
            return m

        chosen_free, chosen_t_free = None, None
        act.after(keys_over)
        dve.after(keys_over)

        def lockstep(*chains):
            last = [None] * len(chains)
            for steps in zip(*chains):
                for n, step in enumerate(steps):
                    dve.after(last[n])
                    last[n] = dve.mark(step())
            return last

        def top16(src, value, at, removed):
            return [lambda: V.max(value[:, 0:8], src),
                    lambda: V.max_index(at[:, 0:8], value[:, 0:8], src),
                    lambda: V.match_replace(src, value[:, 0:8], src, removed),
                    lambda: V.max(value[:, 8:16], src),
                    lambda: V.max_index(at[:, 8:16], value[:, 8:16], src)]

        def sums_of(dst, h):
            return lambda: V.tensor_tensor(dst, top_s[:, h, 0, :].unsqueeze(2).broadcast_to([P, TOPK, TOPK]),
                                           top_s[:, h, 1, :].unsqueeze(1).broadcast_to([P, TOPK, TOPK]), ALU.add)

        routed = {}

        def route_tokens(tb):
            for h in range(HEADS):
                dve.after(score_done[2 * h], score_done[2 * h + 1])
                last = lockstep(*[top16(scores[:, tb, h, c, :], top_s[:, h, c, :], top_i[:, h, c, :], NEG)
                                  for c in range(2)])
                yield
            dve.after(last)
            chain(V.tensor_copy(top_f[:], top_i[:]))
            for h in range(0, HEADS, 2):
                last = lockstep(*[[sums_of(sums[:, n], h + n)] +
                                  top16(sums[:, n].rearrange("p a b -> p (a b)"), best[:, h + n, :], best_at[:, h + n, :],
                                        2 * NEG) for n in range(2)])
                dve.after(last)
                yield
            chain(V.tensor_scalar(half_at[:, 0], best_at[:], 4, None, ALU.logical_shift_right))
            chain(V.tensor_scalar(half_at[:, 1], best_at[:], TOPK - 1, None, ALU.bitwise_and))
            chain(V.tensor_copy(half_f[:], half_at[:]))
            dve.after(chosen_free)
            for c in range(2):
                for q in range(2):
                    hs = slice(4 * q, 4 * q + 4)
                    chain(V.tensor_tensor(equal[:].rearrange("p h a b -> p (h a) b"),
                                          half_f[:, c, hs, :].rearrange("p h s -> p (h s)").unsqueeze(2)
                                          .broadcast_to([P, 4 * TOPK, TOPK]),
                                          const("iota16").unsqueeze(1).broadcast_to([P, 4 * TOPK, TOPK]), ALU.is_equal))
                    for n in range(4):
                        m = dve.mark(V.tensor_tensor(
                            equal[:, n], equal[:, n],
                            top_f[:, 4 * q + n, c, :].unsqueeze(1).broadcast_to([P, TOPK, TOPK]), ALU.mult))
                    dve.after(m)
                    chain(V.tensor_reduce(chosen[:, c, 64 * q:64 * q + 64],
                                          equal[:].rearrange("p h a b -> p (h a) b"), AX_X, ALU.add))
                    yield
            w = chosen[:, 2, :].rearrange("p (h s) -> p h s", h=HEADS)
            m = chain(V.tensor_tensor(w, best[:], best[:, :, 0:1].broadcast_to([P, HEADS, TOPK]), ALU.subtract))
            act.after(m)
            m = act.mark(S.activation(w, w, ACT.Exp))
            dve.after(m)
            chain(V.tensor_reduce(total[:, 0, :], w, AX_X, ALU.add))
            chain(V.reciprocal(total[:, 1, :], total[:, 0, :]))
            routed[tb] = chain(V.tensor_tensor(w, w, total[:, 1, :].unsqueeze(2).broadcast_to([P, HEADS, TOPK]), ALU.mult))
            yield

        stage_free = [None, None]
        hot_free = [None] * N_HOT
        turned = None

        def turn_chosen(tb):
            nonlocal chosen_free, turned
            b, bank, free = banks.take()
            pe.after(free, routed[tb])
            for n in range(3):
                ins = M.transpose(bank[:, n * P:(n + 1) * P], chosen[:, n, :], const("ident"))
            chosen_free = pe.mark(ins)
            act.after(chosen_free, chosen_t_free)
            turned = act.mark(S.activation(chosen_t[:].rearrange("p n t -> p (n t)"), bank[:, 0:3 * P], ACT.Copy))
            banks.free[b] = [turned]

        def place_tokens(tb, quad):
            nonlocal chosen_t_free
            k = quad % N_HOT
            hot = one_hot[k]
            t0 = 4 * quad
            iota = const("iota").unsqueeze(1).broadcast_to([P, 4, P])
            dve.after(turned, hot_free[k])
            dve.mark(V.tensor_tensor(hot[:, 0], chosen_t[:, 0, t0:t0 + 4].unsqueeze(2).broadcast_to([P, 4, P]),
                                     iota, ALU.is_equal))
            for t in range(4):
                m = dve.mark(V.tensor_scalar(hot[:, 1, t, :], const("iota"), chosen_t[:, 1, t0 + t:t0 + t + 1],
                                             chosen_t[:, 2, t0 + t:t0 + t + 1], ALU.is_equal, ALU.mult))
            chosen_t_free = m
            b, bank, free = banks.take()
            pe.after(free, m)
            for t in range(4):
                ins = M.matmul(bank[:, t * P:(t + 1) * P], hot[:, 0, t, :], hot[:, 1, t, :], start=True, stop=True)
            done = pe.mark(ins)
            hot_free[k] = done
            at = (t0 % TOK)
            s = ((tb * P + t0) // TOK)
            st = stage[s % 2]
            act.after(done, stage_free[s % 2] if at == 0 else None)
            e_done = act.mark(S.activation(st[:, :, :, at:at + 4].rearrange("p g j t -> p (g j) t"),
                                           bank[:].rearrange("p (t n) -> p n t", t=4), ACT.Copy))
            banks.free[b] = [e_done]
            if at == TOK - 4:
                sp.after(e_done)
                stage_free[s % 2] = stage_sem[s % 2].mark(nc.sync.dma_start(
                    coefs[:, :, s, :, :].rearrange("g p j t -> p g (j t)"),
                    st[:].rearrange("p g j t -> p g (j t)")))

        hidden_done = {}
        hidden_free = [None, None]
        HALF = GROUP // 2
        hidden_stored = [Landing(sem(f"hidden{i}_stored")) for i in range(2)]
        hidden_saved = {}

        def save_hidden(j):
            g, n = divmod(j - HALF, GROUP)
            if j % HALF == 0 and 0 <= g < KEPT:
                sp.after(hidden_done[j - 1])
                hidden_saved[g] = hidden_stored[g % 2].mark(nc.sync.dma_start(
                    hidden_store[g, :, n:n + HALF, :], hidden[g % 2][:, n:n + HALF, :]))
                hidden_free[g % 2] = hidden_saved[g]

        def hidden_block(j):
            g, n = divmod(j, GROUP)
            b, bank, done = product(stream.next(), h_hi, h_lo, h_ready)
            save_hidden(j)
            act.after(done, hidden_free[g % 2])
            hidden_done[j] = act.mark(S.activation(hidden[g % 2][:, n, :], bank[:], ACT.Gelu))
            banks.free[b] = [hidden_done[j]]

        n_u = AHEAD * GROUP
        router = route_tokens(0)
        for _ in router:
            if len(hidden_done) < FIRST_U:
                hidden_block(len(hidden_done))
        for tb in range(TB):
            turn_chosen(tb)
            router = route_tokens(tb + 1) if tb + 1 < TB else iter(())
            first = len(hidden_done)
            share = (n_u - first) // (TB - tb)
            quads = P // 4
            for n in range(share):
                next(router, None)
                for quad in range(quads * n // share, quads * (n + 1) // share):
                    place_tokens(tb, quad)
                if n >= share - 2 * (ROUTE_PIECES - share):
                    next(router, None)
                hidden_block(first + n)
            for _ in router:
                pass
        save_hidden(n_u)
        route_over = [(act.sem, act.count), (dve.sem, dve.count), (pool.sem, pool.count), (pe.sem, pe.count)] + stage_free
        route.close()
        stream.on_pool = False
        act.after(route_over)
        dve.after(route_over)

        weight = [pb(f"weight{i}", [P, T // TOK, GROUP, TOK]) for i in range(2)]
        weight_landing = [Landing(sem(f"weight{i}_landed")) for i in range(2)]
        mixed_hi = pb("mixed_hi", [P, GROUP, T], F32R)
        mixed_lo = pb("mixed_lo", [P, GROUP, T], F32R)
        weight_landed, weight_used = {}, {}

        mixed = [(mixed_hi, mixed_lo), (h_hi, h_lo)]
        mixed_free = [None, None]
        mixed_ready = {}
        pairs = {}
        for i, g in enumerate(mix_order):
            last_u = N_GROUPS - 1 - KEPT
            pairs[g] = (i - last_u + 1) % 2 if i >= last_u else 0
        late_lo = None

        def finish_mix():
            nonlocal late_lo
            if late_lo:
                g, n, hi_done = late_lo
                hi, lo = mixed[pairs[g]]
                dve.after(hi_done)
                lo_done = dve.mark(V.tensor_tensor(lo[:, n, :], hidden[g % 2][:, n, :], hi[:, n, :].bitcast(F32), ALU.subtract))
                mixed_ready[g].append([hi_done, lo_done])
                late_lo = None

        def mix_tile(i, n):
            nonlocal late_lo
            if i >= len(mix_order):
                return
            g = mix_order[i]
            pair = pairs[g]
            hi, lo = mixed[pair]
            v = hidden[g % 2][:, n, :]
            ready = hidden_done[g * GROUP + n] if g >= KEPT else hidden_loaded[g]
            dve.after(ready, weight_landed[g])
            m = dve.mark(V.tensor_tensor(v.rearrange("p (s t) -> p s t", t=TOK), v.rearrange("p (s t) -> p s t", t=TOK),
                                         weight[g % 2][:, :, n, :], ALU.mult))
            act.after(m, mixed_free[pair])
            dve.after(mixed_free[pair])
            hi_done = act.mark(S.activation(hi[:, n, :], v, ACT.Copy))
            finish_mix()
            mixed_ready.setdefault(g, [])
            late_lo = (g, n, hi_done)
            if n == GROUP - 1:
                finish_mix()
                weight_used[g] = m
                hidden_free[g % 2] = mixed_ready[g][-1]
                if i + 2 < len(mix_order):
                    load_group(mix_order[i + 2])

        hidden_landing = [Landing(sem(f"hidden{i}_landed")) for i in range(2)]
        hidden_loaded = {}

        def load_group(g):
            pool.after(route_over, weight_used.get((g - 2) % N_GROUPS))
            weight_landed[g] = weight_landing[g % 2].mark(G.dma_start(
                weight[g % 2][:].rearrange("p s j t -> p (s j t)"), coefs[g].rearrange("p s j t -> p (s j t)")))
            if g < KEPT:
                pool.after(hidden_saved[g], hidden_free[g % 2])
                hidden_loaded[g] = hidden_landing[g % 2].mark(G.dma_start(hidden[g % 2][:], hidden_store[g]))

        load_group(mix_order[0])
        load_group(mix_order[1])
        for i, g in enumerate(mix_order):
            beside_u = KEPT <= g < N_GROUPS - 1
            if beside_u:
                for n in range(GROUP):
                    mix_tile(i, n)
                    hidden_block((g + 1) * GROUP + n)
                mixed_free[1] = (pe.sem, pe.count)
            for k in range(KD):
                b, bank, done = product(stream.next(), *mixed[pairs[g]], mixed_ready[g], nk=GROUP)
                if not (KEPT <= g < N_GROUPS - 2):
                    mix_tile(i + 1, k)
                dve.after(g2_done)
                x_done[k] = add_to_x(k, b, bank, done, ada[:, 40 + k:41 + k])
            mixed_free[pairs[g]] = done
        peer.close()
        peer_over = [(act.sem, act.count), (dve.sem, dve.count), (pe.sem, pe.count)]
        h_free = (pe.sem, pe.count)

        x_rstd = norm_of_x(x_done)
        for k in range(KD):
            dve.after(x_rstd)
            x_done[k] = dve.mark(V.scalar_tensor_tensor(x[:, k, :], x[:, k, :], col("final", k), rstd[:], ALU.mult, ALU.mult))
            rstd_free[:] = [x_done[k]]
        x_rstd = norm_of_x(x_done)
        h_ready = [normalise(k, x[:, k, :], col("norm_mix", k), None, h_hi[:, k, :], h_lo[:, k, :], x_rstd, h_free)
                   for k in range(KD)]
        att = ExitStack()

        def ab(name, shape, dt=F32):
            return sb(name, shape, dt, att)

        act.after(peer_over)
        dve.after(peer_over)
        pool.after(peer_over)
        sp.after(peer_over)
        q_a = ab("q_a", [P, 4, T])
        k_a = ab("k_a", [P, 4, T])
        v_a = ab("v_a", [P, TB, 512])
        v_b = ab("v_b", [P, TB, 512])
        q_b = ab("q_b", [P, 4, T])
        k_b = ab("k_b", [P, 4, T])
        q_rot = ab("q_rot", [P, 2, T])
        k_rot = ab("k_rot", [P, T])
        key_bias = ab("key_bias", [HEADS, T])
        gates = ab("gates", [P, 16, T])
        latent = gates[:, 13:16, :]
        forget = gates[0:HEADS, 8:13, :]
        turns = gates[:, 7, :]
        position = gates[:, 6, :].bitcast(I32)
        table = gates[:, 5, :]
        early = ExitStack()
        latent_hi = sb("latent_hi", [P, 3, T], F32R, early)
        latent_lo = sb("latent_lo", [P, 3, T], F32R, early)
        rotated = sb("rotated", [P, 2, T], F32, early)

        position_landed = Landing(sem("position_landed")).mark(nc.sync.dma_start(position, a["positions"]))
        dve.after(position_landed)
        chain(V.tensor_copy(table, position))
        chain(V.tensor_scalar(table[:], table[:], col("inv_freq"), None, ALU.mult))
        ROUND = 1.5 * 2.0 ** 23
        for scale, parts in ((256.0, two_pi_parts(256.0, 10, 5)), (1.0, two_pi_parts(1.0, 14, 2))):
            chain(V.tensor_scalar(turns, table, 1.0 / (2 * math.pi * scale), ROUND, ALU.mult, ALU.add))
            chain(V.tensor_scalar(turns, turns, -ROUND, None, ALU.add))
            for part in parts:
                chain(V.scalar_tensor_tensor(table, turns, -part, table, ALU.mult, ALU.add))
        chain(V.tensor_scalar(table, table, col("phase"), None, ALU.add))
        chain(V.tensor_scalar(turns, table, math.pi, -2 * math.pi, ALU.is_gt, ALU.mult))
        chain(V.tensor_tensor(table, table, turns, ALU.add))
        m = chain(V.tensor_scalar(table, table, 3.1415925, -3.1415925, ALU.min, ALU.max))
        act.after(m)
        m = act.mark(S.activation(table, table, ACT.Sin))
        dve.after(m)
        table_done = chain(V.tensor_scalar(table, table, col("sign"), None, ALU.mult))

        def rotate(dsts, bank, ready):
            dve.after(ready, table_done, (dve.sem, dve.count))
            m1 = dve.mark(V.tensor_tensor(rotated[64:96, 0, :], bank[64:96, :], table[64:96, :], ALU.mult))
            dve.after(m1)
            m = dve.mark(V.tensor_tensor(rotated[64:96, 1, :], bank[96:128, :], table[96:128, :], ALU.mult))
            dve.after(m)
            for dst in dsts:
                m2 = dve.mark(V.tensor_tensor(dst, rotated[64:96, 0, :], rotated[64:96, 1, :], ALU.add))
            return m, m2

        b, bank, done = product(stream.next(), h_hi, h_lo, h_ready)
        dve.after(done)
        m = chain(V.tensor_scalar(forget[:, 0, :], bank[0:8, :], columns[0:8, COLUMN_AT["b_forget"]:COLUMN_AT["b_forget"] + 1],
                                  None, ALU.add))
        m_rot, k_rot_done = rotate([k_rot[32 * n:32 * n + 32, :] for n in range(4)], bank, done)
        banks.free[b] = [m_rot, m]
        chain(V.tensor_scalar(forget[:, 1, :], forget[:, 0, :], -1.0, None, ALU.mult))
        m = chain(V.tensor_tensor(forget[:, 1, :], forget[:, 1, :], forget[:, 0, :], ALU.min))
        act.after(m)
        m = act.mark(S.activation(forget[:, 1, :], forget[:, 1, :], ACT.Exp))
        m = log1p_of(forget[:, 2, :], forget[:, 1, :], forget[:, 3, :], forget[:, 4, :], HEADS, m)
        dve.after(m)
        chain(V.scalar_tensor_tensor(forget[:, 1, :], forget[:, 0, :], 0.0, forget[:, 2, :], ALU.min, ALU.subtract))
        chain(V.memset(forget[:, 2, :], 1.0))
        chain(V.tensor_tensor_scan(forget[:, 3, :], forget[:, 2, :], forget[:, 1, :], 0.0, ALU.mult, ALU.add))
        bias_done = chain(V.tensor_scalar(key_bias[:], forget[:, 3, :], -1.0 / ATT_SCALE_A, None, ALU.mult))

        lat = []
        for n in range(3):
            b, bank, done = product(stream.next(), h_hi, h_lo, h_ready)
            act.after(done)
            lat.append(act.mark(S.activation(latent[:, n, :], bank[:], ACT.Copy)))
            banks.free[b] = [lat[-1]]
        add_square(0, 2, squared(latent[:, 0, :], 0, lat[0]))
        summed = add_square(1, 2, squared(latent[:, 1, :], 1, lat[1]))
        rs = inverse_rms(2 * P, summed)
        lat_ready = [normalise(n, latent[:, n, :], col("q_norm", n), None, latent_hi[:, n, :], latent_lo[:, n, :], rs, None)
                     for n in range(2)]
        summed = add_square(0, 1, squared(latent[:, 2, :], 0, lat[2]))
        rs = inverse_rms(P, summed)
        lat_ready.append(normalise(0, latent[:, 2, :], col("kv_norm"), None, latent_hi[:, 2, :], latent_lo[:, 2, :], rs, None))

        qk_done = []
        for n in range(8):
            b, bank, done = product(stream.next(), h_hi, h_lo, h_ready)
            act.after(done)
            qk_done.append(act.mark(S.activation((q_a if n < 4 else k_a)[:, n % 4, :], bank[:], ACT.Copy)))
            banks.free[b] = [qk_done[-1]]
        taken = [banks.take() for _ in range(TB)]
        for n in range(4):
            block = stream.next()
            pe.after(block[3], block[4])
            for kk in range(2):
                k = 2 * n + kk
                for tb, (b, bank, free) in enumerate(taken):
                    pe.after(free if k == 0 else None)
                    w = slice(kk * 512, kk * 512 + 512)
                    t = slice(tb * P, tb * P + P)
                    ins = three(bank[:], h_hi[:, k, t], h_lo[:, k, t], block[1][:, w], block[2][:, w], k == 0, k == KD - 1)
            stream.used[block[0]] = pe.mark(ins)
        va_done = []
        for tb, (b, bank, free) in enumerate(taken):
            act.after(stream.used[block[0]])
            va_done.append(act.mark(S.activation(v_a[:, tb, :], bank[:], ACT.Copy)))
            banks.free[b] = [va_done[-1]]
        qb_done = []
        for h in range(HEADS):
            if h % 4 == 0:
                n, hi, lo, *ready = stream.next()
            b, bank, free = banks.take()
            pe.after(free, ready)
            for k in range(2):
                pe.after(lat_ready[k])
                c = k * 512 + (h % 4) * P
                ins = three(bank[:], hi[:, c:c + P], lo[:, c:c + P], latent_hi[:, k, :], latent_lo[:, k, :], k == 0, k == 1)
            done = pe.mark(ins)
            if h % 4 == 3:
                stream.used[n] = done
            m_rot, rot_done = rotate([q_rot[32 * (h % 4):32 * (h % 4) + 32, h // 4, :]], bank, done)
            act.after(done, m_rot)
            m = act.mark(S.activation(q_b[64 * (h % 2):64 * (h % 2) + 64, h // 2, :], bank[0:64, :], ACT.Copy))
            banks.free[b] = [m_rot, m]
            qb_done.append([m, rot_done])
        block = stream.next()
        kb_done = []
        for h in range(0, HEADS, 2):
            b, bank, free = banks.take()
            pe.after(free, block[3], block[4], lat_ready[2])
            c = h * 64
            done = pe.mark(three(bank[:], block[1][:, c:c + P], block[2][:, c:c + P], latent_hi[:, 2, :], latent_lo[:, 2, :],
                                 True, True))
            act.after(done)
            kb_done.append(act.mark(S.activation(k_b[:, h // 2, :], bank[:], ACT.Copy)))
            banks.free[b] = [kb_done[-1]]
        vb_done = []
        for tb in range(TB):
            b, bank, free = banks.take()
            pe.after(free)
            t = slice(tb * P, tb * P + P)
            done = pe.mark(three(bank[:], latent_hi[:, 2, t], latent_lo[:, 2, t], block[1][:, 512:], block[2][:, 512:], True, True))
            act.after(done)
            vb_done.append(act.mark(S.activation(v_b[:, tb, :], bank[:], ACT.Copy)))
            banks.free[b] = [vb_done[-1]]
        stream.used[block[0]] = done

        gate_done = []

        def gate_block():
            n = len(gate_done)
            b, bank, done = product(stream.next(), h_hi, h_lo, h_ready)
            act.after(done)
            gate_done.append(act.mark(S.activation(gates[:, n, :], bank[:], ACT.Sigmoid, bias=col("b_gate", n))))
            banks.free[b] = [gate_done[-1]]

        for _ in range(16):
            gate_block()
        early_over = [(pe.sem, pe.count), (dve.sem, dve.count), (act.sem, act.count)]
        early.close()
        act.after(early_over)
        dve.after(early_over)
        prob = [square[:, 0, :], square[:, 1, :], scaled[:, 0, :]]
        prob_t = [ab(f"prob_t{i}", [P, TB, T]) for i in range(2)]
        stats = ab("att_stats", [P, 64, 4])
        att_hi, att_lo = h_hi, h_lo
        units = [(kind, h, i) for kind in (0, 1) for h in range(HEADS) for i in range(TB)]
        state = {}
        prob_free, prob_t_free = [None] * 3, [None] * 2
        att_ready = [None] * 8

        def score(u):
            kind, h, i = units[u]
            n = (i + 1) * P
            b, bank, free = banks.take()
            pe.after(free)
            q = slice(i * P, i * P + P)
            if kind == 0:
                r = slice(64 * (h % 2), 64 * (h % 2) + 64)
                pe.after(qk_done[h // 2], qk_done[4 + h // 2], bias_done)
                M.matmul(bank[:, 0:n], q_a[r, h // 2, q], k_a[r, h // 2, 0:n], start=True, stop=False)
                pick_head = const("ident")[0:HEADS, h:h + 1].broadcast_to([HEADS, P])
                M.matmul(bank[:, 0:n], pick_head, key_bias[:, 0:n], start=False, stop=False)
            else:
                pe.after(qb_done[h], kb_done[h // 2], k_rot_done)
                r = slice(64 * (h % 2), 64 * (h % 2) + 64)
                M.matmul(bank[:, 0:n], q_b[r, h // 2, q], k_b[r, h // 2, 0:n], start=True, stop=False)
                r = slice(32 * (h % 4), 32 * (h % 4) + 32)
                M.matmul(bank[:, 0:n], q_rot[r, h // 4, q], k_rot[r, 0:n], start=False, stop=False)
            mask = const("causal" if kind == 0 else "chunk")
            state[u] = {"scored": pe.mark(M.matmul(bank[:, n - P:n], const("ident"), mask, start=False, stop=True)),
                        "bank": bank, "b": b, "n": n}

        def row_max(u):
            s = state[u]
            scale = ATT_SCALE_A if units[u][0] == 0 else ATT_SCALE_B
            dve.after(s["scored"])
            m = dve.mark(V.tensor_reduce(stats[:, u, 0:1], s["bank"][:, 0:s["n"]], AX_X, ALU.max))
            dve.after(m)
            s["max"] = dve.mark(V.tensor_scalar(stats[:, u, 1:2], stats[:, u, 0:1], -scale, None, ALU.mult))

        def exponent(u):
            s = state[u]
            scale = ATT_SCALE_A if units[u][0] == 0 else ATT_SCALE_B
            act.after(s["max"], prob_free[u % 3])
            s["exp"] = act.mark(S.activation(prob[u % 3][:, 0:s["n"]], s["bank"][:, 0:s["n"]], ACT.Exp,
                                             bias=stats[:, u, 1:2], scale=scale, accum_out=stats[:, u, 2:3]))
            banks.free[s["b"]] = [s["exp"]]

        def divide(u):
            s = state[u]
            dve.after(s["exp"])
            m = dve.mark(V.reciprocal(stats[:, u, 3:4], stats[:, u, 2:3]))
            dve.after(m)
            p = prob[u % 3][:, 0:s["n"]]
            s["prob"] = dve.mark(V.tensor_scalar(p, p, stats[:, u, 3:4], None, ALU.mult))

        def turn(u):
            kind, h, i = units[u]
            s = state[u]
            b, bank, free = banks.take()
            pe.after(free, s["prob"])
            for kb in range(i + 1):
                ins = M.transpose(bank[:, kb * P:(kb + 1) * P], prob[u % 3][:, kb * P:(kb + 1) * P], const("ident"))
            s["turned"] = pe.mark(ins)
            prob_free[u % 3] = s["turned"]
            head_no = u // TB
            q, e = (act, S) if u % 2 else (dve, V)
            q.after(s["turned"], prob_t_free[head_no % 2])
            dst = prob_t[head_no % 2][:, 0:i + 1, i * P:(i + 1) * P]
            src = bank[:, 0:(i + 1) * P].rearrange("p (k q) -> p k q", q=P)
            s["kept"] = q.mark(e.activation(dst, src, ACT.Copy) if u % 2 else e.tensor_copy(dst, src))
            banks.free[b] = [s["kept"]]

        def values(head_no):
            kind, h = divmod(head_no, HEADS)
            b, bank, free = banks.take()
            pe.after(free, *[state[head_no * TB + i]["kept"] for i in range(TB)])
            pe.after(va_done if kind == 0 else vb_done)
            v = v_a if kind == 0 else v_b
            pair = slice((h // 2) * P, (h // 2) * P + P)
            for kb in range(TB):
                ins = M.matmul(bank[:, kb * P:T], v[:, kb, pair], prob_t[head_no % 2][:, kb, kb * P:T],
                               start=kb == 0, stop=kb == TB - 1)
            done = pe.mark(ins)
            prob_t_free[head_no % 2] = done
            r = slice(64 * (h % 2), 64 * (h % 2) + 64)
            tile = 4 * kind + h // 2
            act.after(done)
            hi_done = act.mark(S.activation(att_hi[r, tile, :], bank[r, :], ACT.Copy))
            dve.after(hi_done)
            lo_done = dve.mark(V.tensor_tensor(att_lo[r, tile, :], bank[r, :], att_hi[r, tile, :].bitcast(F32), ALU.subtract))
            banks.free[b] = [lo_done]
            att_ready[tile] = (att_ready[tile] or []) + [hi_done, lo_done]

        n_units = len(units)
        for s in range(n_units + 5):
            if s < n_units:
                score(s)
                row_max(s)
                exponent(s)
            if 0 <= s - 1 < n_units:
                divide(s - 1)
            if 0 <= s - 2 < n_units:
                turn(s - 2)
            if s >= 4 and (s - 3) % TB == 0 and (s - 3) // TB <= 2 * HEADS:
                values((s - 3) // TB - 1)
            if s == n_units + 3:
                break

        merged = gates
        for m2 in range(4):
            block = stream.next()
            for n in range(2):
                k = 2 * m2 + n
                b, bank, done = product(block, att_hi[:, 0:4], att_lo[:, 0:4], att_ready[0:4], nk=4, at=n * 512, last_use=n == 1)
                dve.after(done, gate_done[k])
                x_m = dve.mark(V.tensor_tensor(merged[:, k, :], bank[:], gates[:, k, :], ALU.mult))
                banks.free[b] = [x_m]
        pending = []
        for m2 in range(4):
            block = stream.next()
            for n in range(2):
                k = 2 * m2 + n
                b, bank, done = product(block, att_hi[:, 4:8], att_lo[:, 4:8], att_ready[4:8], nk=4, at=n * 512, last_use=n == 1)
                dve.after(done, gate_done[8 + k])
                m = dve.mark(V.tensor_tensor(gates[:, 8 + k, :], bank[:], gates[:, 8 + k, :], ALU.mult))
                banks.free[b] = [m]
                dve.after(m, x_m)
                pending.append(dve.mark(V.tensor_tensor(merged[:, k, :], merged[:, k, :], gates[:, 8 + k, :], ALU.add)))
        h_free = done
        for k in range(KD):
            h_ready[k] = split_to(h_hi[:, k, :], h_lo[:, k, :], merged[:, k, :], pending[k], h_free)

        def residual(n_blocks, m_hi, m_lo, m_ready, gate=None):
            for k in range(KD):
                b, bank, free = banks.take()
                pe.after(free)
                kk = 0
                for n in range(n_blocks):
                    block = stream.next()
                    tiles = stream.plan[block[0]].shape[1] // P
                    done = block_product(bank, block, m_hi, m_lo, m_ready, [(c * P, kk + c) for c in range(tiles)],
                                         n == 0, n == n_blocks - 1)
                    kk += tiles
                    stream.used[block[0]] = done
                x_done[k] = add_to_x(k, b, bank, done, gate)
                sq[k] = squared(x[:, k, :], k, x_done[k])
                if k:
                    add_square(k - 1, KD, sq[k - 1])
            return inverse_rms(D, add_square(KD - 1, KD, sq[KD - 1])), done

        x_rstd, h_free = residual(1, h_hi, h_lo, h_ready)
        att.close()
        att_over = [(act.sem, act.count), (dve.sem, dve.count), (pe.sem, pe.count)]

        h_ready = [normalise(k, x[:, k, :], col("norm_ffn", k), None, h_hi[:, k, :], h_lo[:, k, :], x_rstd, h_free)
                   for k in range(KD)]
        ffn = ExitStack()
        f_hi = sb("ffn_hi", [P, FFN_TILES, T], F32R, ffn)
        f_lo = sb("ffn_lo", [P, FFN_TILES, T], F32R, ffn)
        silu = sb("silu", [P, 2, T], F32, ffn)
        act.after(att_over)
        dve.after(att_over)
        f_ready, silu_free = [], [None, None]
        for f in range(FFN_TILES):
            b, bank, done = product(stream.next(), h_hi, h_lo, h_ready)
            act.after(done, silu_free[f % 2])
            s_done = act.mark(S.activation(silu[:, f % 2, :], bank[:], ACT.Silu))
            banks.free[b] = [s_done]
            b, bank, done = product(stream.next(), h_hi, h_lo, h_ready)
            dve.after(done, s_done)
            m = dve.mark(V.tensor_tensor(silu[:, f % 2, :], bank[:], silu[:, f % 2, :], ALU.mult))
            banks.free[b] = [m]
            f_ready.append(split_to(f_hi[:, f, :], f_lo[:, f, :], silu[:, f % 2, :], m))
            silu_free[f % 2] = f_ready[-1]
        x_rstd, _ = residual(3, f_hi, f_lo, f_ready)
        ffn.close()

        stored = Landing(sem("out_stored"))
        for k in range(KD):
            dve.after(x_rstd)
            m = dve.mark(V.scalar_tensor_tensor(x[:, k, :], x[:, k, :], col("norm_final", k), rstd[:], ALU.mult, ALU.mult))
            sp.after(m)
            end = stored.mark(nc.sync.dma_start(out_cols[:, k, :], x[:, k, :]))
        sp.after(end)
        assert len(stream.used) == len(plan)


def in_tiles(w):
    k, n = w.shape
    return w.reshape(k // P, P, n // P, P).transpose(2, 1, 0, 3).reshape(n // P, P, k)


def per_column(v):
    return np.asarray(v).reshape(-1, P).T


def constant_matrices():
    r = np.arange(P)
    m = {
        "ones": np.ones((P, P)),
        "head_ones": (r[:, None] // HEAD_DIM == r[None, :] // HEAD_DIM),
        "ident": np.eye(P),
        "iota": np.broadcast_to(r[None, :], (P, P)),
        "causal": np.where(r[None, :] <= r[:, None], 0.0, NEG),
        "chunk": np.where(r[None, :] // 64 <= r[:, None] // 64, 0.0, NEG),
        "iota16": np.broadcast_to(np.arange(16)[None, :], (P, 16)),
    }
    return np.concatenate([m[n].astype(np.float32) for n, _ in CONSTS], axis=1)


def lay_out(i):
    f32 = np.float32
    half = ROPE // 2
    row = np.arange(P)
    inv = (10000.0 ** (-np.arange(half, dtype=np.float64) / half)).astype(f32)
    is_cos = (row >= 64) & (row < 96)
    first = (row % 32) < half
    forget_col = np.zeros((P, 1), f32)
    forget_col[0:HEADS, 0] = i["b_forget_2"][0]
    parts = {
        "b_ada": per_column(i["b_ada"][0]), "norm1": per_column(i["norm1_g"][0]),
        "conv_a": per_column(i["conv_a_w"][0]), "conv_b": per_column(i["conv_b_w"][0]),
        "conv_bias": per_column(i["conv_b_b"][0]), "b_r": per_column(i["b_r"][0]), "b_i": per_column(i["b_i"][0]),
        "lam": per_column(i["lru_lambda"][0]),
        "gn": np.concatenate([per_column(i["gn_a"][0]), per_column(i["gn_b"][0])], axis=1),
        "norm2": per_column(i["norm2_g"][0]), "final": per_column(i["final_g"]),
        "norm_mix": per_column(i["norm_mix_g_2"][0]), "q_norm": per_column(i["q_a_norm_g_2"][0]),
        "kv_norm": per_column(i["kv_a_norm_g_2"][0]), "b_gate": per_column(i["b_gate_2"][0]),
        "norm_ffn": per_column(i["norm_ffn_g_2"][0]), "norm_final": per_column(i["norm_final_g_2"]),
        "b_forget": forget_col, "inv_freq": inv[row % half][:, None],
        "phase": np.where(is_cos, math.pi / 2, 0.0).astype(f32)[:, None],
        "sign": np.where(~is_cos & first, -1.0, 1.0).astype(f32)[:, None],
        "eps": np.full((P, 1), EPS, f32),
    }
    out = {"columns": np.concatenate([parts[n] for n, _ in COLUMNS], axis=1), "consts": constant_matrices()}
    out["x"] = i["x"][0].T.reshape(KD, P, T).transpose(1, 0, 2)
    out["c_rows"] = np.broadcast_to(i["c"][0], (P, D))
    out["w_ada"] = i["w_ada"][0].T.reshape(48, P, D)
    out["w_in"] = in_tiles(i["w_in"][0])
    out["w_out"] = in_tiles(i["w_out"][0])
    out["w_q"] = in_tiles(i["w_q"][0])
    gates = np.zeros((P, 2, 4, P), f32)
    for g, name in enumerate(("w_r", "w_i")):
        for h in range(HEADS):
            r = slice(64 * (h % 2), 64 * (h % 2) + 64)
            gates[r, g, h // 2, r] = i[name][0, h]
    out["w_lru_gates"] = gates
    out["keys"] = i["sub_keys"][0].transpose(1, 3, 0, 2).reshape(P, HEADS, N_KEYS)
    out["expert_u"] = i["expert_u"][0].reshape(N_KEYS, N_KEYS, KD, P).transpose(1, 3, 2, 0).reshape(N_KEYS, P, BLOCK)
    out["expert_v"] = i["expert_v"][0].reshape(N_KEYS, N_GROUPS, GROUP, KD, P).transpose(1, 3, 0, 2, 4).reshape(
        N_GROUPS * KD, P, BLOCK)
    w = i["w_in_2"][0]
    qa, ka, va, fa, cq, ckv, kr, ga, gb = np.split(w, np.cumsum([512, 512, 512, 8, 256, 128, 32, 1024]), axis=1)
    small = np.concatenate([fa, np.zeros((D, 56), f32), kr, kr[:, half:], kr[:, :half]], axis=1)
    out["w_small2"] = in_tiles(small)
    out["w_latent2"] = in_tiles(np.concatenate([cq, ckv], axis=1))
    out["w_qk2"] = in_tiles(np.concatenate([qa, ka], axis=1))
    out["w_v2"] = va.reshape(4, 2, P, 512).transpose(0, 2, 1, 3).reshape(4, P, BLOCK)
    out["w_gates2"] = in_tiles(np.concatenate([ga, gb], axis=1))
    qu = i["w_q_up_2"][0].reshape(2 * P, HEADS, NOPE + ROPE)
    qu = np.concatenate([qu, qu[:, :, NOPE + half:], qu[:, :, NOPE:NOPE + half]], axis=2)
    out["w_q_up"] = qu.reshape(2, P, 2, 4, P).transpose(2, 1, 0, 3, 4).reshape(2, P, BLOCK)
    kv = i["w_kv_up_2"][0].reshape(P, HEADS, 2, 64).transpose(0, 2, 1, 3)
    out["w_kv_up"] = kv.reshape(1, P, BLOCK)
    for name, w in (("w_branch_a", i["w_branch_a_2"][0]), ("w_branch_b", i["w_branch_b_2"][0])):
        out[name] = w.reshape(4, P, 4, 2, P).transpose(2, 1, 3, 0, 4).reshape(4, P, BLOCK)
    out["w_out2"] = in_tiles(i["w_out_2"][0])
    out["w_ffn_gate"] = in_tiles(i["w_ffn_gate_2"][0])
    out["w_ffn_up"] = in_tiles(i["w_ffn_up_2"][0])
    out["w_ffn_down"] = in_tiles(i["w_ffn_down_2"][0])
    out["positions"] = np.broadcast_to(i["positions_2"][0], (P, T))
    return {k: np.ascontiguousarray(v) for k, v in out.items()}


def kernel(**inputs):
    import concourse.bacc as bacc
    from concourse.bass_utils import run_bass_kernel_spmd

    arrays = lay_out({k: np.asarray(v) for k, v in inputs.items()})
    nc = bacc.Bacc("TRN2", target_bir_lowering=False, num_devices=1)
    aps = {k: nc.dram_tensor(f"in_{k}", v.shape, mybir.dt.from_np(v.dtype), kind="ExternalInput").ap()
           for k, v in arrays.items()}
    out = nc.dram_tensor("out_cols", (P, KD, T), F32, kind="ExternalOutput").ap()
    build(nc, aps, out)
    r = run_bass_kernel_spmd(nc, [{f"in_{k}": v for k, v in arrays.items()}], core_ids=[0])
    got = np.asarray(r.results[0]["out_cols"])
    return np.ascontiguousarray(got.transpose(1, 0, 2).reshape(1, D, T).transpose(0, 2, 1))
```

```python
import math
from contextlib import ExitStack

import numpy as np
import concourse.bass as bass
from concourse import mybir

F32 = mybir.dt.float32
F32R = mybir.dt.float32r
I32 = mybir.dt.int32
U32 = mybir.dt.uint32
ALU = mybir.AluOpType
ACT = mybir.ActivationFunctionType
AX_X = mybir.AxisListType.X

P = 128
T = 512
D = 1024
KD = D // P
TB = T // P
EPS = 1e-6
NEG = -1e30
BLOCK = KD * P

CONV_TILES = 4
HEADS = 8
HEAD_DIM = 64
LRU_C = 8.0
TOPK = 16
N_KEYS = 128
GROUP = 8
N_GROUPS = N_KEYS // GROUP
AHEAD = 8
KEPT = AHEAD - 1
N_HOT = 4
FIRST_U = 8
PLACE_U = (16, 16, 15, 9)
TOK = 16
ROPE = 32
NOPE = 64
FFN_TILES = 22
ATT_SCALE_A = HEAD_DIM ** -0.5
ATT_SCALE_B = (NOPE + ROPE) ** -0.5

COLUMNS = [("b_ada", 48), ("norm1", 8), ("conv_a", 12), ("conv_b", 16), ("conv_bias", 4), ("b_r", 4),
           ("b_i", 4), ("lam", 4), ("gn", 8), ("norm2", 8), ("final", 8), ("norm_mix", 8), ("q_norm", 2),
           ("kv_norm", 1), ("b_gate", 16), ("norm_ffn", 8), ("norm_final", 8), ("b_forget", 1),
           ("inv_freq", 1), ("phase", 1), ("sign", 1), ("eps", 1)]
COLUMN_AT = {}
_at = 0
for _name, _n in COLUMNS:
    COLUMN_AT[_name] = _at
    _at += _n
N_COLUMNS = _at
CONSTS = [("ones", 128), ("head_pick", 2), ("ident", 128), ("iota", 128), ("causal", 128), ("chunk", 128),
          ("iota16", 16)]
CONST_AT = {}
_at = 0
for _name, _n in CONSTS:
    CONST_AT[_name] = (_at, _at + _n)
    _at += _n
N_CONSTS = _at


def two_pi_parts(scale, bits, n):
    rest, parts = 2 * math.pi * scale, []
    for _ in range(n):
        unit = 2.0 ** (math.floor(math.log2(rest)) + 1 - bits)
        part = math.floor(rest / unit) * unit
        parts.append(part)
        rest -= part
    return parts + [rest]


class Queue:

    def __init__(self, engine, sem):
        self.engine, self.sem, self.count, self.seen = engine, sem, 0, {}

    def after(self, *moments):
        for m in moments:
            if m is None:
                continue
            if isinstance(m, list):
                self.after(*m)
                continue
            sem, value = m
            if self.seen.get(sem.name, 0) < value:
                self.engine.wait_ge(sem, value)
                self.seen[sem.name] = value

    def mark(self, instruction):
        self.count += 1
        instruction.then_inc(self.sem, 1)
        return (self.sem, self.count)


class Landing:

    def __init__(self, sem):
        self.sem, self.count = sem, 0

    def mark(self, dma):
        self.count += 16
        dma.then_inc(self.sem, 16)
        return (self.sem, self.count)


class Banks:

    def __init__(self, tensors):
        self.tensors, self.free, self.at = tensors, [[] for _ in tensors], -1

    def take(self):
        self.at = (self.at + 1) % len(self.tensors)
        return self.at, self.tensors[self.at], self.free[self.at]


class WeightStream:

    RAW, SPLIT = 3, 3

    def __init__(self, nc, ctx, sp, act, dve, pool, plan):
        self.nc, self.sp, self.act, self.dve, self.pool, self.plan = nc, sp, act, dve, pool, plan
        self.raw = [ctx.enter_context(nc.sbuf_tensor(f"weights_raw{i}", [P, BLOCK], F32)) for i in range(self.RAW)]
        self.hi = [ctx.enter_context(nc.sbuf_tensor(f"weights_hi{i}", [P, BLOCK], F32R)) for i in range(self.SPLIT)]
        self.lo = [ctx.enter_context(nc.sbuf_tensor(f"weights_lo{i}", [P, BLOCK], F32R)) for i in range(self.SPLIT)]
        self.landing = [Landing(ctx.enter_context(nc.semaphore(f"weights_raw{i}"))) for i in range(self.RAW)]
        self.loaded, self.hi_done, self.lo_done, self.used = [], [], [], []
        self.on_pool = False

    def load(self):
        n = len(self.loaded)
        if n < len(self.plan):
            if n >= self.RAW:
                self.sp.after(self.hi_done[n - self.RAW], self.lo_done[n - self.RAW])
            src, slot = self.plan[n], n % self.RAW
            self.loaded.append(self.landing[slot].mark(
                self.nc.sync.dma_start(self.raw[slot][:, 0:src.shape[1]], src)))

    def parts(self, n):
        w = self.plan[n].shape[1]
        free = self.used[n - self.SPLIT] if n >= self.SPLIT else None
        assert n < self.SPLIT or free
        return self.raw[n % self.RAW][:, 0:w], self.hi[n % self.SPLIT][:, 0:w], self.lo[n % self.SPLIT][:, 0:w], free

    def split_hi(self):
        n = len(self.hi_done)
        if n < len(self.plan):
            raw, hi, _, free = self.parts(n)
            self.act.after(self.loaded[n], free)
            self.hi_done.append(self.act.mark(self.nc.scalar.activation(hi, raw, ACT.Copy)))

    def split_lo(self):
        n = len(self.lo_done)
        if n < len(self.plan):
            raw, hi, lo, free = self.parts(n)
            q, e = (self.pool, self.nc.gpsimd) if self.on_pool else (self.dve, self.nc.vector)
            q.after(self.hi_done[n], self.loaded[n], free)
            self.lo_done.append(q.mark(e.tensor_tensor(lo, raw, hi.bitcast(F32), ALU.subtract)))
            self.load()

    def next(self):
        n = len(self.used)
        while len(self.hi_done) < min(n + 3, len(self.plan)):
            self.split_hi()
        while len(self.lo_done) < min(n + 2, len(self.plan)):
            self.split_lo()
        self.used.append(None)
        return n, self.hi[n % self.SPLIT], self.lo[n % self.SPLIT], self.hi_done[n], self.lo_done[n]


def build(nc, a, out_cols):
    with ExitStack() as ctx:
        def sb(name, shape, dt=F32, scope=ctx):
            return scope.enter_context(nc.sbuf_tensor(name, shape, dt))

        def sem(name):
            return ctx.enter_context(nc.semaphore(name))

        V, S, G, M = nc.vector, nc.scalar, nc.gpsimd, nc.tensor
        pe, act, dve, pool, sp = (Queue(e, sem(f"{n}_marks")) for n, e in
                                  (("pe", M), ("act", S), ("dve", V), ("pool", G), ("sp", nc.sync)))
        banks = Banks([ctx.enter_context(nc.psum_tensor(f"bank{i}", [P, T], F32)) for i in range(7)])
        stat_bank = ctx.enter_context(nc.psum_tensor("bank_stat", [P, T], F32))
        stat_read = None

        def blocks(name, numbers):
            return [a[name][i] for i in numbers]

        LRU_FIRST = [i for c in range(4) for i in (12 + c, 16 + c)]
        CONV_THEN = [i for c in range(4) for i in (4 + c, 8 + c, c)]
        plan = blocks("w_in", LRU_FIRST + CONV_THEN) + blocks("w_out", range(KD)) + blocks("w_q", range(HEADS))
        plan += blocks("expert_u", range(AHEAD * GROUP))
        mix_order = list(range(KEPT, N_GROUPS)) + list(range(KEPT))
        for g in mix_order:
            if g >= KEPT and g + 1 < N_GROUPS:
                plan += blocks("expert_u", range((g + 1) * GROUP, (g + 2) * GROUP))
            plan += blocks("expert_v", range(g * KD, (g + 1) * KD))
        plan += blocks("w_small2", [0]) + blocks("w_latent2", range(3)) + blocks("w_qk2", range(8)) \
            + blocks("w_v2", range(4)) + blocks("w_q_up", range(2)) + blocks("w_kv_up", [0]) \
            + blocks("w_gates2", range(16))
        plan += blocks("w_branch_a", range(4)) + blocks("w_branch_b", range(4)) + blocks("w_out2", range(KD))
        for f in range(FFN_TILES):
            plan += blocks("w_ffn_gate", [f]) + blocks("w_ffn_up", [f])
        for m in range(KD):
            plan += [a["w_ffn_down"][m][:, c:min(c + BLOCK, FFN_TILES * P)] for c in range(0, FFN_TILES * P, BLOCK)]

        columns = sb("columns", [P, N_COLUMNS])
        consts = sb("consts", [P, N_CONSTS])
        x = sb("residual", [P, KD, T])
        ada = sb("ada", [P, 48])
        gain2 = sb("gain2", [P, KD])
        h_hi = sb("h_hi", [P, KD, T], F32R)
        h_lo = sb("h_lo", [P, KD, T], F32R)
        square = sb("square", [P, 2, T])
        scaled = sb("scaled", [P, 2, T])
        rms = sb("rms", [P, 96])
        gain_mix = sb("gain_mix", [P, KD])
        table = sb("rotation_table", [P, T])
        stream = WeightStream(nc, ctx, sp, act, dve, pool, plan)

        def const(name):
            lo, hi = CONST_AT[name]
            return consts[:, lo:hi]

        def col(name, i=0):
            c = COLUMN_AT[name] + i
            return columns[:, c:c + 1]

        def cols(name, n):
            return columns[:, COLUMN_AT[name]:COLUMN_AT[name] + n]

        small_landed = []

        def load_small():
            for name, dst in (("columns", columns), ("consts", consts)):
                small_landed.append(Landing(sem(f"{name}_landed")).mark(nc.sync.dma_start(dst[:], a[name])))

        def load_x(k):
            return Landing(sem(f"x{k}_landed")).mark(nc.sync.dma_start(x[:, k, :], a["x"][:, k, :]))

        def three(out, w_hi, w_lo, m_hi, m_lo, start, stop):
            M.matmul(out, w_hi, m_lo, start=start, stop=False)
            M.matmul(out, w_hi, m_hi, start=False, stop=False)
            return M.matmul(out, w_lo, m_hi, start=False, stop=stop)

        def tile_of(m, k):
            return m[k] if isinstance(m, list) else m[:, k, :]

        def block_product(bank, block, m_hi, m_lo, m_ready, tiles, start, stop):
            _, hi, lo, hi_ready, lo_ready = block
            pe.after(hi_ready)
            for n, (c, k) in enumerate(tiles):
                pe.after(m_ready[k])
                M.matmul(bank[:], hi[:, c:c + P], tile_of(m_lo, k), start=start and n == 0, stop=False)
                M.matmul(bank[:], hi[:, c:c + P], tile_of(m_hi, k), start=False, stop=False)
            pe.after(lo_ready)
            for n, (c, k) in enumerate(tiles):
                ins = M.matmul(bank[:], lo[:, c:c + P], tile_of(m_hi, k), start=False, stop=stop and n == len(tiles) - 1)
            return pe.mark(ins)

        def product(block, m_hi, m_lo, m_ready, nk=KD, at=0, last_use=True, order=None):
            b, bank, free = banks.take()
            pe.after(free)
            done = block_product(bank, block, m_hi, m_lo, m_ready, [(at + k * P, k) for k in order or range(nk)], True, True)
            if last_use:
                stream.used[block[0]] = done
            return b, bank, done

        def split_to(hi, lo, value, ready, hi_free=None):
            act.after(ready, hi_free)
            hi_done = act.mark(S.activation(hi, value, ACT.Copy))
            dve.after(ready, hi_done, hi_free)
            lo_done = dve.mark(V.tensor_tensor(lo, value, hi.bitcast(F32), ALU.subtract))
            return [hi_done, lo_done]

        square_free = [None, None]
        scaled_free = [None, None]

        def squared(src, n, ready):
            act.after(ready, square_free[n])
            return act.mark(S.activation(square[:, n, :], src, ACT.Square))

        def sum_features(tiles, at, ready, groups=None):
            n = 2 if groups else 1
            picked = const("head_pick") if groups else const("ones")[:, 0:1]
            pe.after(ready, stat_read)
            for tb in range(TB):
                for i, tile in enumerate(tiles):
                    ins = M.matmul(stat_bank[:, at + n * tb:at + n * tb + n], tile[:, tb * P:tb * P + P], picked,
                                   start=i == 0, stop=i == len(tiles) - 1)
            return pe.mark(ins)

        def invert_root(at, n, width, summed):
            nonlocal stat_read
            r = rms[:, at:at + n]
            act.after(summed)
            stat_read = act.mark(S.activation(r, stat_bank[:, at:at + n], ACT.Sqrt, bias=col("eps"), scale=1.0 / width))
            dve.after(stat_read)
            return dve.mark(V.reciprocal(r, r))

        def spread(at, ready, values=None):
            b, bank, free = banks.take()
            pe.after(free, ready)
            for tb in range(TB):
                r = rms[:, at + tb:at + tb + 1].broadcast_to([P, P]) if values is None else values[:, tb * P:tb * P + P]
                ins = M.matmul(bank[:, tb * P:tb * P + P], r, const("ident"), start=True, stop=True)
            return b, bank, pe.mark(ins)

        def load_sqrt():
            act.after(small_landed)
            act.mark(S.activation(rms[0:1, 95:96], col("eps")[0:1], ACT.Sqrt))

        class SquareSum:

            def __init__(self, gain=None):
                self.scales = [None] if gain is None else [None, gain]
                self.added = [None] * len(self.scales)
                self.last = []

            def add(self, k, ready):
                for s, scale in enumerate(self.scales):
                    n = k % 2 if len(self.scales) == 1 else s
                    first, last = k == 0, k == KD - 1
                    dst = scaled[:, s, :] if first else square[:, n, :]
                    act.after(ready, scaled_free[s] if first else square_free[n])
                    made = act.mark(S.activation(dst, x[:, k, :], ACT.Square, scale=1.0 if scale is None else col(scale, k)))
                    if first:
                        self.added[s] = made
                    elif not last:
                        pool.after(made, self.added[s])
                        self.added[s] = pool.mark(G.tensor_tensor(scaled[:, s, :], scaled[:, s, :], dst, ALU.add))
                        square_free[n] = self.added[s]
                    else:
                        self.last.append((s, n, [scaled[:, s, :], dst], [made, self.added[s]]))
                if k == KD - 2:
                    load_sqrt()

            def invert(self):
                for s, n, tiles, ready in self.last:
                    self.summed = scaled_free[s] = square_free[n] = sum_features(tiles, 4 * s, ready)
                return invert_root(0, TB, D, self.summed)

            def rstd(self):
                return spread(0, self.invert())

        def without_rstd(k, gain, free):
            act.after(x_done[k], free)
            hi_done = act.mark(S.activation(h_hi[:, k, :], x[:, k, :], ACT.Copy, scale=gain))
            dve.after(x_done[k], hi_done)
            return [hi_done, dve.mark(V.scalar_tensor_tensor(h_lo[:, k, :], x[:, k, :], gain, h_hi[:, k, :].bitcast(F32),
                                                             ALU.mult, ALU.subtract))]

        def kept(dst, rstd):
            b, bank, done = rstd
            act.after(done)
            m = act.mark(S.activation(dst, bank[:], ACT.Copy))
            banks.free[b] = [m]
            return m

        def temporary(k):
            buffer, free = ((scaled, scaled_free), (square, square_free))[k // 2 % 2]
            return buffer[:, k % 2, :], free, k % 2

        def normalise(k, src, gain, shift, hi, lo, ready, free, rstd, on_pool=False):
            b, bank, spread_done = rstd
            tmp, tmp_free, at = temporary(k)
            dve.after(ready, spread_done, tmp_free[at])
            tmp_done = dve.mark(V.scalar_tensor_tensor(tmp, src, gain, bank[:], ALU.mult, ALU.mult))
            banks.free[b] = [tmp_done]
            act.after(tmp_done, free)
            hi_done = act.mark(S.activation(hi, tmp, ACT.Identity, bias=0.0 if shift is None else shift))
            yield
            q, e = (pool, G) if on_pool and shift is None else (dve, V)
            q.after(tmp_done, hi_done, free)
            if shift is None:
                lo_done = q.mark(e.tensor_tensor(lo, tmp, hi.bitcast(F32), ALU.subtract))
            else:
                lo_done = dve.mark(V.scalar_tensor_tensor(lo, tmp, shift, hi.bitcast(F32), ALU.add, ALU.subtract))
            tmp_free[at] = lo_done
            yield [hi_done, lo_done]

        def normalise_all(tiles):
            ready, before = [], None
            for tile in tiles:
                next(tile)
                if before:
                    ready.append(next(before))
                before = tile
            return ready + [next(before)]

        def add_to_x(k, bank_no, bank, done, gate):
            dve.after(done)
            if gate is None:
                m = dve.mark(V.tensor_tensor(x[:, k, :], bank[:], x[:, k, :], ALU.add))
            else:
                m = dve.mark(V.scalar_tensor_tensor(x[:, k, :], bank[:], gate, x[:, k, :], ALU.mult, ALU.add))
            banks.free[bank_no] = [m]
            return m

        def chain(ins):
            m = dve.mark(ins)
            dve.after(m)
            return m

        def log1p_steps(dst, e, t1, t2, ready):
            dve.after(ready)
            yield chain(V.tensor_scalar(t1, e, 2.0, None, ALU.add))
            yield chain(V.reciprocal(t2, t1))
            yield chain(V.tensor_tensor(t1, e, t2, ALU.mult))
            yield chain(V.tensor_tensor(t2, t1, t1, ALU.mult))
            yield chain(V.tensor_scalar(dst, t2, 2.0 / 17, 2.0 / 15, ALU.mult, ALU.add))
            for n in (13, 11, 9, 7, 5, 3, 1):
                yield chain(V.tensor_tensor(dst, dst, t2, ALU.mult))
                yield chain(V.tensor_scalar(dst, dst, 2.0 / n, None, ALU.add))
            yield chain(V.tensor_tensor(dst, dst, t1, ALU.mult))

        mixer = ExitStack()

        def mb(name, shape, dt=F32):
            return sb(name, shape, dt, mixer)

        RING = 4
        c_act = mb("c_act", [P, D])
        y = mb("y", [P, 8, T])
        ada_raw = [mb(f"ada_raw{i}", [P, D])[:] for i in range(RING)] \
            + [y[:, 2 * i:2 * i + 2, :].rearrange("p k t -> p (k t)") for i in range(RING)]
        ada_scratch = mb("ada_scratch", [P, D])
        ada_sum = mb("ada_sum", [P, 48])
        ada_landing = [Landing(sem(f"ada_raw{i}")) for i in range(2 * RING)]
        ada_landed, ada_done = [], []
        ada_order = [j for k in range(KD) for j in (8 + k, k)] + list(range(16, 48))

        def ada_slot(j):
            return j % (2 * RING) if j < 16 else j % RING

        def load_ada():
            j = len(ada_landed)
            before = [i for i in range(j) if ada_slot(i) == ada_slot(j)]
            if j < 48 and (not before or before[-1] < len(ada_done)):
                sp.after(ada_done[before[-1]] if before else None)
                slot = ada_slot(j)
                ada_landed.append(ada_landing[slot].mark(nc.sync.dma_start(ada_raw[slot], a["w_ada"][ada_order[j]])))

        c_landed = Landing(sem("c_landed")).mark(nc.sync.dma_start(c_act[:], a["c_rows"]))
        x_landed = [load_x(k) for k in range(KD)]
        load_small()
        for _ in range(2 * RING):
            load_ada()
        act.after(c_landed)
        c_ready = act.mark(S.activation(c_act[:], c_act[:], ACT.Silu))

        def ada_tile_aside():
            j = len(ada_done)
            raw = ada_raw[ada_slot(j)]
            pool.after(c_ready, ada_landed[j])
            m = pool.mark(G.tensor_tensor(raw, raw, c_act[:], ALU.mult))
            act.after(m)
            ada_done.append(act.mark(S.activation(raw, raw, ACT.Copy,
                                                  accum_out=ada_sum[:, ada_order[j]:ada_order[j] + 1])))
            load_ada()

        def ada_tile():
            j = len(ada_done)
            dve.after(c_ready, ada_landed[j], ada_done[-1] if ada_done else None)
            ada_done.append(dve.mark(V.tensor_tensor_reduce(
                out=ada_scratch[:], in0=ada_raw[ada_slot(j)], in1=c_act[:], scale=1.0, scalar=0.0,
                op0=ALU.mult, op1=ALU.add, accum_out=ada_sum[:, ada_order[j]:ada_order[j] + 1])))
            load_ada()

        def ada_columns(lo, hi, plus=0.0):
            dve.after([ada_done[ada_order.index(j)] for j in range(lo, hi)], small_landed)
            return dve.mark(V.scalar_tensor_tensor(ada[:, lo:hi], ada_sum[:, lo:hi], plus,
                                                   columns[:, COLUMN_AT["b_ada"] + lo:COLUMN_AT["b_ada"] + hi],
                                                   ALU.add, ALU.add))

        x_sum = SquareSum()
        for k in range(KD):
            x_sum.add(k, x_landed[k] if k < KD - 1 else [x_landed[k], small_landed])
        gain = mb("gain", [P, KD])
        stream.on_pool = True
        made, h_ready = None, []
        for k in range(KD):
            ada_tile()
            ada_tile_aside()
            if k == 0:
                x_rstd = x_sum.rstd()
            if k == 4:
                stream.load()
            if k == 6:
                stream.load()
                stream.load()
            if k == KD - 1:
                stream.split_hi()
                stream.split_lo()
            shift1 = ada_columns(k, k + 1)
            scale1 = ada_columns(8 + k, 9 + k, 1.0)
            dve.after(scale1)
            gain1 = dve.mark(V.tensor_tensor(gain[:, k:k + 1], ada[:, 8 + k:9 + k], col("norm1", k), ALU.mult))
            tile = normalise(k, x[:, k, :], gain[:, k:k + 1], ada[:, k:k + 1], h_hi[:, k, :], h_lo[:, k, :],
                             [gain1, shift1], None, x_rstd)
            next(tile)
            if made:
                h_ready.append(next(made))
            made = tile
        h_ready.append(next(made))
        gain_mix_done = dve.mark(V.tensor_tensor(gain_mix[:], cols("final", 8), cols("norm_mix", 8), ALU.mult))

        lam_t = mb("lam_t", [P, 5, 4])
        dve.after(small_landed)
        m = dve.mark(V.tensor_scalar(lam_t[:, 0, :], cols("lam", 4), -1.0, None, ALU.mult))
        dve.after(m)
        m = dve.mark(V.tensor_tensor(lam_t[:, 1, :], lam_t[:, 0, :], cols("lam", 4), ALU.min))
        act.after(m)
        e_done = act.mark(S.activation(lam_t[:, 1, :], lam_t[:, 1, :], ACT.Exp))
        for _ in log1p_steps(lam_t[:, 2, :], lam_t[:, 1, :], lam_t[:, 3, :], lam_t[:, 4, :], e_done):
            pass
        m = dve.mark(V.scalar_tensor_tensor(lam_t[:, 2, :], lam_t[:, 0, :], 0.0, lam_t[:, 2, :], ALU.max, ALU.add))
        decay, minus_decay = lam_t[:, 3, :], lam_t[:, 4, :]
        dve.after(m)
        dve.mark(V.tensor_scalar(decay, lam_t[:, 2, :], LRU_C, None, ALU.mult))
        decay_done = dve.mark(V.tensor_scalar(minus_decay, lam_t[:, 2, :], -LRU_C, None, ALU.mult))

        gate_w = mb("lru_gate_w", [P, 2, 4, P])
        gate_w_landed = Landing(sem("gate_w_landed")).mark(nc.sync.dma_start(gate_w[:], a["w_lru_gates"]))
        padded = mb("padded", [P, 2, T + 3])
        pad_done = pool.mark(G.memset(padded[:, :, 0:3], 0.0))
        xc = mb("lru_x", [P, 4, T])
        r_gate = mb("r_gate", [P, 4, T])
        i_gate = mb("i_gate", [P, 4, T])
        u_fac = mb("u_fac", [P, 4, T])
        padded_free = [None, None]
        gelu_done, r_done, i_done, xc_done = [], [], [], []
        for c in range(4):
            b, bank, done = product(stream.next(), h_hi, h_lo, h_ready)
            act.after(done, pad_done, padded_free[c % 2])
            m = act.mark(S.activation(padded[:, c % 2, 3:T + 3], bank[:], ACT.Copy))
            banks.free[b] = [m]
            b, bank, done = product(stream.next(), h_hi, h_lo, h_ready)
            act.after(done)
            m2 = act.mark(S.activation(y[:, 4 + c, :], bank[:], ACT.Gelu_apprx_tanh))
            banks.free[b] = [m2]
            gelu_done.append(m2)
            dve.after(m, small_landed)
            m = dve.mark(V.tensor_scalar(xc[:, c, :], padded[:, c % 2, 0:T], col("conv_b", c), col("conv_bias", c),
                                         ALU.mult, ALU.add))
            for j in range(1, 4):
                dve.after(m)
                m = dve.mark(V.scalar_tensor_tensor(xc[:, c, :], padded[:, c % 2, j:j + T], col("conv_b", 4 * j + c),
                                                    xc[:, c, :], ALU.mult, ALU.add))
            padded_free[c % 2] = m
            xc_done.append(m)
            for _ in range(3):
                ada_tile()
        for c in range(4):
            for g, (dst, bias, made) in enumerate(((r_gate, "b_r", r_done), (i_gate, "b_i", i_done))):
                b, bank, free = banks.take()
                pe.after(free, xc_done[c], gate_w_landed)
                done = pe.mark(M.matmul(bank[:], gate_w[:, g, c, :], xc[:, c, :], start=True, stop=True))
                act.after(done)
                made.append(act.mark(S.activation(dst[:, c, :], bank[:], ACT.Sigmoid, bias=col(bias, c))))
                banks.free[b] = [made[-1]]

        conv_pad = mb("conv_pad", [P, 2, T + 2])
        gate_c = mb("gate_c", [P, 2, T])
        conv_pad_zero = pool.mark(G.memset(conv_pad[:, :, 0:2], 0.0))
        conv_free, gate_c_free = [None, None], [None, None]
        y_done = [None] * 8

        def conv_tile(c, after_first=None, after_second=None):
            b, bank, done = product(stream.next(), h_hi, h_lo, h_ready)
            act.after(done, gate_c_free[c % 2])
            gc_done = act.mark(S.activation(gate_c[:, c % 2, :], bank[:], ACT.Copy))
            banks.free[b] = [gc_done]
            ada_tile()
            if after_first:
                after_first()
            b, bank, done = product(stream.next(), h_hi, h_lo, h_ready)
            dve.after(done, gc_done, conv_pad_zero, conv_free[c % 2])
            m = dve.mark(V.tensor_tensor(conv_pad[:, c % 2, 2:T + 2], bank[:], gate_c[:, c % 2, :], ALU.mult))
            gate_c_free[c % 2] = m
            banks.free[b] = [m]
            dve.after(m, small_landed)
            m = dve.mark(V.tensor_scalar(y[:, c, :], conv_pad[:, c % 2, 0:T], col("conv_a", c), None, ALU.mult))
            for j in range(1, 3):
                dve.after(m)
                m = dve.mark(V.scalar_tensor_tensor(y[:, c, :], conv_pad[:, c % 2, j:j + T], col("conv_a", 4 * j + c),
                                                    y[:, c, :], ALU.mult, ALU.add))
            conv_free[c % 2] = m
            ada_tile()
            if after_second:
                after_second()
            b, bank, done = product(stream.next(), h_hi, h_lo, h_ready)
            dve.after(done, m)
            y_done[c] = dve.mark(V.tensor_tensor(y[:, c, :], bank[:], y[:, c, :], ALU.mult))
            banks.free[b] = [y_done[c]]
            ada_tile()

        conv_tile(0)
        u_done, a_done = [], []
        for c in range(4):
            act.after(r_done[c], decay_done)
            u_done.append(act.mark(S.activation(u_fac[:, c, :], r_gate[:, c, :], ACT.Tanh, scale=decay[:, c:c + 1])))
            act.after(u_done[-1])
            a_done.append(act.mark(S.activation(r_gate[:, c, :], r_gate[:, c, :], ACT.Exp, scale=minus_decay[:, c:c + 1])))
        a_square = mb("a_square", [P, T])

        def lru_factor(c, before):
            dve.after(a_done[c], before)
            m = dve.mark(V.tensor_tensor(a_square[:], r_gate[:, c, :], r_gate[:, c, :], ALU.mult))
            dve.after(m, u_done[c])
            m = dve.mark(V.scalar_tensor_tensor(u_fac[:, c, :], a_square[:], 1.0, u_fac[:, c, :], ALU.add, ALU.mult))
            dve.after(i_done[c])
            m2 = dve.mark(V.tensor_tensor(i_gate[:, c, :], i_gate[:, c, :], xc[:, c, :], ALU.mult))
            return m, m2

        def lru_output(c):
            dve.after(root_done[c], f[c][1])
            m = dve.mark(V.tensor_tensor(i_gate[:, c, :], i_gate[:, c, :], u_fac[:, c, :], ALU.mult))
            dve.after(m, a_done[c])
            m = dve.mark(V.tensor_tensor_scan(xc[:, c, :], r_gate[:, c, :], i_gate[:, c, :], 0.0, ALU.mult, ALU.add))
            dve.after(m, gelu_done[c])
            y_done[4 + c] = dve.mark(V.tensor_tensor(y[:, 4 + c, :], y[:, 4 + c, :], xc[:, c, :], ALU.mult))

        lru_hi = mb("lru_hi", [P, 4, T], F32R)
        lru_lo = mb("lru_lo", [P, 4, T], F32R)
        y_hi = [h_hi[:, c, :] for c in range(4)] + [lru_hi[:, c, :] for c in range(4)]
        y_lo = [h_lo[:, c, :] for c in range(4)] + [lru_lo[:, c, :] for c in range(4)]
        y_ready = [None] * 8
        HEAD_SUMS = 16

        def head_sums(tiles):
            for c in tiles:
                squares = squared(y[:, c, :], c % 2, y_done[c])
                summed = square_free[c % 2] = sum_features([square[:, c % 2, :]], HEAD_SUMS + 8 * c, squares, groups=True)
            return invert_root(HEAD_SUMS + 8 * tiles[0], 8 * len(tiles), HEAD_DIM, summed)

        expanded = [a_square, mb("expanded", [P, T])]
        expanded_free = [None, None]

        def norm_heads(tiles, inverted, free):
            rstds = []
            for c in tiles:
                at = HEAD_SUMS + 8 * c
                act.after(inverted, expanded_free[c % 2])
                values = act.mark(S.activation(expanded[c % 2][:].rearrange("p (n d) -> p n d", d=HEAD_DIM),
                                               rms[:, at:at + 8].unsqueeze(2).broadcast_to([P, 8, HEAD_DIM]), ACT.Copy))
                rstds.append(spread(0, values, expanded[c % 2]))
                expanded_free[c % 2] = rstds[-1][2]
            y_ready[tiles[0]:tiles[-1] + 1] = normalise_all(
                [normalise(c, y[:, c, :], col("gn", c), None, y_hi[c], y_lo[c], y_done[c], free, rstd, on_pool=c % 2 == 1)
                 for c, rstd in zip(tiles, rstds)])

        f = [None] * 4
        f[0] = lru_factor(0, None)
        f[1] = lru_factor(1, f[0][0])
        conv_tile(1)
        f[2] = lru_factor(2, f[1][0])
        f[3] = lru_factor(3, f[2][0])
        root_done = []
        for c in range(4):
            act.after(f[c][0])
            root_done.append(act.mark(S.activation(u_fac[:, c, :], u_fac[:, c, :], ACT.Sqrt)))
        for c in range(4):
            lru_output(c)
        conv_tile(2)
        lru_inverted = head_sums([4, 5, 6, 7])
        conv_inverted = []
        conv_tile(3, lambda: norm_heads([4, 5, 6, 7], lru_inverted, None), lambda: conv_inverted.append(head_sums([0, 1, 2])))
        projected = (pe.sem, pe.count)
        norm_heads([0, 1, 2], conv_inverted[0], projected)
        norm_heads([3], head_sums([3]), projected)
        late = ada_columns(16, 24)

        x_done = [None] * KD
        x_sum = SquareSum()
        for k in range(KD):
            b, bank, done = product(stream.next(), y_hi, y_lo, y_ready, order=[4, 5, 6, 7, 0, 1, 2, 3])
            dve.after(late)
            x_done[k] = add_to_x(k, b, bank, done, ada[:, 16 + k:17 + k])
            x_sum.add(k, x_done[k])
            for _ in range(2 if k == 0 else 1):
                if len(ada_done) < 48:
                    ada_tile()
            if k == KD - 2:
                shift2 = ada_columns(24, 32)
                scale2 = ada_columns(32, 40, 1.0)
                g2_done = ada_columns(40, 48)
                dve.after(scale2)
                gain2_done = dve.mark(V.tensor_tensor(gain2[:], ada[:, 32:40], cols("norm2", 8), ALU.mult))
        assert len(ada_done) == 48
        x_rstd = x_sum.rstd()
        h_free = done
        mixer.close()
        mixer_over = [done, (act.sem, act.count), (dve.sem, dve.count), (pool.sem, pool.count)]

        h_ready = normalise_all([normalise(k, x[:, k, :], gain2[:, k:k + 1], ada[:, 24 + k:25 + k], h_hi[:, k, :], h_lo[:, k, :],
                             [shift2, gain2_done], h_free, x_rstd) for k in range(KD)])
        peer = ExitStack()

        def pb(name, shape, dt=F32, scope=peer):
            return sb(name, shape, dt, scope)

        hidden = [pb(f"hidden{i}", [P, GROUP, T]) for i in range(2)]
        route = ExitStack()

        def rb(name, shape, dt=F32):
            return sb(name, shape, dt, route)

        top_s = rb("top_s", [P, HEADS, 2, TOPK])
        top_i = rb("top_i", [P, HEADS, 2, TOPK], U32)
        top_f = top_s
        sums = rb("sums", [P, 4, TOPK, TOPK])
        best = rb("best", [P, HEADS, TOPK])
        best_at = rb("best_at", [P, HEADS, TOPK], U32)
        half_at = rb("half_at", [P, 2, HEADS, TOPK], U32)
        half_f = rb("half_f", [P, 2, HEADS, TOPK])
        chosen = rb("chosen", [P, 3, HEADS * TOPK])
        total = rb("total", [P, 2, HEADS])
        equal = sums
        chosen_t = [rb(f"chosen_t{i}", [P, 3, P]) for i in range(2)]
        one_hot = [rb(f"one_hot{i}", [P, 2, 4, P]) for i in range(N_HOT)]
        stage = [rb(f"stage{i}", [P, N_GROUPS, GROUP, TOK]) for i in range(2)]
        stage_sem = [Landing(sem(f"stage{i}_stored")) for i in range(2)]
        hidden_store = nc.dram_tensor("hidden_store", [KEPT, P, GROUP, T], F32, kind="Internal")
        coefs = nc.dram_tensor("expert_coefs", [N_GROUPS, P, T // TOK, GROUP, TOK], F32, kind="Internal")
        scores = rb("scores", [P, TB, HEADS, 2, N_KEYS])
        q_tile = scaled
        keys = stage[1][:].rearrange("p g j t -> p (g j t)")[:, 0:HEADS * N_KEYS].rearrange("p (h n) -> p h n", h=HEADS)
        sp.after(mixer_over)
        keys_landed = Landing(sem("keys_landed")).mark(nc.sync.dma_start(keys, a["keys"]))
        act.after(mixer_over)
        dve.after(mixer_over)
        pool.after(mixer_over)

        q_free = list(scaled_free)
        q_done, score_done = [None] * HEADS, []

        def query(h):
            b, bank, done = product(stream.next(), h_hi, h_lo, h_ready)
            act.after(done, q_free[h % 2])
            q_done[h] = act.mark(S.activation(q_tile[:, h % 2, :], bank[:], ACT.Copy))
            banks.free[b] = [q_done[h]]

        def key_scores(h):
            for c in range(2):
                b, bank, free = banks.take()
                pe.after(free, q_done[h], keys_landed)
                for tb in range(TB):
                    ins = M.matmul(bank[:, tb * N_KEYS:(tb + 1) * N_KEYS],
                                   q_tile[64 * c:64 * c + 64, h % 2, tb * P:(tb + 1) * P],
                                   keys[64 * c:64 * c + 64, h, :], start=True, stop=True)
                done = pe.mark(ins)
                act.after(done)
                m = act.mark(S.activation(scores[:, :, h, c, :], bank[:].rearrange("p (t n) -> p t n", t=TB), ACT.Copy))
                banks.free[b] = [m]
                score_done.append(m)
            q_free[h % 2] = scaled_free[h % 2] = done


        chosen_free, chosen_t_free = None, [None, None]

        def lockstep(*chains):
            last = [None] * len(chains)
            for steps in zip(*chains):
                for n, step in enumerate(steps):
                    dve.after(last[n])
                    last[n] = dve.mark(step())
            return last

        def top16(src, value, at, removed):
            return [lambda: V.max(value[:, 0:8], src),
                    lambda: V.max_index(at[:, 0:8], value[:, 0:8], src),
                    lambda: V.match_replace(src, value[:, 0:8], src, removed),
                    lambda: V.max(value[:, 8:16], src),
                    lambda: V.max_index(at[:, 8:16], value[:, 8:16], src)]

        def sums_of(dst, h):
            return lambda: V.tensor_tensor(dst, top_s[:, h, 0, :].unsqueeze(2).broadcast_to([P, TOPK, TOPK]),
                                           top_s[:, h, 1, :].unsqueeze(1).broadcast_to([P, TOPK, TOPK]), ALU.add)

        routed = {}

        def route_tokens(tb):
            for h in range(HEADS):
                dve.after(score_done[2 * h], score_done[2 * h + 1])
                last = lockstep(*[top16(scores[:, tb, h, c, :], top_s[:, h, c, :], top_i[:, h, c, :], NEG)
                                  for c in range(2)])
                yield
            dve.after(last)
            for h in range(0, HEADS, 2):
                last = lockstep(*[[sums_of(sums[:, n], h + n)] +
                                  top16(sums[:, n].rearrange("p a b -> p (a b)"), best[:, h + n, :], best_at[:, h + n, :],
                                        2 * NEG) for n in range(2)])
                dve.after(last)
                yield
            chain(V.tensor_scalar(half_at[:, 0], best_at[:], 4, None, ALU.logical_shift_right))
            chain(V.tensor_scalar(half_at[:, 1], best_at[:], TOPK - 1, None, ALU.bitwise_and))
            chain(V.tensor_copy(half_f[:], half_at[:]))
            chain(V.tensor_copy(top_f[:], top_i[:]))
            dve.after(chosen_free)
            for c in range(2):
                for q in range(2):
                    hs = slice(4 * q, 4 * q + 4)
                    chain(V.tensor_tensor(equal[:].rearrange("p h a b -> p (h a) b"),
                                          half_f[:, c, hs, :].rearrange("p h s -> p (h s)").unsqueeze(2)
                                          .broadcast_to([P, 4 * TOPK, TOPK]),
                                          const("iota16").unsqueeze(1).broadcast_to([P, 4 * TOPK, TOPK]), ALU.is_equal))
                    chain(V.tensor_tensor(equal[:], equal[:], top_f[:, 4 * q:4 * q + 4, c, :].unsqueeze(2)
                                          .broadcast_to([P, 4, TOPK, TOPK]), ALU.mult))
                    chain(V.tensor_reduce(chosen[:, c, 64 * q:64 * q + 64],
                                          equal[:].rearrange("p h a b -> p (h a) b"), AX_X, ALU.add))
                    yield
            w = chosen[:, 2, :].rearrange("p (h s) -> p h s", h=HEADS)
            m = chain(V.tensor_tensor(w, best[:], best[:, :, 0:1].broadcast_to([P, HEADS, TOPK]), ALU.subtract))
            act.after(m)
            m = act.mark(S.activation(w, w, ACT.Exp))
            yield
            dve.after(m)
            chain(V.tensor_reduce(total[:, 0, :], w, AX_X, ALU.add))
            chain(V.reciprocal(total[:, 1, :], total[:, 0, :]))
            routed[tb] = chain(V.tensor_tensor(w, w, total[:, 1, :].unsqueeze(2).broadcast_to([P, HEADS, TOPK]), ALU.mult))
            yield

        stage_free = [None, None]
        hot_free = [None] * N_HOT
        turned = {}

        def turn_chosen(tb):
            nonlocal chosen_free
            b, bank, free = banks.take()
            pe.after(free, routed[tb])
            for n in range(3):
                ins = M.transpose(bank[:, n * P:(n + 1) * P], chosen[:, n, :], const("ident"))
            chosen_free = pe.mark(ins)
            act.after(chosen_free, chosen_t_free[tb % 2])
            turned[tb] = act.mark(S.activation(chosen_t[tb % 2][:].rearrange("p n t -> p (n t)"), bank[:, 0:3 * P], ACT.Copy))
            banks.free[b] = [turned[tb]]

        def place_tokens(tb, quad):
            k = quad % N_HOT
            placed = chosen_t[tb % 2]
            hot = one_hot[k]
            t0 = 4 * quad
            iota = const("iota").unsqueeze(1).broadcast_to([P, 4, P])
            dve.after(turned[tb], hot_free[k])
            dve.mark(V.tensor_tensor(hot[:, 0], placed[:, 0, t0:t0 + 4].unsqueeze(2).broadcast_to([P, 4, P]),
                                     iota, ALU.is_equal))
            for t in range(4):
                m = dve.mark(V.tensor_scalar(hot[:, 1, t, :], const("iota"), placed[:, 1, t0 + t:t0 + t + 1],
                                             placed[:, 2, t0 + t:t0 + t + 1], ALU.is_equal, ALU.mult))
            chosen_t_free[tb % 2] = m
            b, bank, free = banks.take()
            pe.after(free, m)
            for t in range(4):
                ins = M.matmul(bank[:, t * P:(t + 1) * P], hot[:, 0, t, :], hot[:, 1, t, :], start=True, stop=True)
            done = pe.mark(ins)
            hot_free[k] = done
            at = (t0 % TOK)
            s = ((tb * P + t0) // TOK)
            st = stage[s % 2]
            act.after(done, stage_free[s % 2] if at == 0 else None)
            e_done = act.mark(S.activation(st[:, :, :, at:at + 4].rearrange("p g j t -> p (g j) t"),
                                           bank[:].rearrange("p (t n) -> p n t", t=4), ACT.Copy))
            banks.free[b] = [e_done]
            if at == TOK - 4:
                sp.after(e_done)
                stage_free[s % 2] = stage_sem[s % 2].mark(nc.sync.dma_start(
                    coefs[:, :, s, :, :].rearrange("g p j t -> p g (j t)"),
                    st[:].rearrange("p g j t -> p g (j t)")))

        hidden_done = {}
        hidden_free = [None, None]
        HALF = GROUP // 2
        hidden_stored = [Landing(sem(f"hidden{i}_stored")) for i in range(2)]
        hidden_saved = {}

        def save_hidden(j):
            g, n = divmod(j - HALF, GROUP)
            if j % HALF == 0 and 0 <= g < KEPT:
                sp.after(hidden_done[j - 1])
                hidden_saved[g] = hidden_stored[g % 2].mark(nc.sync.dma_start(
                    hidden_store[g, :, n:n + HALF, :], hidden[g % 2][:, n:n + HALF, :]))
                hidden_free[g % 2] = hidden_saved[g]

        def hidden_block(j):
            g, n = divmod(j, GROUP)
            b, bank, done = product(stream.next(), h_hi, h_lo, h_ready)
            save_hidden(j)
            act.after(done, hidden_free[g % 2])
            hidden_done[j] = act.mark(S.activation(hidden[g % 2][:, n, :], bank[:], ACT.Gelu))
            banks.free[b] = [hidden_done[j]]

        router = route_tokens(0)
        for h in range(HEADS + 1):
            if h < HEADS:
                query(h)
            if h:
                key_scores(h - 1)
                next(router)
        stage_free[1] = (pe.sem, pe.count)

        n_u = AHEAD * GROUP
        for _ in router:
            if len(hidden_done) < FIRST_U:
                hidden_block(len(hidden_done))
        turn_chosen(0)
        for tb in range(TB):
            router = route_tokens(tb + 1) if tb + 1 < TB else iter(())
            first = len(hidden_done)
            share = PLACE_U[tb]
            quads = P // 4
            for n in range(share):
                next(router, None)
                for quad in range(quads * n // share, quads * (n + 1) // share):
                    place_tokens(tb, quad)
                if n % 2 and n > 1:
                    next(router, None)
                if n == share - 1:
                    for _ in router:
                        pass
                if n == share - 1 and tb + 1 < TB:
                    turn_chosen(tb + 1)
                hidden_block(first + n)
        save_hidden(n_u)
        route_over = [(act.sem, act.count), (dve.sem, dve.count), (pool.sem, pool.count), (pe.sem, pe.count)] + stage_free
        route.close()
        stream.on_pool = False
        act.after(route_over)
        dve.after(route_over)

        weight = [pb(f"weight{i}", [P, T // TOK, GROUP, TOK]) for i in range(2)]
        weight_landing = [Landing(sem(f"weight{i}_landed")) for i in range(2)]
        mixed_hi = pb("mixed_hi", [P, GROUP, T], F32R)
        mixed_lo = pb("mixed_lo", [P, GROUP, T], F32R)
        weight_landed, weight_used = {}, {}

        mixed = [(mixed_hi, mixed_lo), (h_hi, h_lo)]
        mixed_free = [None, None]
        mixed_ready = {}
        pairs = {}
        for i, g in enumerate(mix_order):
            last_u = N_GROUPS - 1 - KEPT
            pairs[g] = (i - last_u + 1) % 2 if i >= last_u else 0
        late_lo = None

        def finish_mix():
            nonlocal late_lo
            if late_lo:
                g, n, hi_done = late_lo
                hi, lo = mixed[pairs[g]]
                dve.after(hi_done)
                lo_done = dve.mark(V.tensor_tensor(lo[:, n, :], hidden[g % 2][:, n, :], hi[:, n, :].bitcast(F32), ALU.subtract))
                mixed_ready[g].append([hi_done, lo_done])
                late_lo = None

        def mix_tile(i, n):
            nonlocal late_lo
            if i >= len(mix_order):
                return
            g = mix_order[i]
            pair = pairs[g]
            hi, lo = mixed[pair]
            v = hidden[g % 2][:, n, :]
            ready = hidden_done[g * GROUP + n] if g >= KEPT else hidden_loaded[g]
            dve.after(ready, weight_landed[g])
            m = dve.mark(V.tensor_tensor(v.rearrange("p (s t) -> p s t", t=TOK), v.rearrange("p (s t) -> p s t", t=TOK),
                                         weight[g % 2][:, :, n, :], ALU.mult))
            act.after(m, mixed_free[pair])
            dve.after(mixed_free[pair])
            hi_done = act.mark(S.activation(hi[:, n, :], v, ACT.Copy))
            finish_mix()
            mixed_ready.setdefault(g, [])
            late_lo = (g, n, hi_done)
            if n == GROUP - 1:
                finish_mix()
                weight_used[g] = m
                hidden_free[g % 2] = mixed_ready[g][-1]
                if i + 2 < len(mix_order):
                    load_group(mix_order[i + 2])

        hidden_landing = [Landing(sem(f"hidden{i}_landed")) for i in range(2)]
        hidden_loaded = {}

        def load_group(g):
            pool.after(route_over, weight_used.get((g - 2) % N_GROUPS))
            weight_landed[g] = weight_landing[g % 2].mark(G.dma_start(
                weight[g % 2][:].rearrange("p s j t -> p (s j t)"), coefs[g].rearrange("p s j t -> p (s j t)")))
            if g < KEPT:
                pool.after(hidden_saved[g], hidden_free[g % 2])
                hidden_loaded[g] = hidden_landing[g % 2].mark(G.dma_start(hidden[g % 2][:], hidden_store[g]))

        position = pb("position", [P, T], I32)
        turns = pb("turns", [P, T])

        def make_table():
            pool.after(route_over)
            position_landed = Landing(sem("position_landed")).mark(G.dma_start(position[:], a["positions"]))
            dve.after(position_landed)
            yield chain(V.tensor_copy(table[:], position[:]))
            yield chain(V.tensor_scalar(table[:], table[:], col("inv_freq"), None, ALU.mult))
            ROUND = 1.5 * 2.0 ** 23
            for scale, parts in ((256.0, two_pi_parts(256.0, 10, 5)), (1.0, two_pi_parts(1.0, 14, 2))):
                yield chain(V.tensor_scalar(turns[:], table[:], 1.0 / (2 * math.pi * scale), ROUND, ALU.mult, ALU.add))
                yield chain(V.tensor_scalar(turns[:], turns[:], -ROUND, None, ALU.add))
                for part in parts:
                    yield chain(V.scalar_tensor_tensor(table[:], turns[:], -part, table[:], ALU.mult, ALU.add))
            yield chain(V.tensor_scalar(table[:], table[:], col("phase"), None, ALU.add))
            yield chain(V.tensor_scalar(turns[:], table[:], math.pi, -2 * math.pi, ALU.is_gt, ALU.mult))
            yield chain(V.tensor_tensor(table[:], table[:], turns[:], ALU.add))
            m = chain(V.tensor_scalar(table[:], table[:], 3.1415925, -3.1415925, ALU.min, ALU.max))
            act.after(m)
            m = act.mark(S.activation(table[:], table[:], ACT.Sin))
            yield
            dve.after(m)
            chain(V.tensor_scalar(table[:], table[:], col("sign"), None, ALU.mult))

        load_group(mix_order[0])
        load_group(mix_order[1])
        table_steps = make_table()
        x_sum = SquareSum("final")
        for i, g in enumerate(mix_order):
            beside_u = KEPT <= g < N_GROUPS - 1
            if beside_u:
                for n in range(GROUP):
                    mix_tile(i, n)
                    hidden_block((g + 1) * GROUP + n)
                mixed_free[1] = (pe.sem, pe.count)
            for k in range(KD):
                b, bank, done = product(stream.next(), *mixed[pairs[g]], mixed_ready[g], nk=GROUP)
                if not (KEPT <= g < N_GROUPS - 2):
                    mix_tile(i + 1, k)
                dve.after(g2_done)
                x_done[k] = add_to_x(k, b, bank, done, ada[:, 40 + k:41 + k])
                if i >= len(mix_order) - KEPT:
                    next(table_steps, None)
                if i == len(mix_order) - 1:
                    assert pairs[g] == 0
                    h_ready[k] = without_rstd(k, gain_mix[:, k:k + 1], [gain_mix_done, mixed_free[1]])
                    x_sum.add(k, x_done[k])
            mixed_free[pairs[g]] = done
        peer.close()
        peer_over = [(act.sem, act.count), (dve.sem, dve.count), (pe.sem, pe.count)]

        def final_x():
            for k in range(KD):
                dve.after(final_kept, h_ready[k])
                x_done[k] = dve.mark(V.scalar_tensor_tensor(x[:, k, :], x[:, k, :], col("final", k), final_rstd, ALU.mult,
                                                            ALU.mult))
                yield

        stream.on_pool = True
        att = ExitStack()

        def ab(name, shape, dt=F32):
            return sb(name, shape, dt, att)

        act.after(peer_over)
        dve.after(peer_over)
        pool.after(peer_over)
        sp.after(peer_over)
        gates = ab("gates", [P, 16, T])
        h_scale = ab("h_scale", [P, T])
        heads = ExitStack()

        def hb(name, shape, dt=F32):
            return sb(name, shape, dt, heads)

        q_a = hb("q_a", [P, 4, T])
        k_a = hb("k_a", [P, 4, T])
        v_a = hb("v_a", [P, TB, 512])
        v_b = hb("v_b", [P, TB, 512])
        q_b = hb("q_b", [P, 4, T])
        k_b = hb("k_b", [P, 4, T])
        q_rot = hb("q_rot", [P, 2, T])
        k_rot = hb("k_rot", [P, T])
        key_bias = hb("key_bias", [HEADS, T])
        latent = gates[:, 13:16, :]
        forget = gates[0:HEADS, 8:13, :]
        final_rstd = gates[:, 7, :]
        early = ExitStack()
        latent_hi = sb("latent_hi", [P, 3, T], F32R, early)
        latent_lo = sb("latent_lo", [P, 3, T], F32R, early)
        rotated = sb("rotated", [P, 2, T], F32, early)

        def rotate(dsts, bank, ready):
            dve.after(ready, (dve.sem, dve.count))
            m1 = dve.mark(V.tensor_tensor(rotated[64:96, 0, :], bank[64:96, :], table[64:96, :], ALU.mult))
            dve.after(m1)
            m = dve.mark(V.tensor_tensor(rotated[64:96, 1, :], bank[96:128, :], table[96:128, :], ALU.mult))
            dve.after(m)
            for dst in dsts:
                m2 = dve.mark(V.tensor_tensor(dst, rotated[64:96, 0, :], rotated[64:96, 1, :], ALU.add))
            return m, m2

        small_product = product(stream.next(), h_hi, h_lo, h_ready)
        latent_products = [product(stream.next(), h_hi, h_lo, h_ready)]
        r_x, r_new, r_both = rms[:, 0:4], rms[:, 4:8], rms[:, 8:12]
        x_inverted = x_sum.invert()
        dve.after(x_inverted)
        chain(V.tensor_tensor(r_both, r_x, r_x, ALU.mult))
        m = chain(V.tensor_tensor(r_new, stat_bank[:, 4:8], r_both, ALU.mult))
        act.after(m)
        stat_read = act.mark(S.activation(r_new, r_new, ACT.Sqrt, bias=col("eps"), scale=1.0 / D))
        dve.after(stat_read)
        chain(V.reciprocal(r_new, r_new))
        both = chain(V.tensor_tensor(r_both, r_new, r_x, ALU.mult))
        latent_products.append(product(stream.next(), h_hi, h_lo, h_ready))
        scale_kept = kept(h_scale[:], spread(8, both))
        final_kept = kept(final_rstd, spread(0, x_inverted))
        latent_products.append(product(stream.next(), h_hi, h_lo, h_ready))
        x_steps = final_x()

        def scaled_product(dst, b, bank, done):
            dve.after(done, scale_kept)
            m = dve.mark(V.tensor_tensor(dst, bank[:], h_scale[:], ALU.mult))
            banks.free[b] = [m]
            return m

        lat = [scaled_product(latent[:, n, :], *latent_products[n]) for n in range(3)]
        small = gates[:, 6, :]
        done = scaled_product(small, *small_product)
        dve.after(done)
        chain(V.tensor_scalar(forget[:, 0, :], small[0:8], columns[0:8, COLUMN_AT["b_forget"]:COLUMN_AT["b_forget"] + 1],
                              None, ALU.add))
        _, k_rot_done = rotate([k_rot[32 * n:32 * n + 32, :] for n in range(4)], small, done)

        def forget_steps():
            yield chain(V.tensor_scalar(forget[:, 1, :], forget[:, 0, :], -1.0, None, ALU.mult))
            m = chain(V.tensor_tensor(forget[:, 1, :], forget[:, 1, :], forget[:, 0, :], ALU.min))
            act.after(m)
            m = act.mark(S.activation(forget[:, 1, :], forget[:, 1, :], ACT.Exp))
            yield
            yield from log1p_steps(forget[:, 2, :], forget[:, 1, :], forget[:, 3, :], forget[:, 4, :], m)
            yield chain(V.scalar_tensor_tensor(forget[:, 1, :], forget[:, 0, :], 0.0, forget[:, 2, :], ALU.min, ALU.subtract))
            chain(V.memset(forget[:, 2, :], 1.0))
            yield chain(V.tensor_tensor_scan(forget[:, 3, :], forget[:, 2, :], forget[:, 1, :], 0.0, ALU.mult, ALU.add))
            yield chain(V.tensor_scalar(key_bias[:], forget[:, 3, :], -1.0 / ATT_SCALE_A, None, ALU.mult))

        def latent_sums():
            squares = [squared(latent[:, n, :], n, lat[n]) for n in range(2)]
            square_free[0] = square_free[1] = sum_features([square[:, 0, :], square[:, 1, :]], 0, squares)
            q_inverted = invert_root(0, TB, 2 * P, square_free[0])
            squares = squared(latent[:, 2, :], 0, lat[2])
            square_free[0] = sum_features([square[:, 0, :]], 4, squares)
            return q_inverted, invert_root(4, TB, P, square_free[0])

        def latent_norms(q_inverted, kv_inverted):
            rstd = spread(0, q_inverted)
            ready = normalise_all([normalise(n, latent[:, n, :], col("q_norm", n), None, latent_hi[:, n, :],
                                             latent_lo[:, n, :], None, None, rstd) for n in range(2)])
            return ready + normalise_all([normalise(0, latent[:, 2, :], col("kv_norm"), None, latent_hi[:, 2, :],
                                                    latent_lo[:, 2, :], None, None, spread(4, kv_inverted))])

        forget_left = forget_steps()
        qk_done = []
        for n in range(8):
            b, bank, done = product(stream.next(), h_hi, h_lo, h_ready)
            qk_done.append(scaled_product((q_a if n < 4 else k_a)[:, n % 4, :], b, bank, done))
            next(x_steps, None)
            next(forget_left, None)
            if n == 0:
                inverted = latent_sums()
            if n == 1:
                lat_ready = latent_norms(*inverted)
        taken = [banks.take() for _ in range(TB)]
        for n in range(4):
            block = stream.next()
            pe.after(block[3], block[4])
            for kk in range(2):
                k = 2 * n + kk
                for tb, (b, bank, free) in enumerate(taken):
                    pe.after(free if k == 0 else None)
                    w = slice(kk * 512, kk * 512 + 512)
                    t = slice(tb * P, tb * P + P)
                    ins = three(bank[:], h_hi[:, k, t], h_lo[:, k, t], block[1][:, w], block[2][:, w], k == 0, k == KD - 1)
            stream.used[block[0]] = pe.mark(ins)
            for _ in range(4):
                next(forget_left, None)
        va_done = []
        for tb, (b, bank, free) in enumerate(taken):
            act.after(stream.used[block[0]])
            va_done.append(act.mark(S.activation(v_a[:, tb, :], bank[:], ACT.Copy, scale=r_both[:, tb:tb + 1])))
            banks.free[b] = [va_done[-1]]
        qb_done = []
        for h in range(HEADS):
            if h % 4 == 0:
                n, hi, lo, *ready = stream.next()
            b, bank, free = banks.take()
            pe.after(free, ready)
            for k in range(2):
                pe.after(lat_ready[k])
                c = k * 512 + (h % 4) * P
                ins = three(bank[:], hi[:, c:c + P], lo[:, c:c + P], latent_hi[:, k, :], latent_lo[:, k, :], k == 0, k == 1)
            done = pe.mark(ins)
            if h % 4 == 3:
                stream.used[n] = done
            m_rot, rot_done = rotate([q_rot[32 * (h % 4):32 * (h % 4) + 32, h // 4, :]], bank, done)
            act.after(done, m_rot)
            m = act.mark(S.activation(q_b[64 * (h % 2):64 * (h % 2) + 64, h // 2, :], bank[0:64, :], ACT.Copy))
            banks.free[b] = [m_rot, m]
            qb_done.append([m, rot_done])
        block = stream.next()
        kb_done = []
        for h in range(0, HEADS, 2):
            b, bank, free = banks.take()
            pe.after(free, block[3], block[4], lat_ready[2])
            c = h * 64
            done = pe.mark(three(bank[:], block[1][:, c:c + P], block[2][:, c:c + P], latent_hi[:, 2, :], latent_lo[:, 2, :],
                                 True, True))
            act.after(done)
            kb_done.append(act.mark(S.activation(k_b[:, h // 2, :], bank[:], ACT.Copy)))
            banks.free[b] = [kb_done[-1]]
        vb_done = []
        for tb in range(TB):
            b, bank, free = banks.take()
            pe.after(free)
            t = slice(tb * P, tb * P + P)
            done = pe.mark(three(bank[:], latent_hi[:, 2, t], latent_lo[:, 2, t], block[1][:, 512:], block[2][:, 512:], True, True))
            act.after(done)
            vb_done.append(act.mark(S.activation(v_b[:, tb, :], bank[:], ACT.Copy)))
            banks.free[b] = [vb_done[-1]]
        stream.used[block[0]] = done

        gate_done = []

        def gate_block():
            n = len(gate_done)
            b, bank, done = product(stream.next(), h_hi, h_lo, h_ready)
            act.after(scaled_product(gates[:, n, :], b, bank, done))
            gate_done.append(act.mark(S.activation(gates[:, n, :], gates[:, n, :], ACT.Sigmoid, bias=col("b_gate", n))))

        stream.on_pool = False
        for _ in forget_left:
            pass
        bias_done = (dve.sem, dve.count)
        for _ in range(16):
            gate_block()
        early_over = [(pe.sem, pe.count), (dve.sem, dve.count), (act.sem, act.count)]
        early.close()
        act.after(early_over)
        dve.after(early_over)
        prob = [square[:, 0, :], square[:, 1, :], scaled[:, 0, :], scaled[:, 1, :]]
        prob_t = [hb(f"prob_t{i}", [P, TB, T]) for i in range(2)]
        stats = hb("att_stats", [P, 64, 4])
        att_hi, att_lo = h_hi, h_lo
        units = [(kind, h, i) for kind in (0, 1) for h in range(HEADS) for i in range(TB)]
        state = {}
        prob_free, prob_t_free = [None] * 4, [None] * 2
        att_ready = [None] * 8

        def score(u):
            kind, h, i = units[u]
            n = (i + 1) * P
            b, bank, free = banks.take()
            pe.after(free)
            q = slice(i * P, i * P + P)
            if kind == 0:
                r = slice(64 * (h % 2), 64 * (h % 2) + 64)
                pe.after(qk_done[h // 2], qk_done[4 + h // 2], bias_done)
                M.matmul(bank[:, 0:n], q_a[r, h // 2, q], k_a[r, h // 2, 0:n], start=True, stop=False)
                pick_head = const("ident")[0:HEADS, h:h + 1].broadcast_to([HEADS, P])
                M.matmul(bank[:, 0:n], pick_head, key_bias[:, 0:n], start=False, stop=False)
            else:
                pe.after(qb_done[h], kb_done[h // 2], k_rot_done)
                r = slice(64 * (h % 2), 64 * (h % 2) + 64)
                M.matmul(bank[:, 0:n], q_b[r, h // 2, q], k_b[r, h // 2, 0:n], start=True, stop=False)
                r = slice(32 * (h % 4), 32 * (h % 4) + 32)
                M.matmul(bank[:, 0:n], q_rot[r, h // 4, q], k_rot[r, 0:n], start=False, stop=False)
            mask = const("causal" if kind == 0 else "chunk")
            state[u] = {"scored": pe.mark(M.matmul(bank[:, n - P:n], const("ident"), mask, start=False, stop=True)),
                        "bank": bank, "b": b, "n": n}

        def row_max(u):
            s = state[u]
            scale = ATT_SCALE_A if units[u][0] == 0 else ATT_SCALE_B
            dve.after(s["scored"])
            m = dve.mark(V.tensor_reduce(stats[:, u, 0:1], s["bank"][:, 0:s["n"]], AX_X, ALU.max))
            dve.after(m)
            s["max"] = dve.mark(V.tensor_scalar(stats[:, u, 1:2], stats[:, u, 0:1], -scale, None, ALU.mult))

        def exponent(u):
            s = state[u]
            scale = ATT_SCALE_A if units[u][0] == 0 else ATT_SCALE_B
            act.after(s["max"], prob_free[u % 4])
            s["exp"] = act.mark(S.activation(prob[u % 4][:, 0:s["n"]], s["bank"][:, 0:s["n"]], ACT.Exp,
                                             bias=stats[:, u, 1:2], scale=scale, accum_out=stats[:, u, 2:3]))
            banks.free[s["b"]] = [s["exp"]]

        def divide(u):
            s = state[u]
            dve.after(s["exp"])
            m = dve.mark(V.reciprocal(stats[:, u, 3:4], stats[:, u, 2:3]))
            dve.after(m)
            p = prob[u % 4][:, 0:s["n"]]
            s["prob"] = dve.mark(V.tensor_scalar(p, p, stats[:, u, 3:4], None, ALU.mult))

        def turn(u):
            kind, h, i = units[u]
            s = state[u]
            b, bank, free = banks.take()
            pe.after(free, s["prob"])
            for kb in range(i + 1):
                ins = M.transpose(bank[:, kb * P:(kb + 1) * P], prob[u % 4][:, kb * P:(kb + 1) * P], const("ident"))
            s["turned"] = pe.mark(ins)
            prob_free[u % 4] = s["turned"]
            head_no = u // TB
            q, e = (act, S) if u % 2 else (dve, V)
            q.after(s["turned"], prob_t_free[head_no % 2])
            dst = prob_t[head_no % 2][:, 0:i + 1, i * P:(i + 1) * P]
            src = bank[:, 0:(i + 1) * P].rearrange("p (k q) -> p k q", q=P)
            s["kept"] = q.mark(e.activation(dst, src, ACT.Copy) if u % 2 else e.tensor_copy(dst, src))
            banks.free[b] = [s["kept"]]

        def values(head_no):
            kind, h = divmod(head_no, HEADS)
            b, bank, free = banks.take()
            pe.after(free, *[state[head_no * TB + i]["kept"] for i in range(TB)])
            pe.after(va_done if kind == 0 else vb_done)
            v = v_a if kind == 0 else v_b
            pair = slice((h // 2) * P, (h // 2) * P + P)
            for kb in range(TB):
                ins = M.matmul(bank[:, kb * P:T], v[:, kb, pair], prob_t[head_no % 2][:, kb, kb * P:T],
                               start=kb == 0, stop=kb == TB - 1)
            done = pe.mark(ins)
            prob_t_free[head_no % 2] = done
            r = slice(64 * (h % 2), 64 * (h % 2) + 64)
            tile = 4 * kind + h // 2
            act.after(done)
            hi_done = act.mark(S.activation(att_hi[r, tile, :], bank[r, :], ACT.Copy))
            dve.after(hi_done)
            lo_done = dve.mark(V.tensor_tensor(att_lo[r, tile, :], bank[r, :], att_hi[r, tile, :].bitcast(F32), ALU.subtract))
            banks.free[b] = [lo_done]
            att_ready[tile] = (att_ready[tile] or []) + [hi_done, lo_done]

        n_units = len(units)
        for s in range(n_units + 5):
            if s < n_units:
                score(s)
                row_max(s)
                exponent(s)
            if 0 <= s - 1 < n_units:
                divide(s - 1)
            if 0 <= s - 3 < n_units:
                turn(s - 3)
            if s % TB == 0 and s >= 2 * TB:
                values(s // TB - 2)

        stream.on_pool = True
        heads_over = [(pe.sem, pe.count), (dve.sem, dve.count), (act.sem, act.count)]
        heads.close()
        act.after(heads_over)
        dve.after(heads_over)
        merged_hi = ab("merged_hi", [P, KD, T], F32R)
        merged_lo = ab("merged_lo", [P, KD, T], F32R)
        merged_ready = [None] * KD
        merged = gates
        for m2 in range(4):
            block = stream.next()
            for n in range(2):
                k = 2 * m2 + n
                b, bank, done = product(block, att_hi[:, 0:4], att_lo[:, 0:4], att_ready[0:4], nk=4, at=n * 512, last_use=n == 1)
                dve.after(done, gate_done[k])
                x_m = dve.mark(V.tensor_tensor(merged[:, k, :], bank[:], gates[:, k, :], ALU.mult))
                banks.free[b] = [x_m]
        for m2 in range(4):
            block = stream.next()
            for n in range(2):
                k = 2 * m2 + n
                b, bank, done = product(block, att_hi[:, 4:8], att_lo[:, 4:8], att_ready[4:8], nk=4, at=n * 512, last_use=n == 1)
                dve.after(done, gate_done[8 + k])
                m = dve.mark(V.tensor_tensor(gates[:, 8 + k, :], bank[:], gates[:, 8 + k, :], ALU.mult))
                banks.free[b] = [m]
                dve.after(m, x_m)
                m = dve.mark(V.tensor_tensor(merged[:, k, :], merged[:, k, :], gates[:, 8 + k, :], ALU.add))
                merged_ready[k] = split_to(merged_hi[:, k, :], merged_lo[:, k, :], merged[:, k, :], m)
        h_free = done

        def residual(n_blocks, m_hi, m_lo, m_ready, gate=None, each=None):
            x_sum = SquareSum()
            for k in range(KD):
                b, bank, free = banks.take()
                pe.after(free)
                kk = 0
                for n in range(n_blocks):
                    block = stream.next()
                    tiles = stream.plan[block[0]].shape[1] // P
                    done = block_product(bank, block, m_hi, m_lo, m_ready, [(c * P, kk + c) for c in range(tiles)],
                                         n == 0, n == n_blocks - 1)
                    kk += tiles
                    stream.used[block[0]] = done
                x_done[k] = add_to_x(k, b, bank, done, gate)
                if each:
                    each(k)
                x_sum.add(k, x_done[k])
            return x_sum

        def h_tile(k):
            h_ready[k] = without_rstd(k, col("norm_ffn", k), h_free)

        stream.on_pool = False
        x_sum = residual(1, merged_hi, merged_lo, merged_ready, each=h_tile)
        att.close()
        att_over = [(act.sem, act.count), (dve.sem, dve.count), (pe.sem, pe.count)]

        ffn = ExitStack()
        f_hi = sb("ffn_hi", [P, FFN_TILES, T], F32R, ffn)
        f_lo = sb("ffn_lo", [P, FFN_TILES, T], F32R, ffn)
        silu = sb("silu", [P, 2, T], F32, ffn)
        ffn_scale = sb("ffn_scale", [P, T], F32, ffn)
        act.after(att_over)
        dve.after(att_over)
        pool.after(att_over)
        ffn_products = [product(stream.next(), h_hi, h_lo, h_ready)]
        inverted = x_sum.invert()
        ffn_products.append(product(stream.next(), h_hi, h_lo, h_ready))
        scale_kept = kept(ffn_scale[:], spread(0, inverted))
        f_ready, silu_free = [], [None, None]
        for f in range(FFN_TILES):
            s = silu[:, f % 2, :]
            b, bank, done = ffn_products[0] if f == 0 else product(stream.next(), h_hi, h_lo, h_ready)
            dve.after(done, scale_kept, silu_free[f % 2])
            m = dve.mark(V.tensor_tensor(s, bank[:], ffn_scale[:], ALU.mult))
            banks.free[b] = [m]
            act.after(m)
            s_done = act.mark(S.activation(s, s, ACT.Silu))
            pool.after(s_done, scale_kept)
            s_done = pool.mark(G.tensor_tensor(s, s, ffn_scale[:], ALU.mult))
            b, bank, done = ffn_products[1] if f == 0 else product(stream.next(), h_hi, h_lo, h_ready)
            dve.after(done, s_done)
            m = dve.mark(V.tensor_tensor(s, bank[:], s, ALU.mult))
            banks.free[b] = [m]
            f_ready.append(split_to(f_hi[:, f, :], f_lo[:, f, :], silu[:, f % 2, :], m))
            silu_free[f % 2] = f_ready[-1]
        x_rstd = residual(3, f_hi, f_lo, f_ready).rstd()
        ffn.close()

        stored = Landing(sem("out_stored"))
        for k in range(KD):
            dve.after(x_rstd[2])
            m = dve.mark(V.scalar_tensor_tensor(x[:, k, :], x[:, k, :], col("norm_final", k), x_rstd[1][:], ALU.mult, ALU.mult))
            sp.after(m)
            end = stored.mark(nc.sync.dma_start(out_cols[:, k, :], x[:, k, :]))
        sp.after(end)
        assert len(stream.used) == len(plan)


def in_tiles(w):
    k, n = w.shape
    return w.reshape(k // P, P, n // P, P).transpose(2, 1, 0, 3).reshape(n // P, P, k)


def per_column(v):
    return np.asarray(v).reshape(-1, P).T


def constant_matrices():
    r = np.arange(P)
    m = {
        "ones": np.ones((P, P)),
        "head_pick": (r[:, None] // HEAD_DIM == np.arange(2)[None, :]),
        "ident": np.eye(P),
        "iota": np.broadcast_to(r[None, :], (P, P)),
        "causal": np.where(r[None, :] <= r[:, None], 0.0, NEG),
        "chunk": np.where(r[None, :] // 64 <= r[:, None] // 64, 0.0, NEG),
        "iota16": np.broadcast_to(np.arange(16)[None, :], (P, 16)),
    }
    return np.concatenate([m[n].astype(np.float32) for n, _ in CONSTS], axis=1)


def lay_out(i):
    f32 = np.float32
    half = ROPE // 2
    row = np.arange(P)
    inv = (10000.0 ** (-np.arange(half, dtype=np.float64) / half)).astype(f32)
    is_cos = (row >= 64) & (row < 96)
    first = (row % 32) < half
    forget_col = np.zeros((P, 1), f32)
    forget_col[0:HEADS, 0] = i["b_forget_2"][0]
    parts = {
        "b_ada": per_column(i["b_ada"][0]), "norm1": per_column(i["norm1_g"][0]),
        "conv_a": per_column(i["conv_a_w"][0]), "conv_b": per_column(i["conv_b_w"][0]),
        "conv_bias": per_column(i["conv_b_b"][0]), "b_r": per_column(i["b_r"][0]), "b_i": per_column(i["b_i"][0]),
        "lam": per_column(i["lru_lambda"][0]),
        "gn": np.concatenate([per_column(i["gn_a"][0]), per_column(i["gn_b"][0])], axis=1),
        "norm2": per_column(i["norm2_g"][0]), "final": per_column(i["final_g"]),
        "norm_mix": per_column(i["norm_mix_g_2"][0]), "q_norm": per_column(i["q_a_norm_g_2"][0]),
        "kv_norm": per_column(i["kv_a_norm_g_2"][0]), "b_gate": per_column(i["b_gate_2"][0]),
        "norm_ffn": per_column(i["norm_ffn_g_2"][0]), "norm_final": per_column(i["norm_final_g_2"]),
        "b_forget": forget_col, "inv_freq": inv[row % half][:, None],
        "phase": np.where(is_cos, math.pi / 2, 0.0).astype(f32)[:, None],
        "sign": np.where(~is_cos & first, -1.0, 1.0).astype(f32)[:, None],
        "eps": np.full((P, 1), EPS, f32),
    }
    out = {"columns": np.concatenate([parts[n] for n, _ in COLUMNS], axis=1), "consts": constant_matrices()}
    out["x"] = i["x"][0].T.reshape(KD, P, T).transpose(1, 0, 2)
    out["c_rows"] = np.broadcast_to(i["c"][0], (P, D))
    out["w_ada"] = i["w_ada"][0].T.reshape(48, P, D)
    out["w_in"] = in_tiles(i["w_in"][0])
    out["w_out"] = in_tiles(i["w_out"][0])
    out["w_q"] = in_tiles(i["w_q"][0])
    gates = np.zeros((P, 2, 4, P), f32)
    for g, name in enumerate(("w_r", "w_i")):
        for h in range(HEADS):
            r = slice(64 * (h % 2), 64 * (h % 2) + 64)
            gates[r, g, h // 2, r] = i[name][0, h]
    out["w_lru_gates"] = gates
    out["keys"] = i["sub_keys"][0].transpose(1, 3, 0, 2).reshape(P, HEADS, N_KEYS)
    out["expert_u"] = i["expert_u"][0].reshape(N_KEYS, N_KEYS, KD, P).transpose(1, 3, 2, 0).reshape(N_KEYS, P, BLOCK)
    out["expert_v"] = i["expert_v"][0].reshape(N_KEYS, N_GROUPS, GROUP, KD, P).transpose(1, 3, 0, 2, 4).reshape(
        N_GROUPS * KD, P, BLOCK)
    w = i["w_in_2"][0]
    qa, ka, va, fa, cq, ckv, kr, ga, gb = np.split(w, np.cumsum([512, 512, 512, 8, 256, 128, 32, 1024]), axis=1)
    small = np.concatenate([fa, np.zeros((D, 56), f32), kr, kr[:, half:], kr[:, :half]], axis=1)
    out["w_small2"] = in_tiles(small)
    out["w_latent2"] = in_tiles(np.concatenate([cq, ckv], axis=1))
    out["w_qk2"] = in_tiles(np.concatenate([qa, ka], axis=1))
    out["w_v2"] = va.reshape(4, 2, P, 512).transpose(0, 2, 1, 3).reshape(4, P, BLOCK)
    out["w_gates2"] = in_tiles(np.concatenate([ga, gb], axis=1))
    qu = i["w_q_up_2"][0].reshape(2 * P, HEADS, NOPE + ROPE)
    qu = np.concatenate([qu, qu[:, :, NOPE + half:], qu[:, :, NOPE:NOPE + half]], axis=2)
    out["w_q_up"] = qu.reshape(2, P, 2, 4, P).transpose(2, 1, 0, 3, 4).reshape(2, P, BLOCK)
    kv = i["w_kv_up_2"][0].reshape(P, HEADS, 2, 64).transpose(0, 2, 1, 3)
    out["w_kv_up"] = kv.reshape(1, P, BLOCK)
    for name, w in (("w_branch_a", i["w_branch_a_2"][0]), ("w_branch_b", i["w_branch_b_2"][0])):
        out[name] = w.reshape(4, P, 4, 2, P).transpose(2, 1, 3, 0, 4).reshape(4, P, BLOCK)
    out["w_out2"] = in_tiles(i["w_out_2"][0])
    out["w_ffn_gate"] = in_tiles(i["w_ffn_gate_2"][0])
    out["w_ffn_up"] = in_tiles(i["w_ffn_up_2"][0])
    out["w_ffn_down"] = in_tiles(i["w_ffn_down_2"][0])
    out["positions"] = np.broadcast_to(i["positions_2"][0], (P, T))
    return {k: np.ascontiguousarray(v) for k, v in out.items()}


def kernel(**inputs):
    import concourse.bacc as bacc
    from concourse.bass_utils import run_bass_kernel_spmd

    arrays = lay_out({k: np.asarray(v) for k, v in inputs.items()})
    nc = bacc.Bacc("TRN2", target_bir_lowering=False, num_devices=1)
    aps = {k: nc.dram_tensor(f"in_{k}", v.shape, mybir.dt.from_np(v.dtype), kind="ExternalInput").ap()
           for k, v in arrays.items()}
    out = nc.dram_tensor("out_cols", (P, KD, T), F32, kind="ExternalOutput").ap()
    build(nc, aps, out)
    r = run_bass_kernel_spmd(nc, [{f"in_{k}": v for k, v in arrays.items()}], core_ids=[0])
    got = np.asarray(r.results[0]["out_cols"])
    return np.ascontiguousarray(got.transpose(1, 0, 2).reshape(1, D, T).transpose(0, 2, 1))
```
